# Optimizing a Trainium2 kernel written in Bass

```python
import jax, jax.numpy as jnp
from jax import lax
import numpy as np
import jax
import jax.numpy as jnp

D_MODEL = 1024
BATCH = 1
SEQ = 256
DEPTH = 2

GDN_HEADS = D_MODEL // 256
GDN_DK = 128
GDN_DV = 128
GDN_CONV = 4
GDN_CHUNK = 64
MOBA_HEADS = D_MODEL // 128
MOBA_DH = 64
MOBA_BLOCK = 256
MOBA_TOPK = 3
MOBA_QCHUNK = 32
ROPE_DIMS = MOBA_DH // 4
ROPE_THETA = 500000.0
GDN_QK_W = GDN_HEADS * GDN_DK
GDN_V_W = GDN_HEADS * GDN_DV
MOBA_W = MOBA_HEADS * MOBA_DH
D_MIX = GDN_V_W + MOBA_W
IN_SPLITS = (GDN_QK_W, GDN_QK_W, GDN_V_W, GDN_HEADS, GDN_HEADS, GDN_V_W, MOBA_W, MOBA_W, MOBA_W)
N_IN = sum(IN_SPLITS)
D_FF = 256 * ((8 * D_MODEL // 3 + 255) // 256)
FFN_CONV = 3
DEEPNORM_ALPHA = (2 * DEPTH) ** 0.25
DEEPNORM_BETA = (8 * DEPTH) ** -0.25
LN_EPS = 1e-5
NORM_EPS = 1e-6


def layer_norm(x, g, b):
    xf = x.astype(jnp.float32)
    mu = xf.mean(-1, keepdims=True)
    var = jnp.square(xf - mu).mean(-1, keepdims=True)
    return ((xf - mu) * lax.rsqrt(var + LN_EPS) * g + b).astype(x.dtype)

def causal_dwconv(x, w):
    k_w = w.shape[0]
    s = x.shape[1]
    xp = jnp.pad(x, ((0, 0), (k_w - 1, 0), (0, 0)))
    return sum(xp[:, j:j + s, :] * w[j] for j in range(k_w))

def l2norm(x):
    return x * lax.rsqrt(jnp.sum(x * x, -1, keepdims=True) + NORM_EPS)

def split_heads(t, n_heads):
    b, s, _ = t.shape
    return t.reshape(b, s, n_heads, -1).transpose(0, 2, 1, 3)

def partial_rotary(x, pos):
    half = ROPE_DIMS // 2
    inv = ROPE_THETA ** (-jnp.arange(half, dtype=jnp.float32) / half)
    ang = pos.astype(jnp.float32)[:, None] * inv[None, :]
    cos = jnp.cos(ang).astype(x.dtype)
    sin = jnp.sin(ang).astype(x.dtype)
    x1, x2, rest = x[..., :half], x[..., half:ROPE_DIMS], x[..., ROPE_DIMS:]
    return jnp.concatenate([x1 * cos - x2 * sin, x2 * cos + x1 * sin, rest], -1)

def gated_delta_rule(q, k, v, g, beta):
    b_, h, s, dk = q.shape
    dv = v.shape[-1]
    c = GDN_CHUNK
    n = s // c
    q = q * dk ** -0.5
    resh = lambda t: t.reshape(b_, h, n, c, *t.shape[3:])
    q, k, v, g, beta = map(resh, (q, k, v, g, beta))
    g = jnp.cumsum(g, axis=-1)
    idx = jnp.arange(c)
    lower_incl = idx[:, None] >= idx[None, :]
    decay = jnp.exp(jnp.where(lower_incl, g[..., :, None] - g[..., None, :], -jnp.inf))
    k_beta = k * beta[..., None]
    a_strict = jnp.where(idx[:, None] > idx[None, :],
                         jnp.einsum('bhncd,bhnmd->bhncm', k_beta, k) * decay, 0.0)
    t_mat = a_strict + jnp.eye(c, dtype=q.dtype)
    rhs = jnp.concatenate([v * beta[..., None], k_beta * jnp.exp(g)[..., None]], -1)
    sol = lax.linalg.triangular_solve(t_mat, rhs, left_side=True, lower=True, unit_diagonal=True)
    u, w = sol[..., :dv], sol[..., dv:]
    attn_intra = jnp.einsum('bhncd,bhnmd->bhncm', q, k) * decay
    q_dec = q * jnp.exp(g)[..., None]
    g_last = g[..., -1]
    k_dec = k * jnp.exp(g_last[..., None] - g)[..., None]

    def step(state, xs):
        q_c, k_c, u_c, w_c, a_c, gl = xs
        v_new = u_c - jnp.einsum('bhcd,bhde->bhce', w_c, state)
        o = jnp.einsum('bhcd,bhde->bhce', q_c, state) + jnp.einsum('bhcm,bhme->bhce', a_c, v_new)
        state = state * jnp.exp(gl)[..., None, None] + jnp.einsum('bhcd,bhce->bhde', k_c, v_new)
        return state, o

    xs = tuple(jnp.moveaxis(t, 2, 0) for t in (q_dec, k_dec, u, w, attn_intra, g_last))
    s0 = jnp.zeros((b_, h, dk, dv), q.dtype)
    _, o = lax.scan(step, s0, xs)
    return jnp.moveaxis(o, 0, 2).reshape(b_, h, s, dv)

def gdn_mixer(q, k, v, a_logit, b_logit, z, conv_w, a_log, dt_bias, norm_g):
    b_, s, _ = q.shape
    qkv = jax.nn.silu(causal_dwconv(jnp.concatenate([q, k, v], -1), conv_w))
    q, k, v = jnp.split(qkv, [GDN_QK_W, 2 * GDN_QK_W], -1)
    f32 = jnp.float32
    qh = l2norm(split_heads(q, GDN_HEADS).astype(f32))
    kh = l2norm(split_heads(k, GDN_HEADS).astype(f32))
    vh = split_heads(v, GDN_HEADS).astype(f32)
    beta = jax.nn.sigmoid(b_logit.astype(f32)).transpose(0, 2, 1)
    g = (-jnp.exp(a_log.astype(f32)) * jax.nn.softplus(a_logit.astype(f32) + dt_bias.astype(f32))).transpose(0, 2, 1)
    o = gated_delta_rule(qh, kh, vh, g, beta).transpose(0, 2, 1, 3)
    o = o * lax.rsqrt(jnp.mean(o * o, -1, keepdims=True) + NORM_EPS) * norm_g.astype(f32)
    o = o * jax.nn.silu(z.reshape(b_, s, GDN_HEADS, GDN_DV).astype(f32))
    return o.reshape(b_, s, GDN_V_W).astype(q.dtype)

def moba_mixer(q, k, v, pos):
    b_, s, _ = q.shape
    h, dh, blk, qc_len = MOBA_HEADS, MOBA_DH, MOBA_BLOCK, MOBA_QCHUNK
    qh = partial_rotary(split_heads(q, h), pos)
    kh = partial_rotary(split_heads(k, h), pos)
    vh = split_heads(v, h)
    nb = -(-s // blk)
    pad = nb * blk - s
    n_sel = min(MOBA_TOPK, nb)
    kb = jnp.pad(kh, ((0, 0), (0, 0), (0, pad), (0, 0))).reshape(b_, h, nb, blk, dh)
    vb = jnp.pad(vh, ((0, 0), (0, 0), (0, pad), (0, 0))).reshape(b_, h, nb, blk, dh)
    k_mean = kb.mean(axis=3)
    nq = s // qc_len
    q_chunks = jnp.moveaxis(qh.reshape(b_, h, nq, qc_len, dh), 2, 0)
    scale = dh ** -0.5
    bi = jnp.arange(b_)[:, None, None, None]
    hi = jnp.arange(h)[None, :, None, None]
    blk_ids = jnp.arange(nb)
    sel_rank = jnp.arange(n_sel)

    def attend(args):
        q_c, ci = args
        t = ci * qc_len + jnp.arange(qc_len)
        own = (ci * qc_len) // blk
        gate = jnp.einsum('bhqd,bhnd->bhqn', q_c, k_mean).astype(jnp.float32)
        gate = jnp.where(blk_ids < own, gate, -jnp.inf)
        _, sel = lax.top_k(gate, n_sel)
        sel_valid = sel_rank < own
        k_sel = kb[bi, hi, sel]
        v_sel = vb[bi, hi, sel]
        s_sel = jnp.einsum('bhqd,bhqjkd->bhqjk', q_c, k_sel).astype(jnp.float32) * scale
        s_sel = jnp.where(sel_valid[:, None], s_sel, -jnp.inf).reshape(b_, h, qc_len, n_sel * blk)
        k_own = lax.dynamic_index_in_dim(kb, own, axis=2, keepdims=False)
        v_own = lax.dynamic_index_in_dim(vb, own, axis=2, keepdims=False)
        s_own = jnp.einsum('bhqd,bhkd->bhqk', q_c, k_own).astype(jnp.float32) * scale
        key_pos = own * blk + jnp.arange(blk)
        s_own = jnp.where(key_pos[None, :] <= t[:, None], s_own, -jnp.inf)
        p = jax.nn.softmax(jnp.concatenate([s_own, s_sel], -1), axis=-1).astype(v_sel.dtype)
        p_own = p[..., :blk]
        p_sel = p[..., blk:].reshape(b_, h, qc_len, n_sel, blk)
        return (jnp.einsum('bhqk,bhkd->bhqd', p_own, v_own)
                + jnp.einsum('bhqjk,bhqjkd->bhqd', p_sel, v_sel))

    o = lax.map(attend, (q_chunks, jnp.arange(nq)))
    o = jnp.moveaxis(o, 0, 2).reshape(b_, h, s, dh)
    return o.transpose(0, 2, 1, 3).reshape(b_, s, MOBA_W)

def hybrid_layer(x, w_in, gdn_conv_w, gdn_a_log, gdn_dt_bias, gdn_norm_g, w_out,
                 ln1_g, ln1_b, w_up, ffn_conv_w, ffn_conv_b, w_down, ln2_g, ln2_b, pos):
    proj = x @ w_in
    offs = np.cumsum(IN_SPLITS)[:-1].tolist()
    q_a, k_a, v_a, a_logit, b_logit, z, q_b, k_b, v_b = jnp.split(proj, offs, -1)
    o_a = gdn_mixer(q_a, k_a, v_a, a_logit, b_logit, z, gdn_conv_w, gdn_a_log, gdn_dt_bias, gdn_norm_g)
    o_b = moba_mixer(q_b, k_b, v_b, pos)
    mix = jnp.concatenate([o_a, o_b], -1) @ w_out
    x = layer_norm(DEEPNORM_ALPHA * x + mix, ln1_g, ln1_b)
    hid = causal_dwconv(x @ w_up, ffn_conv_w) + ffn_conv_b
    gate, val = jnp.split(hid, 2, -1)
    ffn = (jax.nn.silu(gate) * val) @ w_down
    return layer_norm(DEEPNORM_ALPHA * x + ffn, ln2_g, ln2_b)

def first_inputs(seed: int = 0) -> dict:
    key = jax.random.key(seed)
    ks = jax.random.split(key, 16)
    f = jnp.float32
    nrm = lambda k, shape, scale: jax.random.normal(k, shape, f) * scale
    x = jax.random.normal(ks[0], (BATCH, SEQ, D_MODEL), f)
    w_in = nrm(ks[1], (DEPTH, D_MODEL, N_IN), D_MODEL ** -0.5)
    gdn_conv_w = nrm(ks[2], (DEPTH, GDN_CONV, 2 * GDN_QK_W + GDN_V_W), GDN_CONV ** -0.5)
    gdn_a_log = jnp.log(jax.random.uniform(ks[3], (DEPTH, GDN_HEADS), f, 1.0, 16.0))
    dt = jnp.exp(jax.random.uniform(ks[4], (DEPTH, GDN_HEADS), f, float(np.log(1e-3)), float(np.log(1e-1))))
    gdn_dt_bias = dt + jnp.log(-jnp.expm1(-dt))
    gdn_norm_g = 1.0 + nrm(ks[5], (DEPTH, GDN_DV), 0.02)
    w_out = nrm(ks[6], (DEPTH, D_MIX, D_MODEL), DEEPNORM_BETA * D_MIX ** -0.5)
    ln1_g = 1.0 + nrm(ks[7], (DEPTH, D_MODEL), 0.02)
    ln1_b = nrm(ks[8], (DEPTH, D_MODEL), 0.02)
    w_up = nrm(ks[9], (DEPTH, D_MODEL, 2 * D_FF), D_MODEL ** -0.5)
    ffn_conv_w = nrm(ks[10], (DEPTH, FFN_CONV, 2 * D_FF), FFN_CONV ** -0.5)
    ffn_conv_b = nrm(ks[11], (DEPTH, 2 * D_FF), 0.01)
    w_down = nrm(ks[12], (DEPTH, D_FF, D_MODEL), DEEPNORM_BETA * D_FF ** -0.5)
    ln2_g = 1.0 + nrm(ks[13], (DEPTH, D_MODEL), 0.02)
    ln2_b = nrm(ks[14], (DEPTH, D_MODEL), 0.02)
    return {'x': x, 'w_in': w_in, 'gdn_conv_w': gdn_conv_w, 'gdn_a_log': gdn_a_log,
            'gdn_dt_bias': gdn_dt_bias, 'gdn_norm_g': gdn_norm_g, 'w_out': w_out,
            'ln1_g': ln1_g, 'ln1_b': ln1_b, 'w_up': w_up, 'ffn_conv_w': ffn_conv_w,
            'ffn_conv_b': ffn_conv_b, 'w_down': w_down, 'ln2_g': ln2_g, 'ln2_b': ln2_b}

def first_block(x, w_in, gdn_conv_w, gdn_a_log, gdn_dt_bias, gdn_norm_g, w_out,
              ln1_g, ln1_b, w_up, ffn_conv_w, ffn_conv_b, w_down, ln2_g, ln2_b):
    pos = jnp.arange(x.shape[1], dtype=jnp.int32)
    for l in range(DEPTH):
        x = hybrid_layer(x, w_in[l], gdn_conv_w[l], gdn_a_log[l], gdn_dt_bias[l], gdn_norm_g[l],
                         w_out[l], ln1_g[l], ln1_b[l], w_up[l], ffn_conv_w[l], ffn_conv_b[l],
                         w_down[l], ln2_g[l], ln2_b[l], pos)
    return x


GRID_W = 64
CTX_LEN = 256
N_MIXERS = 2
RET_HEADS = 4
RET_QK_DIM = D_MODEL // RET_HEADS
RET_V_DIM = 2 * D_MODEL // RET_HEADS
RET_CHUNK = 128
NAT_HEAD_DIM = 32
NAT_HEADS = D_MODEL // NAT_HEAD_DIM
NAT_WIN_ROWS = 8
NAT_WIN_COLS = 16
MLP_HIDDEN = 4 * D_MODEL
ROPE_BASE = 10000.0
DN_ALPHA = (2.0 * DEPTH) ** 0.25
DN_BETA = (8.0 * DEPTH) ** -0.25
N_RET_LAYERS = (DEPTH + 1) // 2
N_NAT_LAYERS = DEPTH // 2


def layer_norm_2(x, g, b):
    xf = x.astype(jnp.float32)
    mu = jnp.mean(xf, axis=-1, keepdims=True)
    var = jnp.mean(jnp.square(xf - mu), axis=-1, keepdims=True)
    return ((xf - mu) * lax.rsqrt(var + LN_EPS) * g + b).astype(x.dtype)

def axial_rope_angles(n, axis_dim):
    t = jnp.arange(n)
    row = (t // GRID_W).astype(jnp.float32)
    col = (t % GRID_W).astype(jnp.float32)
    inv = 1.0 / (ROPE_BASE ** (jnp.arange(0, axis_dim, 2, dtype=jnp.float32) / axis_dim))
    return row[:, None] * inv, col[:, None] * inv

def rope_rotate(x, ang):
    cos = jnp.cos(ang).astype(x.dtype)
    sin = jnp.sin(ang).astype(x.dtype)
    x1, x2 = jnp.split(x, 2, axis=-1)
    return jnp.concatenate([x1 * cos - x2 * sin, x2 * cos + x1 * sin], axis=-1)

def axial_rope(x, ang_row, ang_col):
    xr, xc = jnp.split(x, 2, axis=-1)
    return jnp.concatenate([rope_rotate(xr, ang_row), rope_rotate(xc, ang_col)], axis=-1)

def retention_chunk_scan(q, k, v, log_gamma, state0, with_out):
    b, h, n, dk = q.shape
    dv = v.shape[-1]
    cs = RET_CHUNK
    nc = n // cs
    dt = v.dtype
    pos = jnp.arange(cs, dtype=jnp.float32)
    lg = log_gamma.astype(jnp.float32)[:, None]
    rel = pos[:, None] - pos[None, :]
    intra = jnp.where(rel >= 0, jnp.exp(lg[:, :, None] * jnp.maximum(rel, 0.0)), 0.0).astype(dt)
    q_dec = jnp.exp(lg * (pos + 1.0))[..., None].astype(dt)
    k_dec = jnp.exp(lg * (cs - 1.0 - pos))[..., None].astype(dt)
    chunk_dec = jnp.exp(lg * cs)[..., None].astype(dt)

    def to_chunks(t):
        return jnp.moveaxis(t.reshape(b, h, nc, cs, t.shape[-1]), 2, 0)

    def step(state, qkv):
        qc, kc, vc = qkv
        new_state = state * chunk_dec + jnp.einsum('bhsd,bhse->bhde', kc * k_dec, vc)
        if with_out:
            scores = jnp.einsum('bhcd,bhsd->bhcs', qc, kc) * intra
            out = (jnp.einsum('bhcs,bhse->bhce', scores, vc)
                   + jnp.einsum('bhcd,bhde->bhce', qc * q_dec, state))
            return new_state, out
        return new_state, None

    state, outs = lax.scan(step, state0, (to_chunks(q), to_chunks(k), to_chunks(v)))
    if with_out:
        outs = jnp.moveaxis(outs, 0, 2).reshape(b, h, n, dv)
    return state, outs

def retention_mixer(h_lat, h_ctx, w_in, w_o, decay_param, ang_row, ang_col, ctx_out):
    b = h_lat.shape[0]
    qk_w = RET_HEADS * RET_QK_DIM
    v_w = RET_HEADS * RET_V_DIM

    def heads(t, hd):
        return t.reshape(b, t.shape[1], RET_HEADS, hd).transpose(0, 2, 1, 3)

    def project(h, w):
        p = h @ w
        q = heads(p[..., :qk_w], RET_QK_DIM)
        k = heads(p[..., qk_w:2 * qk_w], RET_QK_DIM) * (RET_QK_DIM ** -0.5)
        v = heads(p[..., 2 * qk_w:2 * qk_w + v_w], RET_V_DIM)
        return q, k, v, p[..., 2 * qk_w + v_w:]

    def flip(t):
        return t[:, :, ::-1]

    def finish(o, g):
        of = o.astype(jnp.float32)
        mu = jnp.mean(of, axis=-1, keepdims=True)
        var = jnp.mean(jnp.square(of - mu), axis=-1, keepdims=True)
        on = ((of - mu) * lax.rsqrt(var + LN_EPS)).astype(o.dtype)
        on = on.transpose(0, 2, 1, 3).reshape(b, o.shape[2], v_w)
        return (on * jax.nn.silu(g)) @ w_o

    log_gamma = -jnp.exp(decay_param.astype(jnp.float32))
    w_ctx = w_in if ctx_out else w_in[:, :2 * qk_w + v_w]
    q_c, k_c, v_c, g_c = project(h_ctx, w_ctx)
    zeros = jnp.zeros((b, RET_HEADS, RET_QK_DIM, RET_V_DIM), v_c.dtype)
    s_f, o_cf = retention_chunk_scan(q_c, k_c, v_c, log_gamma[0], zeros, ctx_out)
    s_b, o_cb = retention_chunk_scan(flip(q_c), flip(k_c), flip(v_c), log_gamma[1], zeros, ctx_out)

    q_l, k_l, v_l, g_l = project(h_lat, w_in)
    q_l = axial_rope(q_l, ang_row, ang_col)
    k_l = axial_rope(k_l, ang_row, ang_col)
    _, o_lf = retention_chunk_scan(q_l, k_l, v_l, log_gamma[0], s_f, True)
    _, o_lb = retention_chunk_scan(flip(q_l), flip(k_l), flip(v_l), log_gamma[1], s_b, True)
    y_lat = finish(o_lf + flip(o_lb), g_l)
    y_ctx = finish(o_cf + flip(o_cb), g_c) if ctx_out else None
    return y_lat, y_ctx

def neighbourhood_mixer(h_lat, h_ctx, w_in, w_o, rpb, ctx_out):
    b, n, d = h_lat.shape
    rows = n // GRID_W
    kh = min(NAT_WIN_ROWS, rows)
    kw = NAT_WIN_COLS
    nh, hd = NAT_HEADS, NAT_HEAD_DIM
    scale = hd ** -0.5

    p = h_lat @ w_in
    q = p[..., :d].reshape(b, rows, GRID_W, nh, hd) * scale
    k = p[..., d:2 * d].reshape(b, rows, GRID_W, nh, hd)
    v = p[..., 2 * d:].reshape(b, rows, GRID_W, nh, hd)

    pc = h_ctx @ (w_in if ctx_out else w_in[:, d:])
    pc = pc[..., d:] if ctx_out else pc
    L = h_ctx.shape[1]
    k_c = pc[..., :d].reshape(b, L, nh, hd)
    v_c = pc[..., d:].reshape(b, L, nh, hd)

    row_start = jnp.clip(jnp.arange(rows) - kh // 2, 0, rows - kh)
    cols = jnp.arange(GRID_W)
    col_start = jnp.clip(cols - kw // 2, 0, GRID_W - kw)
    col_in = (cols[None, :] >= col_start[:, None]) & (cols[None, :] < col_start[:, None] + kw)
    dc_idx = jnp.clip(cols[None, :] - cols[:, None] + NAT_WIN_COLS - 1, 0, 2 * NAT_WIN_COLS - 2)
    rpb_f = rpb.astype(jnp.float32)
    band = kh * GRID_W

    def row_block(args):
        q_r, r = args
        start = row_start[r]
        k_band = lax.dynamic_slice_in_dim(k, start, kh, axis=1)
        v_band = lax.dynamic_slice_in_dim(v, start, kh, axis=1)
        dr_idx = start + jnp.arange(kh) - r + NAT_WIN_ROWS - 1
        bias = rpb_f[:, dr_idx[None, :, None], dc_idx[:, None, :]]
        bias = jnp.where(col_in[:, None, :], bias, -jnp.inf)
        s_loc = jnp.einsum('bqhd,bikhd->bhqik', q_r, k_band).astype(jnp.float32) + bias
        s_ctx = jnp.einsum('bqhd,blhd->bhql', q_r, k_c).astype(jnp.float32)
        s = jnp.concatenate([s_loc.reshape(b, nh, GRID_W, band), s_ctx], axis=-1)
        prob = jax.nn.softmax(s, axis=-1).astype(v.dtype)
        p_loc = prob[..., :band].reshape(b, nh, GRID_W, kh, GRID_W)
        return (jnp.einsum('bhqik,bikhd->bqhd', p_loc, v_band)
                + jnp.einsum('bhql,blhd->bqhd', prob[..., band:], v_c))

    o = lax.map(row_block, (jnp.moveaxis(q, 1, 0), jnp.arange(rows)))
    y_lat = jnp.moveaxis(o, 0, 1).reshape(b, n, d) @ w_o

    y_ctx = None
    if ctx_out:
        q_c = pc_q = (h_ctx @ w_in[:, :d]).reshape(b, L, nh, hd) * scale
        s = jnp.einsum('blhd,bmhd->bhlm', q_c, k_c).astype(jnp.float32)
        prob = jax.nn.softmax(s, axis=-1).astype(v_c.dtype)
        y_ctx = jnp.einsum('bhlm,bmhd->blhd', prob, v_c).reshape(b, L, d) @ w_o
    return y_lat, y_ctx

def sq_relu_mlp(h, w1, w2):
    return jnp.square(jax.nn.relu(h @ w1)) @ w2

def second_inputs(seed: int = 0) -> dict:
    key = jax.random.key(seed)
    ks = jax.random.split(key, 17)
    f32 = jnp.float32

    def nrm(k, shape, scale):
        return jax.random.normal(k, shape, f32) * scale

    qk_w = RET_HEADS * RET_QK_DIM
    v_w = RET_HEADS * RET_V_DIM
    base_decay = jnp.log(-jnp.log(1.0 - 2.0 ** (-5.0 - jnp.arange(RET_HEADS, dtype=f32))))
    return {
        'x': nrm(ks[0], (BATCH, SEQ, D_MODEL), 1.0),
        'c': nrm(ks[1], (BATCH, D_MODEL), 1.0),
        'ctx': nrm(ks[2], (BATCH, CTX_LEN, D_MODEL), 1.0),
        'c_ctx': nrm(ks[3], (D_MODEL,), 1.0),
        'ada_w': nrm(ks[4], (DEPTH, D_MODEL, 6 * D_MODEL), 0.5 * D_MODEL ** -0.5),
        'ada_b': nrm(ks[5], (DEPTH, 6 * D_MODEL), 0.02),
        'ret_w_in': nrm(ks[6], (N_RET_LAYERS, D_MODEL, 2 * qk_w + 2 * v_w), D_MODEL ** -0.5),
        'ret_w_o': nrm(ks[7], (N_RET_LAYERS, v_w, D_MODEL), DN_BETA * v_w ** -0.5),
        'ret_decay': base_decay + nrm(ks[8], (N_RET_LAYERS, 2, RET_HEADS), 0.1),
        'nat_w_in': nrm(ks[9], (N_NAT_LAYERS, D_MODEL, 3 * D_MODEL), D_MODEL ** -0.5),
        'nat_w_o': nrm(ks[10], (N_NAT_LAYERS, D_MODEL, D_MODEL), DN_BETA * D_MODEL ** -0.5),
        'nat_rpb': nrm(ks[11], (N_NAT_LAYERS, NAT_HEADS, 2 * NAT_WIN_ROWS - 1, 2 * NAT_WIN_COLS - 1), 0.1),
        'mlp_w1': nrm(ks[12], (DEPTH, D_MODEL, MLP_HIDDEN), D_MODEL ** -0.5),
        'mlp_w2': nrm(ks[13], (DEPTH, MLP_HIDDEN, D_MODEL), DN_BETA * MLP_HIDDEN ** -0.5),
        'ln_g': 1.0 + nrm(ks[14], (DEPTH, 2, D_MODEL), 0.02),
        'ln_b': nrm(ks[15], (DEPTH, 2, D_MODEL), 0.02),
    }

def second_block(x, c, ctx, c_ctx, ada_w, ada_b, ret_w_in, ret_w_o, ret_decay,
              nat_w_in, nat_w_o, nat_rpb, mlp_w1, mlp_w2, ln_g, ln_b):
    n = x.shape[1]
    ang_row, ang_col = axial_rope_angles(n, RET_QK_DIM // 2)
    silu_c = jax.nn.silu(c)
    silu_cc = jax.nn.silu(c_ctx)
    for i in range(DEPTH):
        last = i == DEPTH - 1
        j = i // N_MIXERS
        mod = (silu_c @ ada_w[i] + ada_b[i])[:, None, :]
        mod_c = silu_cc @ ada_w[i] + ada_b[i]
        sh1, sc1, g1, sh2, sc2, g2 = jnp.split(mod, 6, axis=-1)
        sh1c, sc1c, g1c, sh2c, sc2c, g2c = jnp.split(mod_c, 6, axis=-1)

        h = x * (1.0 + sc1) + sh1
        hc = ctx * (1.0 + sc1c) + sh1c
        if i % N_MIXERS == 0:
            y, yc = retention_mixer(h, hc, ret_w_in[j], ret_w_o[j], ret_decay[j],
                                    ang_row, ang_col, not last)
        else:
            y, yc = neighbourhood_mixer(h, hc, nat_w_in[j], nat_w_o[j], nat_rpb[j], not last)

        x = layer_norm_2(DN_ALPHA * x + g1 * y, ln_g[i, 0], ln_b[i, 0])
        h = x * (1.0 + sc2) + sh2
        x = layer_norm_2(DN_ALPHA * x + g2 * sq_relu_mlp(h, mlp_w1[i], mlp_w2[i]), ln_g[i, 1], ln_b[i, 1])

        if not last:
            ctx = layer_norm_2(DN_ALPHA * ctx + g1c * yc, ln_g[i, 0], ln_b[i, 0])
            hc = ctx * (1.0 + sc2c) + sh2c
            ctx = layer_norm_2(DN_ALPHA * ctx + g2c * sq_relu_mlp(hc, mlp_w1[i], mlp_w2[i]),
                             ln_g[i, 1], ln_b[i, 1])
    return x


def setup_inputs(seed=0):
    out = dict(first_inputs(seed))
    for name, value in second_inputs(seed + 1).items():
        if name != "x":
            out[name + "_2"] = value
    return out


def reference(
    x, w_in, gdn_conv_w, gdn_a_log, gdn_dt_bias, gdn_norm_g, w_out, ln1_g, ln1_b, w_up,
    ffn_conv_w, ffn_conv_b, w_down, ln2_g, ln2_b, c_2, ctx_2, c_ctx_2, ada_w_2, ada_b_2,
    ret_w_in_2, ret_w_o_2, ret_decay_2, nat_w_in_2, nat_w_o_2, nat_rpb_2, mlp_w1_2, mlp_w2_2,
    ln_g_2, ln_b_2,
):
    x = first_block(
        x, w_in, gdn_conv_w, gdn_a_log, gdn_dt_bias, gdn_norm_g, w_out, ln1_g, ln1_b, w_up,
        ffn_conv_w, ffn_conv_b, w_down, ln2_g, ln2_b,
    )
    return second_block(
        x, c_2, ctx_2, c_ctx_2, ada_w_2, ada_b_2, ret_w_in_2, ret_w_o_2, ret_decay_2,
        nat_w_in_2, nat_w_o_2, nat_rpb_2, mlp_w1_2, mlp_w2_2, ln_g_2, ln_b_2,
    )


_drawn_inputs = setup_inputs


def setup_inputs(seed=0):
    import zlib

    import numpy as np

    out = dict(_drawn_inputs(seed))
    spreads = {}
    factors = {'gdn_norm_g': 8.0, 'ffn_conv_b': 8.0, 'ada_b_2': 3.209, 'nat_rpb_2': 64.0}
    for name, (base, spread) in spreads.items():
        noise = np.random.default_rng([zlib.crc32(name.encode()), seed]).standard_normal(out[name].shape)
        drawn = base * np.exp(spread * noise) if base else spread * noise
        out[name] = jnp.asarray(drawn.astype(out[name].dtype))
    for name, factor in factors.items():
        out[name] = (out[name] * factor).astype(out[name].dtype)
    return out
```

```python
from contextlib import ExitStack, contextmanager

import concourse.bass as bass
from concourse import mybir

F32 = mybir.dt.float32
F32R = mybir.dt.float32r
ALU = mybir.AluOpType
ACT = mybir.ActivationFunctionType
AX_X = mybir.AxisListType.X

P = 128
D = 1024
KT = D // P
SEQ = 256
NT = SEQ // P
DEPTH = 2
ALPHA = (2 * DEPTH) ** 0.25
LN_EPS, NORM_EPS = 1e-5, 1e-6
HG, CHUNK = 4, 64
N_CHUNKS = SEQ // CHUNK
HM, DH = 8, 64
D_FF = 2816
FT = D_FF // P
COL_A, COL_Z, COL_QB = 1536, 1544, 2056
RH, RDK, RDV = 4, 256, 512
MLP = 4096
NH, ND = 32, 32
GRID_W = 64
RAW_SLOTS, SPLIT_SLOTS, UNIT = 4, 2, 2048
NEG = -1e30

C_ID, C_TRI, C_BD, C_ONE, C_INC, C_STR, C_M1, C_LEV = (P * i for i in range(8))
C_CAUSAL = C_LEV + 6 * P
C_COS = C_CAUSAL + 3 * P
C_SIN = C_COS + NT * 8
C_HALF = C_SIN + NT * 8
C_NAT = C_HALF + 2
C_MISC = C_NAT + GRID_W
C_FOLD = C_MISC + 2
C_REV = C_FOLD + 2
C_END = C_REV + P
R_DEL, R_COS, R_SIN, R_END = 0, 256, 768, 1280


def constants():
    import numpy as np
    p = np.arange(P)
    c, m = p[:, None], p[None, :]
    same = c // CHUNK == m // CHUNK
    t = np.zeros((P, C_END), np.float32)
    t[:, C_ID:C_ID + P] = c == m
    t[:, C_TRI:C_TRI + P] = same & (c <= m)
    t[:, C_BD:C_BD + P] = same
    t[:, C_ONE:C_ONE + P] = 1
    t[:, C_INC:C_INC + P] = same & (c >= m)
    t[:, C_STR:C_STR + P] = same & (c > m)
    for n in range(6):
        s = 2 ** n
        lev = (c // (2 * s) == m // (2 * s)) & ((c // s) % 2 == 1) & ((m // s) % 2 == 0)
        if n == 0:
            t[:, C_M1:C_M1 + P] = lev
        t[:, C_LEV + n * P:C_LEV + (n + 1) * P] = lev.T
    tri = np.where(c >= m, 0.0, NEG)
    t[:, C_CAUSAL:C_CAUSAL + P] = tri
    t[:, C_CAUSAL + 2 * P:C_CAUSAL + 3 * P] = tri
    inv = np.float32(500000.0) ** (-np.arange(8, dtype=np.float32) / np.float32(8))
    ang = (np.arange(SEQ, dtype=np.float32)[:, None] * inv).reshape(NT, P, 8).transpose(1, 0, 2)
    t[:, C_COS:C_COS + 16] = np.cos(ang).reshape(P, 16)
    t[:, C_SIN:C_SIN + 16] = np.sin(ang).reshape(P, 16)
    t[:, C_HALF] = p < CHUNK
    t[:, C_HALF + 1] = p >= CHUNK
    cq = (GRID_W - 1 - p % GRID_W)[:, None]
    t[:, C_REV:C_REV + P] = (c // GRID_W == m // GRID_W) & (m % GRID_W == cq)
    ck = np.arange(GRID_W)[None, :]
    start = np.clip(cq - 8, 0, GRID_W - 16)
    t[:, C_NAT:C_NAT + GRID_W] = np.where((ck >= start) & (ck < start + 16), 0.0, NEG)
    t[:, C_MISC] = -0.5
    t[:, C_MISC + 1] = 0.0

    t[0:4, C_FOLD:C_FOLD + 2] = np.arange(4)[:, None] % 2 == np.arange(2)[None, :]

    r = np.zeros((P, R_END), np.float32)
    r[:, R_DEL:R_DEL + SEQ] = np.arange(SEQ)[None, :] - p[:, None]
    inv = (1.0 / (np.float32(10000.0) ** (np.arange(0, P, 2, dtype=np.float32) / np.float32(P)))).astype(np.float32)
    tok = np.arange(SEQ)
    for n, pos in enumerate((tok // GRID_W, tok % GRID_W)):
        ang = (pos.astype(np.float32)[:, None] * inv).T
        r[:, R_COS + SEQ * n:R_COS + SEQ * (n + 1)] = np.tile(np.cos(ang), (2, 1))
        r[:, R_SIN + SEQ * n:R_SIN + SEQ * (n + 1)] = np.concatenate([np.sin(ang), -np.sin(ang)], 0)
    return t, r


TURNS = {
    "sync.ada": {"made raw_full0": 32, "made raw_full1": 32, "made raw_full2": 32, "made raw_full3": 32,
        "used w_split": 4},
    "sync.up": {"made raw_full0": 32, "made raw_full1": 32, "made raw_full2": 32, "made raw_full3": 32,
        "used w_split": 4},
    "sync.ret": {"made raw_full0": 64, "made raw_full1": 64, "made raw_full2": 64, "made raw_full3": 64,
        "used w_split": 8},
    "sync.mlp": {"made raw_full0": 64, "made raw_full1": 64, "made raw_full2": 64, "made raw_full3": 64,
        "used w_split": 8},
    "sync.nat": {"made raw_full0": 32, "made raw_full1": 32, "made raw_full2": 32, "made raw_full3": 32,
        "used w_split": 4},
    "gpsimd.ret": {"made pow_out": 1, "used pow_in": 1},
    "scalar.ada": {"made w_hi": 4, "made ada_row": 2, "used w_used": 4, "used raw_full0": 32, "used raw_full1": 32,
        "used raw_full2": 32, "used ada_ps": 2, "used raw_full3": 32},
    "scalar.up": {"made w_hi": 4, "made tap_f": 8, "made silu_f": 4, "made h_hi": 4, "used w_used": 4,
        "used raw_full0": 32, "used raw_full1": 32, "used raw_full2": 32, "used raw_full3": 32, "used up_ps": 4,
        "used conv_f": 4, "used gated": 4},
    "scalar.ret": {"made w_hi": 8, "made a_step": 6, "made r_exp": 2, "made rqk_c": 4, "made rv": 4, "made rg": 4,
        "made rt_hi": 4, "used w_used": 8, "used raw_full0": 64, "used raw_full1": 64, "used raw_full2": 64,
        "used raw_full3": 64, "used proj_ps": 4, "used r_arg": 2, "used rt_ps": 4},
    "scalar.mlp4": {"made w_hi": 8, "made relu": 8, "made hh_hi": 8, "used w_used": 8, "used raw_full0": 64,
        "used raw_full1": 64, "used raw_full2": 64, "used raw_full3": 64, "used up_ps": 4, "used hh": 8,
        "used hm": 8},
    "scalar.nat": {"made w_hi": 4, "made n_q": 16, "made n_exp": 32, "made n_pt": 32, "made nt_hi": 4,
        "used w_used": 4, "used raw_full0": 32, "used raw_full1": 32, "used raw_full2": 32, "used raw_full3": 32,
        "used nqk_ps": 4, "used n_max": 32, "used nt_ps": 32, "used no_ps": 4},
    "scalar.mlp2": {"made w_hi": 8, "made relu": 8, "made hh_hi": 8, "used w_used": 8, "used raw_full0": 64,
        "used raw_full1": 64, "used raw_full2": 64, "used raw_full3": 64, "used up_ps": 4, "used hh": 8,
        "used hm": 8},
    "vector.ada": {"made w_split": 4, "made mod_raw": 2, "used w_hi": 4, "used fold_ps": 2},
    "vector.up": {"made w_split": 4, "made v_step": 12, "made conv_f": 4, "made gated": 4, "made h": 4,
        "used w_hi": 4, "used tap_f": 8, "used silu_f": 4, "used h_hi": 4},
    "vector.ret": {"made w_split": 8, "made v_step": 43, "made pow_in": 1, "made y_add": 8, "made r_arg": 2,
        "made rqk": 2, "made rs": 3, "made ro": 4, "made rt": 4, "used w_hi": 8, "used pow_out": 1,
        "used r_exp": 2, "used rqk_c": 4, "used rs_ps": 3, "used pv_ps": 4, "used rg": 4, "used rt_hi": 4,
        "used dn_ps": 8},
    "vector.mlp4": {"made w_split": 8, "made y_add": 16, "made hh": 8, "made hm": 8, "used w_hi": 8,
        "used dn_ps": 16, "used relu": 8, "used hh_hi": 8},
    "vector.nat": {"made w_split": 4, "made v_step": 64, "made nt": 4, "made n_k": 4, "made n_biased": 32,
        "made n_max": 32, "made n_diag": 32, "used w_hi": 4, "used nqk_ps": 4, "used n_bias": 4, "used ns_ps": 32,
        "used n_exp": 32, "used nt_hi": 4},
    "vector.mlp2": {"made w_split": 8, "made y_add": 8, "made hh": 8, "made hm": 8, "used w_hi": 8,
        "used dn_ps": 8, "used relu": 8, "used hh_hi": 8},
    "tensor.ada": {"made w_used": 4, "made ada_ps": 2, "made fold_ps": 2, "used w_split": 4, "used ada_row": 2},
    "tensor.up": {"made w_used": 4, "made up_ps": 4, "used w_split": 4, "used conv_f": 4},
    "tensor.ret": {"made w_used": 8, "made proj_ps": 4, "made rs_ps": 3, "made pv_ps": 4, "made rt_ps": 4,
        "made dn_ps": 8, "used w_split": 8, "used rqk": 2, "used rv": 4, "used rs": 3, "used ro": 4, "used rg": 4,
        "used rt": 4, "used y_add": 8},
    "tensor.mlp4": {"made w_used": 8, "made up_ps": 4, "made dn_ps": 16, "used w_split": 8, "used y_add": 16,
        "used hh": 8},
    "tensor.nat": {"made w_used": 4, "made nqk_ps": 4, "made ns_ps": 32, "made nt_ps": 32, "made no_ps": 4,
        "used w_split": 4, "used n_q": 16, "used n_k": 4, "used n_diag": 32, "used nt": 4, "used n_v": 4,
        "used n_pt": 32},
    "tensor.mlp2": {"made w_used": 8, "made up_ps": 4, "made dn_ps": 8, "used w_split": 8, "used y_add": 8,
        "used hh": 8},
}


class Lane:

    def __init__(self, name, eng):
        self.name, self.eng = name, eng
        self.made, self.used, self.loop, self.unit = {}, {}, None, 0

    def _value(self, kind, counts, sem):
        counts.setdefault(sem, 0)
        if self.loop is None:
            return counts[sem]
        i, per = self.loop
        step = per.get(f"{kind} {sem}", 0)
        return counts[sem] + i * step if step else counts[sem]

    def gives(self, sem, by=1):
        self.made[sem] = self.made.get(sem, 0) + by
        return by

    def takes(self, sem, by=1):
        self.used[sem] = self.used.get(sem, 0) + by
        return self._value("used", self.used, sem)

    def beyond(self, sem, ahead):
        return self._value("used", self.used, sem) + ahead

    def given(self, sem):
        return self._value("made", self.made, sem)

    @contextmanager
    def turns(self, key, n):
        key = f"{self.name}.{key}"
        per = TURNS.get(key, {})
        kinds = (("made", self.made), ("used", self.used))
        before = {f"{kind} {sem}": v for kind, counts in kinds for sem, v in counts.items()}
        with self.eng.Fori(0, n) as i:
            self.loop = (i, per)
            yield i
            self.loop = None
        found = {}
        for kind, counts in kinds:
            for sem, v in counts.items():
                if v != before.get(f"{kind} {sem}", 0):
                    found[f"{kind} {sem}"] = v - before.get(f"{kind} {sem}", 0)
                    counts[sem] += (n - 1) * found[f"{kind} {sem}"]
        assert found == per, (key, found)


def build(nc, a, out):
    with ExitStack() as ctx:
        held = {}

        def on(name):
            if name not in held:
                held[name] = ctx.enter_context(nc.semaphore(name))
            return held[name]

        def tensors(scope):
            return lambda name, shape, dt=F32: scope.enter_context(nc.sbuf_tensor(name, [P] + shape, dt))

        sb = tensors(ctx)
        cst = sb("cst", [C_END])
        raw = sb("raw", [RAW_SLOTS, UNIT])
        w_hi = sb("w_hi", [SPLIT_SLOTS, UNIT], F32R)
        w_lo = sb("w_lo", [SPLIT_SLOTS, UNIT], F32R)
        xs = sb("xs", [NT, D])
        rows = sb("rows", [3, P])
        par = sb("par", [3, P])
        rows2 = sb("rows2", [2, P])
        par2 = sb("par2", [2, P])
        mod = sb("mod", [DEPTH, 48, 2])
        coef = sb("coef", [7, 2, KT])
        small = sb("small", [64])
        one = ExitStack()
        sb1 = tensors(one)
        lay = sb1("lay", [200])
        xt_hi = sb1("xt_hi", [KT, SEQ], F32R)
        xt_lo = sb1("xt_lo", [KT, SEQ], F32R)
        pa = ExitStack()
        sa = tensors(pa)
        qkv = sa("qkv", [12, SEQ])
        ab_hi = sa("ab_hi", [KT, 8], F32R)
        ab_lo = sa("ab_lo", [KT, 8], F32R)
        k_tok = sa("k_tok", [NT, 512])
        v_beta = sa("v_beta", [NT, 512])
        k_bg = sa("k_bg", [NT, 512])
        k_dec = sa("k_dec", [NT, 512])
        kn = sa("kn", [HG, SEQ])
        dec_y = sa("dec_y", [NT, 512])
        d_inc = sa("d_inc", [NT, 512])
        d_beta = sa("d_beta", [NT, 512])
        a_mat = sa("a_mat", [NT, 512])
        attn = sa("attn", [NT, 512])
        att2 = sa("att2", [2, NT, 512])
        x_inv = sa("x_inv", [NT, 512])
        xt_inv = sa("xt_inv", [NT, 512])
        state = sa("state", [512])
        silu_z = sa("silu_z", [NT, 512])
        gp = sa("gp", [320])
        qk_tok = sa("qk_tok", [NT, 2 * HM, DH])
        v_tok = sa("v_tok", [NT, 512])
        qk_t = sa("qk_t", [2 * HM // 2, SEQ])
        rot = sa("rot", [4, 2 * HM, 8])
        pm = sa("pm", [384])
        pm_t = sa("pm_t", [384])
        ms = sa("ms", [64])
        w_t = d_beta[:, :, :].rearrange("p t (h c) -> p (t h c)", h=4).rearrange("p (h c) -> p h c", h=HG)
        squares = att2[:, :, :, :].rearrange("p a t n -> p (a t n)").rearrange("p (f c) -> p f c", f=8)
        m_lev = [qkv[:, 4:8, :].rearrange("p f c -> p (f c)").rearrange("p (t n) -> p t n", t=NT),
                 qkv[:, 8:12, :].rearrange("p f c -> p (f c)").rearrange("p (t n) -> p t n", t=NT)]
        pa.close()
        pb = ExitStack()
        sbb = tensors(pb)
        pz = ExitStack()
        sz = tensors(pz)
        cs_hl = sz("cs_hl", [KT, P], F32R)
        ada_row = sz("ada_row", [2, 512])
        pz.close()
        h_hi = sbb("h_hi", [FT, SEQ], F32R)
        h_lo = sbb("h_lo", [FT, SEQ], F32R)
        ln_gb = sbb("ln_gb", [2, 2, D])
        xn1 = sbb("xn1", [NT, D])
        xf1 = sbb("xf1", [NT, KT, P])
        hid = sbb("hid", [4, 2, SEQ])
        pb.close()
        one.close()
        two = ExitStack()
        s2 = tensors(two)
        zt_hi = s2("zt_hi", [KT, 2 * SEQ], F32R)
        zt_lo = s2("zt_lo", [KT, 2 * SEQ], F32R)
        xc = s2("xc", [NT, D])
        pc = ExitStack()
        sc = tensors(pc)
        y = sc("y", [2 * NT, D])
        pr = ExitStack()
        sr = tensors(pr)
        rqk = sr("rqk", [2, 2, 2 * SEQ])
        rv = sr("rv", [2 * NT, RDV])
        rg = sr("rg", [2 * NT, RDV])
        rs = sr("rs", [3, 2 * SEQ])
        rt_hi = sr("rt_hi", [4, 2 * SEQ], F32R)
        rt_lo = sr("rt_lo", [4, 2 * SEQ], F32R)
        wd = sr("wd", [2, 2 * SEQ])
        rope = sr("rope", [R_END])
        rtmp = sr("rtmp", [4, SEQ])
        rsm = sr("rsm", [96])
        r_stat = rsm[:, 0:48].rearrange("p (t c) -> p t c", t=4)
        pr.close()
        pm2 = ExitStack()
        sm = tensors(pm2)
        gate_b = sm("gate_b", [2, D])
        gn2 = sm("gn2", [2, D])
        xf2 = sm("xf2", [2, KT, P])
        hm = sm("hm", [4, 2 * SEQ])
        hh_hi = sm("hh_hi", [2, 4, 2 * SEQ], F32R)
        hh_lo = sm("hh_lo", [2, 4, 2 * SEQ], F32R)
        pm2.close()
        pc.close()
        pn = ExitStack()
        sn = tensors(pn)
        nv = sn("nv", [2 * NT, D])
        nq = sn("nq", [2, 4, SEQ])
        nk = sn("nk", [2, 2 * SEQ])
        nb = sn("nb", [2, 4, 6, GRID_W])
        npr = sn("npr", [3, 2 * SEQ])
        npt = sn("npt", [4, NT, P])
        nvf = sn("nvf", [4, 4, P])
        nd = sn("nd", [3, P])
        nt_hi = sn("nt_hi", [KT, SEQ], F32R)
        nt_lo = sn("nt_lo", [KT, SEQ], F32R)
        nsm = sn("nsm", [64])
        pn.close()
        two.close()

        ps = [ctx.enter_context(nc.psum_tensor(f"ps{i}", [P, 512], F32)) for i in range(8)]

        V, A, G, T = nc.vector, nc.scalar, nc.gpsimd, nc.tensor
        ident = cst[:, C_ID:C_ID + P]
        ones = cst[:, C_ONE:C_ONE + P]

        def heads(ap, n):
            return ap.rearrange("p (h c) -> p h c", h=n)

        def per_head(ap, width):
            return ap.unsqueeze(2).to_broadcast([P, ap.shape[1], width])

        def over_heads(ap, n):
            return ap.unsqueeze(1).to_broadcast([P, n, ap.shape[1]])

        def fetch(sp, halves):
            s = sp.unit % RAW_SLOTS
            sp.unit += 1
            sp.eng.wait_ge(on("w_split"), sp.takes("w_split"))
            for n, src in enumerate(halves):
                dst = raw[:, s, n * 1024:(n + 1) * 1024].rearrange("p (k c) -> p k c", k=src.shape[1])
                sp.eng.dma_start(dst, src).then_inc(on(f"raw_full{s}"), sp.gives(f"raw_full{s}", 16))

        def cols_unit(w, c0, c1):
            v = w.rearrange("(k p) n -> p k n", p=P)
            return [v[:, :, bass.ds(c, P)] for c in (c0, c1)]

        def rows_unit(w, k0, c0, n_k=4, width=512):
            v = w.rearrange("(k p) n -> p k n", p=P)
            h = n_k // 2
            return [v[:, bass.ds(k0 + h * j, h), bass.ds(c0, width)] for j in range(2)]

        def split_hi(act):
            s, t = act.unit % RAW_SLOTS, act.unit % SPLIT_SLOTS
            act.unit += 1
            act.eng.wait_ge(on(f"raw_full{s}"), act.takes(f"raw_full{s}", 32))
            if act.started >= SPLIT_SLOTS:
                act.eng.wait_ge(on("w_used"), act.takes("w_used"))
            act.started += 1
            nc.scalar.activation(w_hi[:, t, :], raw[:, s, :], ACT.Copy).then_inc(on("w_hi"), act.gives("w_hi"))

        def split_lo(dve):
            s, t = dve.unit % RAW_SLOTS, dve.unit % SPLIT_SLOTS
            dve.unit += 1
            dve.eng.wait_ge(on("w_hi"), dve.takes("w_hi"))
            nc.vector.tensor_tensor(w_lo[:, t, :], raw[:, s, :], w_hi[:, t, :].bitcast(F32),
                                            ALU.subtract).then_inc(on("w_split"), dve.gives("w_split"))

        def unit_slot(pe):
            t = pe.unit % SPLIT_SLOTS
            pe.unit += 1
            pe.eng.wait_ge(on("w_split"), pe.takes("w_split"))
            return w_hi[:, t, :], w_lo[:, t, :]

        def three(out_ap, l_hi, l_lo, r_hi, r_lo, start, stop):
            first = nc.tensor.matmul(out_ap, l_hi, r_hi, start=start, stop=False)
            nc.tensor.matmul(out_ap, l_hi, r_lo, start=False, stop=False)
            return first, nc.tensor.matmul(out_ap, l_lo, r_hi, start=False, stop=stop)

        def begun(pe, first):
            if not pe.released:
                first.then_inc(on("w_used"), pe.gives("w_used"))
            pe.released = False

        def release(pe):
            t = (pe.unit - 1) % SPLIT_SLOTS
            T.matmul(ps[7][:, 508:510], w_hi[:, t, 0:P], w_hi[:, t, 0:2], start=True, stop=True).then_inc(on("w_used"), pe.gives("w_used"))
            pe.released = True

        def up_unit(pe, outs, x_hi, x_lo, sem, toks=(slice(None), slice(None))):
            hi, lo = unit_slot(pe)
            for f in range(2):
                for k in range(KT):
                    c = f * 1024 + k * P
                    first, last = three(outs[f], hi[:, c:c + P], lo[:, c:c + P], x_hi[:, k, toks[f]],
                                        x_lo[:, k, toks[f]], k == 0, k == KT - 1)
                    if f == k == 0:
                        begun(pe, first)
            last.then_inc(on(sem), pe.gives(sem))

        def rows_product(pe, outs, x_hi, x_lo, ks, first_k, last_k, sem, n_k=4, width=512):
            hi, lo = unit_slot(pe)
            for j in range(n_k):
                for t in range(len(outs)):
                    for c in range(len(outs[t])):
                        w = slice(j * width + c * 512, j * width + (c + 1) * 512)
                        x = slice(t * P, (t + 1) * P)
                        first, last = three(outs[t][c], x_hi[:, ks[j], x], x_lo[:, ks[j], x], hi[:, w], lo[:, w],
                                            first_k and j == 0, last_k and j == n_k - 1)
                        if j == t == c == 0:
                            begun(pe, first)
            if sem:
                last.then_inc(on(sem), pe.gives(sem))

        def mixer_steps():
            rule = ["ss", "gate", "gsum", "kv", "kn", "gram", "turn"]
            for n in range(1, 6):
                rule += [("y", n), ("x", n)]
            rule += ["uw"]
            for n in range(N_CHUNKS):
                rule += [("ws", n), ("ov", n)]
                if n % 2:
                    rule += [("out", n // 2)]
            att = [("mt", n) for n in range(4)]
            for h in range(HM):
                att += [("ma", h), ("mb", h), ("mc", h)]
            order = []
            while rule or att:
                order += rule[:1] + att[:1]
                rule, att = rule[1:], att[1:]
            return order

        def hs(h):
            return slice(h * P, (h + 1) * P)

        def pe_start(pe):
            pe.eng.wait_ge(on("cst_in"), pe.takes("cst_in", 16))
            pe.eng.wait_ge(on("rows2_in"), pe.takes("rows2_in", 80))
            for n in range(2):
                ins = T.transpose(ps[6][:, hs(n)], rows2[:, n, :], ident)
            ins.then_inc(on("par2_ps"), pe.gives("par2_ps"))
            pe.eng.wait_ge(on("x_in"), pe.takes("x_in", 16))
            for t in range(NT):
                for k in range(KT):
                    ins = T.transpose(ps[2 * t + k // 4][:, hs(k % 4)], xs[:, t, k * P:(k + 1) * P], ident)
            ins.then_inc(on("x0_ps"), pe.gives("x0_ps"))

        def pe_params(pe):
            pe.eng.wait_ge(on("rows_in"), pe.takes("rows_in", 16 * 8))
            for n in range(3):
                ins = T.transpose(ps[6][:, hs(n)], rows[:, n, :], ident)
            ins.then_inc(on("par_ps"), pe.gives("par_ps"))

        def pe_mixer(pe, l):
            for u in range(6):
                if u >= 3:
                    pe.eng.wait_ge(on("conv"), pe.takes("conv"))
                b = ps[4 + u % 3] if u % 3 < 2 else ps[0]
                if u == 0 and l == 0:
                    pe.eng.wait_ge(on("x0"), pe.takes("x0", 4))
                up_unit(pe, [b[:, 0:SEQ], b[:, SEQ:2 * SEQ]], xt_hi, xt_lo, "qkv_ps")
                if u == 0:
                    if l == 0:
                        pe.eng.wait_ge(on("mod_raw"), pe.takes("mod_raw", 12 * DEPTH))
                    pe_params(pe)
            pe.eng.wait_ge(on("ab_split"), pe.takes("ab_split"))
            for t in range(NT):
                for k in range(KT):
                    _, ins = three(ps[7][:, 8 * t:8 * t + 8], xt_hi[:, k, t * P:(t + 1) * P],
                                   xt_lo[:, k, t * P:(t + 1) * P], ab_hi[:, k, :], ab_lo[:, k, :],
                                   k == 0, k == KT - 1)
            ins.then_inc(on("ab_ps"), pe.gives("ab_ps"))
            pe.eng.wait_ge(on("conv"), pe.takes("conv", 3))
            for n in range(4):
                if n >= 2:
                    pe.eng.wait_ge(on("tok_out"), pe.takes("tok_out", 2))
                b = 2 * (n % 2)
                for j in range(2):
                    rows_product(pe, [[ps[b + t][:, :]] for t in range(NT)], xt_hi, xt_lo, range(4 * j, 4 * j + 4),
                                 j == 0, j == 1, "proj_ps" if j else None)
            release(pe)
            pe.eng.wait_ge(on("tok_out"), pe.takes("tok_out", 4))
            for step in mixer_steps():
                pe_step(pe, step)
            pe.eng.wait_ge(on("mix_rule"), pe.takes("mix_rule", 2))
            pe.eng.wait_ge(on("mix_att"), pe.takes("mix_att"))
            for c in range(2):
                for j in range(2):
                    rows_product(pe, [[ps[2 * c + t][:, :]] for t in range(NT)], xt_hi, xt_lo,
                                 range(4 * j, 4 * j + 4), j == 0, j == 1, "y_ps" if j else None)
            release(pe)

        def pe_step(pe, step):
            name, n = step if isinstance(step, tuple) else (step, 0)
            if name == "ss":
                pe.eng.wait_ge(on("sq"), pe.takes("sq", 4))
                for t in range(NT):
                    for f in range(8):
                        c = 16 + 8 * t + f
                        ins = T.matmul(ps[7][:, c:c + 1], squares[:, f, t * P:(t + 1) * P], ones[:, 0:1],
                                       start=True, stop=True)
                ins.then_inc(on("ss_ps"), pe.gives("ss_ps"))
            elif name == "gsum":
                pe.eng.wait_ge(on("gates"), pe.takes("gates"))
                for t in range(NT):
                    raw_g = gp[:, 16 + 4 * t:20 + 4 * t]
                    T.matmul(ps[7][:, 32 + 4 * t:36 + 4 * t], cst[:, C_TRI:C_TRI + P], raw_g, start=True, stop=True)
                    T.matmul(ps[7][:, 40 + 4 * t:44 + 4 * t], cst[:, C_BD:C_BD + P], raw_g, start=True, stop=True)
                    ins = T.matmul(ps[7][:, 48 + 8 * t:56 + 8 * t], ones, gp[:, 128 + 8 * t:136 + 8 * t],
                                   start=True, stop=True)
                ins.then_inc(on("gs_ps"), pe.gives("gs_ps"))
                for t in range(NT):
                    for h in range(HG):
                        ins = T.matmul(ps[t][:, hs(h)], dec_y[:, t, hs(h)], cst[:, C_TRI:C_TRI + P],
                                       start=True, stop=True)
                    ins.then_inc(on("grow_ps"), pe.gives("grow_ps"))
            elif name == "kv":
                pe.eng.wait_ge(on("silu"), pe.takes("silu", 6))
                for t in range(NT):
                    for h in range(HG):
                        T.transpose(ps[2 + t][:, hs(h)], qkv[:, 4 + h, t * P:(t + 1) * P], ident)
                    for h in range(HG):
                        ins = T.transpose(ps[4 + t][:, hs(h)], qkv[:, 8 + h, t * P:(t + 1) * P], ident)
                    ins.then_inc(on("kv_ps"), pe.gives("kv_ps"))
            elif name == "kn":
                for t in range(NT):
                    pe.eng.wait_ge(on("kv_out"), pe.takes("kv_out"))
                    for h in range(HG):
                        ins = T.transpose(ps[2 + t][:, hs(h)], k_tok[:, t, hs(h)], ident)
                    ins.then_inc(on("rule_ps"), pe.gives("rule_ps"))
            elif name == "gram":
                for t in range(NT):
                    pe.eng.wait_ge(on("kn"), pe.takes("kn"))
                    tok = slice(t * P, (t + 1) * P)
                    for h in range(HG):
                        T.matmul(ps[4 + t][:, hs(h)], kn[:, h, tok], kn[:, h, tok], start=True, stop=True)
                    for h in range(HG):
                        ins = T.matmul(ps[2 + t][:, hs(h)], qkv[:, h, tok], kn[:, h, tok], start=True, stop=True)
                    ins.then_inc(on("gram_ps"), pe.gives("gram_ps"))
            elif name == "turn":
                for t in range(NT):
                    pe.eng.wait_ge(on("gram"), pe.takes("gram"))
                    for h in range(HG):
                        T.transpose(ps[t][:, hs(h)], a_mat[:, t, hs(h)], ident)
                    for h in range(HG):
                        ins = T.transpose(ps[4 + t][:, hs(h)], attn[:, t, hs(h)], ident)
                    ins.then_inc(on("rule_ps"), pe.gives("rule_ps"))
            elif name == "y":
                for t in range(NT):
                    pe.eng.wait_ge(on("x_inv"), pe.takes("x_inv"))
                    pe.eng.wait_ge(on("m_lev"), pe.takes("m_lev"))
                    for h in range(HG):
                        ins = T.matmul(ps[2 + t][:, hs(h)], m_lev[n % 2][:, t, hs(h)], x_inv[:, t, hs(h)],
                                       start=True, stop=True)
                    ins.then_inc(on("yy_ps"), pe.gives("yy_ps"))
            elif name == "x":
                for t in range(NT):
                    pe.eng.wait_ge(on("yy"), pe.takes("yy"))
                    if n < 5:
                        for h in range(HG):
                            T.matmul(ps[t][:, hs(h)], xt_inv[:, t, hs(h)], dec_y[:, t, hs(h)], start=True, stop=True)
                    for h in range(HG):
                        ins = T.matmul(ps[4 + t][:, hs(h)], dec_y[:, t, hs(h)], xt_inv[:, t, hs(h)],
                                       start=True, stop=True)
                    ins.then_inc(on("xx_ps"), pe.gives("xx_ps"))
            elif name == "uw":
                for t in range(NT):
                    pe.eng.wait_ge(on("x_inv"), pe.takes("x_inv"))
                    if t == 0:
                        pe.eng.wait_ge(on("k_bg"), pe.takes("k_bg", 2))
                    for h in range(HG):
                        T.matmul(ps[2 + t][:, hs(h)], xt_inv[:, t, hs(h)], v_beta[:, t, hs(h)], start=True, stop=True)
                    for h in range(HG):
                        ins = T.matmul(ps[t][:, hs(h)], k_bg[:, t, hs(h)], xt_inv[:, t, hs(h)], start=True, stop=True)
                    ins.then_inc(on("rule_ps"), pe.gives("rule_ps"))
                pe.eng.wait_ge(on("uw"), pe.takes("uw", 2))
            elif name == "ws":
                t, lo = n // 2, CHUNK * (n % 2)
                half, tok = slice(lo, lo + CHUNK), slice(n * CHUNK, (n + 1) * CHUNK)
                pe.eng.wait_ge(on("state" if n else "state0"), pe.takes("state" if n else "state0"))
                for h in range(HG):
                    ins = T.matmul(ps[4][half, hs(h)], w_t[:, h, tok], state[:, hs(h)], start=True, stop=True)
                ins.then_inc(on("ws_ps"), pe.gives("ws_ps"))
                for h in range(HG):
                    ins = T.matmul(ps[t][half, hs(h)], qkv[:, h, tok], state[:, hs(h)], start=True, stop=True)
                ins.then_inc(on("os_ps"), pe.gives("os_ps"))
            elif name == "ov":
                t, lo = n // 2, CHUNK * (n % 2)
                half = slice(lo, lo + CHUNK)
                pe.eng.wait_ge(on("v_new"), pe.takes("v_new"))
                if n < N_CHUNKS - 1:
                    for h in range(HG):
                        ins = T.matmul(ps[5][:, hs(h)], k_dec[half, t, hs(h)], a_mat[half, t, hs(h)],
                                       start=True, stop=True)
                    ins.then_inc(on("st_ps"), pe.gives("st_ps"))
                for h in range(HG):
                    ins = T.matmul(ps[2 + t][half, hs(h)], att2[half, 1, t, h * P + lo:h * P + lo + CHUNK],
                                   a_mat[half, t, hs(h)], start=True, stop=True)
                ins.then_inc(on("ov_ps"), pe.gives("ov_ps"))
            elif name == "out":
                pe.eng.wait_ge(on("o_rule"), pe.takes("o_rule"))
                for h in range(HG):
                    ins = T.transpose(ps[n][:, hs(h)], attn[:, n, hs(h)], ident)
                ins.then_inc(on("rule_ps"), pe.gives("rule_ps"))
            elif name == "mt":
                t, g = n // 2, n % 2
                if g == 0:
                    pe.eng.wait_ge(on("rot"), pe.takes("rot"))
                if n:
                    pe.eng.wait_ge(on("qk_t"), pe.takes("qk_t"))
                for j in range(4):
                    f = 4 * g + j
                    ins = T.transpose(ps[6][:, hs(j)], qk_tok[:, t, 2 * f:2 * f + 2, :].rearrange("p h d -> p (h d)"),
                                      ident)
                ins.then_inc(on("att_ps"), pe.gives("att_ps"))
            elif name == "ma":
                if n == 0:
                    pe.eng.wait_ge(on("qk_t"), pe.takes("qk_t"))
                f, r = n // 2, slice(DH * (n % 2), DH * (n % 2) + DH)
                T.matmul(ps[6][:, 0:P], qk_t[r, f, 0:P], qk_t[r, 4 + f, 0:P], start=True, stop=True)
                ins = T.matmul(ps[6][:, P:3 * P], qk_t[r, f, P:2 * P], qk_t[r, 4 + f, 0:2 * P], start=True, stop=True)
                ins.then_inc(on("ma_ps"), pe.gives("ma_ps"))
            elif name == "mb":
                pe.eng.wait_ge(on("prob"), pe.takes("prob"))
                for j in range(3):
                    ins = T.transpose(ps[6][:, hs(j)], pm[:, hs(j)], ident)
                ins.then_inc(on("att_ps"), pe.gives("att_ps"))
            elif name == "mc":
                pe.eng.wait_ge(on("prob_t"), pe.takes("prob_t"))
                if n % 2 == 0 and n:
                    pe.eng.wait_ge(on("mix_att"), pe.takes("mix_att"))
                r = slice(DH * (n % 2), DH * (n % 2) + DH)
                c = slice(n * DH, (n + 1) * DH)
                T.matmul(ps[7][r, 128:256], v_tok[:, 0, c], pm_t[:, 0:P], start=True, stop=True)
                T.matmul(ps[7][r, 256:384], v_tok[:, 0, c], pm_t[:, P:2 * P], start=True, stop=False)
                ins = T.matmul(ps[7][r, 256:384], v_tok[:, 1, c], pm_t[:, 2 * P:3 * P], start=False, stop=True)
                ins.then_inc(on("att_ps"), pe.gives("att_ps"))

        def pe_norm(pe, src):
            for t in range(NT):
                pe.eng.wait_ge(on("xn"), pe.takes("xn"))
                for k in range(KT):
                    ins = T.transpose(ps[4 + 2 * t + k // 4][:, hs(k % 4)], src(t)[:, k * P:(k + 1) * P], ident)
                ins.then_inc(on("xnt_ps"), pe.gives("xnt_ps"))
            pe.eng.wait_ge(on("xT"), pe.takes("xT", NT))

        def pe_ffn(pe):
            def up(j):
                up_unit(pe, [ps[4 + j % 4][:, 0:SEQ], ps[4 + j % 4][:, SEQ:2 * SEQ]], xt_hi, xt_lo, "up_ps")

            for j in range(2):
                up(j)
            with pe.turns("up", (FT - 2) // 4):
                for j in range(2, 6):
                    pe.eng.wait_ge(on("conv_f"), pe.takes("conv_f"))
                    up(j)
            release(pe)
            pe.eng.wait_ge(on("conv_f"), pe.takes("conv_f", 2))
            pe.eng.wait_ge(on("h"), pe.takes("h", FT))
            for j in range(FT // 2):
                rows_product(pe, [[ps[t][:, :], ps[2 + t][:, :]] for t in range(NT)], h_hi, h_lo,
                             (2 * j, 2 * j + 1), j == 0, j == FT // 2 - 1,
                             "y_ps" if j == FT // 2 - 1 else None, n_k=2, width=D)
            release(pe)

        def sp_layer(sp, l):
            w_in, w_out, w_up, w_down = a["w_in"][l], a["w_out"][l], a["w_up"][l], a["w_down"][l]
            for u in range(6):
                fetch(sp, cols_unit(w_in, 256 * u, 256 * u + P))
            for c0 in (COL_Z, COL_QB, COL_QB + 512, COL_QB + 1024):
                for j in range(2):
                    fetch(sp, rows_unit(w_in, 4 * j, c0))
            for c in range(2):
                for j in range(2):
                    fetch(sp, rows_unit(w_out, 4 * j, 512 * c))
            for j in range(2):
                fetch(sp, cols_unit(w_up, j * P, D_FF + j * P))
            with sp.turns("up", (FT - 2) // 4) as i:
                for j in range(2, 6):
                    c = i * (4 * P) + j * P
                    fetch(sp, cols_unit(w_up, c, c + D_FF))
            for j in range(FT // 2):
                fetch(sp, rows_unit(w_down, 2 * j, 0, n_k=2, width=D))

        def pool_start(pool):
            pool.eng.dma_start(cst[:, :], a["table_1"]).then_inc(on("cst_in"), pool.gives("cst_in", 16))
            G.memset(rows[:, :, :], 0.0).then_inc(on("p_step"), pool.gives("p_step"))
            G.memset(rows2[:, :, :], 0.0).then_inc(on("p_step"), pool.gives("p_step"))
            G.memset(cs_hl[:, :, :].bitcast(F32), 0.0).then_inc(on("cs_zero"), pool.gives("cs_zero"))
            pool.eng.wait_ge(on("p_step"), pool.given("p_step"))

            def as_rows(v):
                return v.rearrange("(r c) -> r c", c=P)

            r = 0
            for v in ("ln_g_2", "ln_b_2"):
                pool.eng.dma_start(rows2[r:r + 32, 0, :], a[v].rearrange("l n (r c) -> (l n r) c", c=P)).then_inc(on("rows2_in"), pool.gives("rows2_in", 16))
                r += 32
            pool.eng.dma_start(rows2[64:72, 0, :], a["c_2"].rearrange("a (r c) -> (a r) c", c=P)).then_inc(on("rows2_in"), pool.gives("rows2_in", 16))
            pool.eng.dma_start(rows2[72:80, 0, :], as_rows(a["c_ctx_2"])).then_inc(on("rows2_in"), pool.gives("rows2_in", 16))
            pool.eng.dma_start(rows2[0:96, 1, :], a["ada_b_2"].rearrange("l (r c) -> (l r) c", c=P)).then_inc(on("rows2_in"), pool.gives("rows2_in", 16))

        def pool_params(pool, l):
            if l:
                pool.eng.wait_ge(on("par_ps"), pool.takes("par_ps"))
            e = pool.eng

            def as_rows(v):
                return v.rearrange("(r c) -> r c", c=P)

            def load(dst, src, sem="rows_in"):
                e.dma_start(dst, src).then_inc(on(sem), pool.gives(sem, 16))

            load(rows[0:48, 2, :], a["gdn_conv_w"][l].rearrange("j (r c) -> (j r) c", c=P))
            load(rows[0:88, 0, :], a["ffn_conv_w"][l, 0:2].rearrange("j (r c) -> (j r) c", c=P))
            for n, v in enumerate(("ln1_g", "ln1_b", "ln2_g", "ln2_b")):
                load(rows[88 + 8 * n:96 + 8 * n, 0, :], as_rows(a[v][l]))
            load(rows[0:44, 1, :], as_rows(a["ffn_conv_w"][l, 2]))
            load(rows[44:88, 1, :], as_rows(a["ffn_conv_b"][l]))
            load(lay[:, 0:4], a["gdn_a_log"][l].partition_broadcast(P), "lay_in")
            load(lay[:, 4:8], a["gdn_dt_bias"][l].partition_broadcast(P), "lay_in")
            load(lay[:, 8:136], a["gdn_norm_g"][l].partition_broadcast(P), "lay_in")
            load(lay[:, 136:200].rearrange("p (k n) -> p k n", n=8),
                 a["w_in"][l].rearrange("(k p) n -> p k n", p=P)[:, :, COL_A:COL_A + 8], "lay_in")

        def pool_gains(pool, l):
            pool.eng.wait_ge(on("y_ps"), pool.takes("y_ps", 2))
            for n in range(2):
                for m, v in enumerate((("ln1_g", "ln1_b"), ("ln2_g", "ln2_b"))[n]):
                    pool.eng.dma_start(ln_gb[:, n, m, :], a[v][l].partition_broadcast(P)).then_inc(on("gains_in"), pool.gives("gains_in", 16))

        def pool_mixer(pool, l):
            if l:
                pool.eng.wait_ge(on("xT"), pool.takes("xT", 2 * NT))
            G.memset(state[:, :], 0.0).then_inc(on("state0"), pool.gives("state0"))
            for step in mixer_steps():
                name, n = step if isinstance(step, tuple) else (step, 0)
                if name == "ss":
                    pool.eng.wait_ge(on("pow_in"), pool.takes("pow_in"))
                    G.tensor_tensor(gp[:, 64:80], gp[:, 64:80],
                                             cst[:, C_MISC:C_MISC + 1].to_broadcast([P, 16]), ALU.pow).then_inc(on("pow_out"), pool.gives("pow_out"))
                elif name == "kv":
                    pool.eng.wait_ge(on("gate_x"), pool.takes("gate_x"))
                    for t in range(NT):
                        pool.eng.wait_ge(on("kv_out"), pool.takes("kv_out"))
                        for dst, at in ((k_bg, 112), (k_dec, 120)):
                            ins = G.tensor_tensor(heads(dst[:, t, :], HG), heads(k_tok[:, t, :], HG),
                                                  per_head(gp[:, at + 4 * t:at + 4 * t + 4], P), ALU.mult)
                        ins.then_inc(on("k_bg"), pool.gives("k_bg"))
                elif name == "turn":
                    for t in range(NT):
                        pool.eng.wait_ge(on("turn_A"), pool.takes("turn_A"))
                        pool_level(pool, 1, t)
                    for t in range(NT):
                        pool_level(pool, 2, t)
                elif name == "x":
                    pool.eng.wait_ge(on("yy_ps"), pool.takes("yy_ps", NT))
                    for t in range(NT if n < 4 else 0):
                        pool_level(pool, n + 2, t)
                elif name == "out":
                    pool.eng.wait_ge(on("pow_in"), pool.takes("pow_in"))
                    at = 176 + 4 * n
                    G.tensor_tensor(gp[:, at:at + 4], gp[:, at:at + 4],
                                             cst[:, C_MISC:C_MISC + 1].to_broadcast([P, 4]), ALU.pow).then_inc(on("pow_out"), pool.gives("pow_out"))

        def pool_level(pool, n, t):
            lev = cst[:, C_LEV + n * P:C_LEV + (n + 1) * P]
            G.tensor_tensor(heads(m_lev[n % 2][:, t, :], HG), heads(att2[:, 0, t, :], HG),
                                     over_heads(lev, HG), ALU.mult).then_inc(on("m_lev"), pool.gives("m_lev"))

        def pool_norm(pool, src, n):
            for t in range(NT):
                pool.eng.wait_ge(on("pow_in"), pool.takes("pow_in"))
                c = 32 * t + 16
                G.tensor_tensor(small[:, c:c + 1], small[:, c:c + 1],
                                         cst[:, C_MISC:C_MISC + 1], ALU.pow).then_inc(on("pow_out"), pool.gives("pow_out"))
            if n == 0:
                pool.eng.wait_ge(on("gains_in"), pool.takes("gains_in", 64))
            for t in range(NT):
                pool.eng.wait_ge(on("xn"), pool.takes("xn"))
                G.tensor_tensor(xs[:, t, :], src(t), ln_gb[:, n, 0, :], ALU.mult).then_inc(on("p_step"), pool.gives("p_step"))
                pool.eng.wait_ge(on("p_step"), pool.given("p_step"))
                G.tensor_tensor(xs[:, t, :], xs[:, t, :], ln_gb[:, n, 1, :], ALU.add).then_inc(on("xs_new"), pool.gives("xs_new"))

        def act_copy(dst, src):
            return A.activation(dst, src, ACT.Copy)

        def act_start(act):
            act.started = 0
            act.used["w_used"] = 1
            for _ in range(SPLIT_SLOTS):
                split_hi(act)
            act.eng.wait_ge(on("par2_ps"), act.takes("par2_ps"))
            act_copy(par2[:, :, :], ps[6][:, 0:2 * P]).then_inc(on("a_step"), act.gives("a_step"))
            act.eng.wait_ge(on("a_step"), act.given("a_step"))
            silu_c = small[:, 0:16]
            A.activation(silu_c, par2[:, 0, 64:80], ACT.Silu).then_inc(on("a_step"), act.gives("a_step"))
            act.eng.wait_ge(on("a_step"), act.given("a_step"))
            act.eng.wait_ge(on("cs_zero"), act.takes("cs_zero"))
            for n in range(2):
                act_copy(cs_hl[:, :, n], small[:, 8 * n:8 * n + 8]).then_inc(on("start_hi"), act.gives("start_hi"))
            act.eng.wait_ge(on("x0_ps"), act.takes("x0_ps"))
            for t in range(NT):
                for g in range(2):
                    act_copy(xt_hi[:, 4 * g:4 * g + 4, t * P:(t + 1) * P], heads(ps[2 * t + g][:, :], 4)).then_inc(on("start_hi"), act.gives("start_hi"))

        def act_mixer(act, l):
            act.eng.wait_ge(on("par_ps"), act.takes("par_ps"))
            act_copy(par[:, :, :], ps[6][:, 0:3 * P]).then_inc(on("par"), act.gives("par"))
            act.eng.wait_ge(on("lay_in"), act.takes("lay_in", 64))
            act_copy(ab_hi[:, :, :], lay[:, 136:200].rearrange("p (k n) -> p k n", n=8)).then_inc(on("ab_hi"), act.gives("ab_hi"))
            act.eng.wait_ge(on("par"), act.given("par"))
            for u in range(6):
                act.eng.wait_ge(on("qkv_ps"), act.takes("qkv_ps"))
                b = ps[4 + u % 3] if u % 3 < 2 else ps[0]
                for g in range(2):
                    f = 2 * u + g
                    A.activation(qkv[:, f, :], b[:, g * SEQ:(g + 1) * SEQ], ACT.Copy,
                                         scale=par[:, 2, 36 + f:37 + f]).then_inc(on("tap"), act.gives("tap"))
                split_hi(act)
                act.eng.wait_ge(on("conv"), act.takes("conv"))
                A.activation(qkv[:, 2 * u:2 * u + 2, :], qkv[:, 2 * u:2 * u + 2, :], ACT.Silu).then_inc(on("silu"), act.gives("silu"))
                if u < 4:
                    act.eng.wait_ge(on("silu"), act.given("silu"))
                    A.activation(squares[:, 2 * u:2 * u + 2, :], qkv[:, 2 * u:2 * u + 2, :], ACT.Square).then_inc(on("sq"), act.gives("sq"))
            for n in range(4):
                split_hi(act)
                act.eng.wait_ge(on("proj_ps"), act.takes("proj_ps"))
                for t in range(NT):
                    src = ps[2 * (n % 2) + t][:, :]
                    if n == 0:
                        ins = A.activation(silu_z[:, t, :], src, ACT.Silu)
                    elif n == 3:
                        ins = act_copy(v_tok[:, t, :], src)
                    else:
                        ins = act_copy(qk_tok[:, t, HM * (n - 1):HM * n, :], heads(src, HM))
                    ins.then_inc(on("tok_out"), act.gives("tok_out"))
                split_hi(act)
            for step in mixer_steps():
                act_step(act, step)
            for _ in range(4):
                split_hi(act)

        def act_step(act, step):
            name, n = step if isinstance(step, tuple) else (step, 0)
            if name == "gate":
                act.eng.wait_ge(on("gate_vec"), act.takes("gate_vec"))
                A.activation(gp[:, 56:64], gp[:, 40:48], ACT.Exp, scale=-1.0).then_inc(on("a_step"), act.gives("a_step"))
                act.eng.wait_ge(on("a_step"), act.given("a_step"))
                A.activation(gp[:, 56:64], gp[:, 56:64], ACT.Ln, bias=ones[:, 0:1]).then_inc(on("a_step"), act.gives("a_step"))
                A.activation(gp[:, 168:172], lay[:, 0:4], ACT.Exp).then_inc(on("a_step"), act.gives("a_step"))
                A.activation(gp[:, 24:32].rearrange("p (t h) -> p t h", t=NT),
                                     gp[:, 0:16].rearrange("p (t h) -> p t h", t=NT)[:, :, 4:8], ACT.Exp,
                                     scale=-1.0).then_inc(on("gate_act"), act.gives("gate_act"))
            elif name == "gsum":
                act.eng.wait_ge(on("gate_vec"), act.takes("gate_vec"))
                A.activation(gp[:, 104:112], gp[:, 88:96], ACT.Exp).then_inc(on("a_step"), act.gives("a_step"))
                A.activation(gp[:, 144:160], ps[7][:, 48:64], ACT.Exp).then_inc(on("gate_act"), act.gives("gate_act"))
                act.eng.wait_ge(on("gate_vec"), act.takes("gate_vec"))
                A.activation(gp[:, 120:128], gp[:, 120:128], ACT.Exp).then_inc(on("gate_x"), act.gives("gate_x"))
                for t in range(NT):
                    act.eng.wait_ge(on("gate_vec"), act.takes("gate_vec"))
                    A.activation(dec_y[:, t, :], dec_y[:, t, :], ACT.Exp).then_inc(on("gate_act"), act.gives("gate_act"))
            elif name == "kn":
                for t in range(NT):
                    act.eng.wait_ge(on("rule_ps"), act.takes("rule_ps"))
                    act_copy(kn[:, :, t * P:(t + 1) * P], heads(ps[2 + t][:, :], HG)).then_inc(on("kn"), act.gives("kn"))
            elif name == "turn":
                for t in range(NT):
                    act.eng.wait_ge(on("rule_ps"), act.takes("rule_ps"))
                    act_copy(att2[:, 0, t, :], ps[t][:, :]).then_inc(on("turn_A"), act.gives("turn_A"))
                    act_copy(att2[:, 1, t, :], ps[4 + t][:, :]).then_inc(on("turn_q"), act.gives("turn_q"))
            elif name == "y":
                for t in range(NT):
                    act.eng.wait_ge(on("yy_ps"), act.takes("yy_ps"))
                    act_copy(dec_y[:, t, :], ps[2 + t][:, :]).then_inc(on("yy"), act.gives("yy"))
            elif name == "uw":
                for t in range(NT):
                    act.eng.wait_ge(on("rule_ps"), act.takes("rule_ps"))
                    act_copy(d_inc[:, t, :], ps[2 + t][:, :]).then_inc(on("a_step"), act.gives("a_step"))
                    act_copy(w_t[:, :, t * P:(t + 1) * P], heads(ps[t][:, :], HG)).then_inc(on("uw"), act.gives("uw"))
            elif name == "out":
                act.eng.wait_ge(on("rule_ps"), act.takes("rule_ps"))
                act_copy(xt_hi[:, 0:HG, n * P:(n + 1) * P], heads(ps[n][:, :], HG)).then_inc(on("o_hi"), act.gives("o_hi"))
            elif name == "mt":
                act.eng.wait_ge(on("att_ps"), act.takes("att_ps"))
                act_copy(qk_t[:, 4 * (n % 2):4 * (n % 2) + 4, (n // 2) * P:(n // 2 + 1) * P],
                                 heads(ps[6][:, :], 4)).then_inc(on("qk_t"), act.gives("qk_t"))
            elif name == "ma":
                act.eng.wait_ge(on("p_max"), act.takes("p_max"))
                A.activation(pm[:, 0:P], pm[:, 0:P], ACT.Exp, bias=ms[:, 2:3], scale=DH ** -0.5,
                                     accum_out=ms[:, 4:5]).then_inc(on("a_step"), act.gives("a_step"))
                A.activation(pm[:, P:3 * P], pm[:, P:3 * P], ACT.Exp, bias=ms[:, 3:4], scale=DH ** -0.5,
                                     accum_out=ms[:, 5:6]).then_inc(on("p_exp"), act.gives("p_exp"))
            elif name == "mb":
                act.eng.wait_ge(on("att_ps"), act.takes("att_ps"))
                act_copy(pm_t[:, :], ps[6][:, 0:3 * P]).then_inc(on("prob_t"), act.gives("prob_t"))
            elif name == "mc":
                act.eng.wait_ge(on("att_ps"), act.takes("att_ps"))
                if n % 2:
                    act_copy(xt_hi[:, 4 + n // 2, :], ps[7][:, P:3 * P]).then_inc(on("a_hi"), act.gives("a_hi"))

        def act_norm(act, gain, bias, fine, hi):
            for t in range(NT):
                act.eng.wait_ge(on("xnt_ps"), act.takes("xnt_ps"))
                for k in range(KT):
                    A.activation(fine[:, t, k, :], ps[4 + 2 * t + k // 4][:, hs(k % 4)], ACT.Identity,
                                         scale=gain[:, k:k + 1], bias=bias[:, k:k + 1]).then_inc(on("a_step"), act.gives("a_step"))
                act.eng.wait_ge(on("a_step"), act.given("a_step"))
                act_copy(hi[:, :, t * P:(t + 1) * P], fine[:, t, :, :]).then_inc(on("x_hi"), act.gives("x_hi"))

        def act_ffn(act):
            def up(j, f):
                act.eng.wait_ge(on("up_ps"), act.takes("up_ps"))
                b = ps[4 + j % 4]
                for g in range(2):
                    A.activation(hid[:, j % 4, g, :], b[:, g * SEQ:(g + 1) * SEQ], ACT.Identity,
                                 scale=par[:, 1, bass.ds(f + FT * g, 1)],
                                 bias=par[:, 1, bass.ds(f + 44 + FT * g, 1)]).then_inc(on("tap_f"), act.gives("tap_f"))
                split_hi(act)
                if j:
                    up_end(j - 1, f - 1)
                act.eng.wait_ge(on("conv_f"), act.takes("conv_f"))
                A.activation(hid[:, j % 4, 0, :], hid[:, j % 4, 0, :], ACT.Silu).then_inc(
                    on("silu_f"), act.gives("silu_f"))

            def up_end(j, f):
                act.eng.wait_ge(on("gated"), act.takes("gated"))
                act_copy(h_hi[:, bass.ds(f, 1), :], hid[:, j % 4, 1:2, :]).then_inc(on("h_hi"), act.gives("h_hi"))

            for j in range(2):
                up(j, j)
            with act.turns("up", (FT - 2) // 4) as i:
                for j in range(2, 6):
                    up(j, 4 * i + j)
            up_end(FT - 1, FT - 1)
            for _ in range(FT // 2):
                split_hi(act)

        def dve_start(dve):
            dve.eng.sem_inc(on("w_split"), RAW_SLOTS)
            for _ in range(SPLIT_SLOTS):
                split_lo(dve)
            dve.eng.wait_ge(on("start_hi"), dve.takes("start_hi", 2))
            for n in range(2):
                V.tensor_tensor(cs_hl[:, :, 2 + n], small[:, 8 * n:8 * n + 8],
                                        cs_hl[:, :, n].bitcast(F32), ALU.subtract).then_inc(on("c_lo"), dve.gives("c_lo"))
            dve.eng.wait_ge(on("x0_ps"), dve.takes("x0_ps"))
            for t in range(NT):
                for g in range(2):
                    dve.eng.wait_ge(on("start_hi"), dve.takes("start_hi"))
                    x = (slice(None), slice(4 * g, 4 * g + 4), slice(t * P, (t + 1) * P))
                    V.tensor_tensor(xt_lo[x], heads(ps[2 * t + g][:, :], 4), xt_hi[x].bitcast(F32),
                                            ALU.subtract).then_inc(on("x0"), dve.gives("x0"))

        def taps(dve, dst, src, weights):
            for d, w in enumerate(weights, 1):
                V.scalar_tensor_tensor(dst[:, d:SEQ], src[:, 0:SEQ - d], w, dst[:, d:SEQ], ALU.mult, ALU.add).then_inc(on("v_step"), dve.gives("v_step"))
                dve.eng.wait_ge(on("v_step"), dve.given("v_step"))

        def dve_mixer(dve, l):
            dve.eng.wait_ge(on("ab_hi"), dve.takes("ab_hi"))
            V.tensor_tensor(ab_lo[:, :, :], lay[:, 136:200].rearrange("p (k n) -> p k n", n=8),
                                    ab_hi[:, :, :].bitcast(F32), ALU.subtract).then_inc(on("ab_split"), dve.gives("ab_split"))
            dve.eng.wait_ge(on("par"), dve.takes("par"))
            for u in range(6):
                b = ps[4 + u % 3] if u % 3 < 2 else ps[0]
                dve.eng.wait_ge(on("tap"), dve.takes("tap", 2))
                for g in range(2):
                    f = 2 * u + g
                    dst, src = qkv[:, f, :], b[:, g * SEQ:(g + 1) * SEQ]
                    w = [par[:, 2, 12 * j + f:12 * j + f + 1] for j in (2, 1, 0)]
                    taps(dve, dst, src, w if g == 0 else w[:2])
                V.scalar_tensor_tensor(dst[:, 3:SEQ], src[:, 0:SEQ - 3], w[2], dst[:, 3:SEQ],
                                               ALU.mult, ALU.add).then_inc(on("conv"), dve.gives("conv"))
                split_lo(dve)
            for _ in range(8):
                split_lo(dve)
            dve.eng.wait_ge(on("tok_out"), dve.takes("tok_out", 8))
            for step in mixer_steps():
                dve_step(dve, step)
            for _ in range(4):
                split_lo(dve)

        def dve_step(dve, step):
            name, n = step if isinstance(step, tuple) else (step, 0)
            tt, tsc = V.tensor_tensor, V.tensor_scalar

            def two_by(ap):
                return ap.rearrange("p (t h) -> p t h", t=NT)

            if name == "ss":
                dve.eng.wait_ge(on("ss_ps"), dve.takes("ss_ps"))
                tsc(gp[:, 64:80], ps[7][:, 16:32], NORM_EPS, None, ALU.add).then_inc(on("pow_in"), dve.gives("pow_in"))
            elif name == "gate":
                dve.eng.wait_ge(on("ab_ps"), dve.takes("ab_ps"))
                V.tensor_copy(gp[:, 0:16], ps[7][:, 0:16]).then_inc(on("v_step"), dve.gives("v_step"))
                dve.eng.wait_ge(on("v_step"), dve.given("v_step"))
                tt(two_by(gp[:, 32:40]), two_by(gp[:, 0:16])[:, :, 0:4], over_heads(lay[:, 4:8], NT), ALU.add).then_inc(on("v_step"), dve.gives("v_step"))
                dve.eng.wait_ge(on("v_step"), dve.given("v_step"))
                x = gp[:, 32:40]
                V.scalar_tensor_tensor(gp[:, 40:48], x, -1.0, x, ALU.mult, ALU.max).then_inc(on("gate_vec"), dve.gives("gate_vec"))
                dve.eng.wait_ge(on("gate_act"), dve.takes("gate_act"))
                V.scalar_tensor_tensor(x, x, 0.0, gp[:, 56:64], ALU.max, ALU.add).then_inc(on("v_step"), dve.gives("v_step"))
                dve.eng.wait_ge(on("v_step"), dve.given("v_step"))
                V.scalar_tensor_tensor(two_by(gp[:, 16:24]), two_by(x), -1.0, over_heads(gp[:, 168:172], NT),
                                               ALU.mult, ALU.mult).then_inc(on("v_step"), dve.gives("v_step"))
                tsc(gp[:, 24:32], gp[:, 24:32], 1.0, None, ALU.add).then_inc(on("v_step"), dve.gives("v_step"))
                dve.eng.wait_ge(on("v_step"), dve.given("v_step"))
                V.reciprocal(gp[:, 24:32], gp[:, 24:32]).then_inc(on("v_step"), dve.gives("v_step"))
                dve.eng.wait_ge(on("v_step"), dve.given("v_step"))
                gm = gp[:, 128:144].rearrange("p (t a h) -> p t a h", t=NT, a=2)
                for half in range(2):
                    tsc(gm[:, :, half, :], two_by(gp[:, 16:24]), cst[:, C_HALF + half:C_HALF + half + 1], None,
                                ALU.mult).then_inc(on("v_step"), dve.gives("v_step"))
                for t in range(NT):
                    ins = tt(heads(dec_y[:, t, :], HG), over_heads(ones, HG),
                             per_head(gp[:, 16 + 4 * t:20 + 4 * t], P), ALU.mult)
                    ins.then_inc(on("v_step" if t == 0 else "gates"), dve.gives("v_step" if t == 0 else "gates"))
                for t in range(NT):
                    tt(heads(silu_z[:, t, :], HG), heads(silu_z[:, t, :], HG), over_heads(lay[:, 8:136], HG),
                               ALU.mult).then_inc(on("v_step"), dve.gives("v_step"))
            elif name == "gsum":
                dve.eng.wait_ge(on("gs_ps"), dve.takes("gs_ps"))
                V.tensor_copy(gp[:, 88:104], ps[7][:, 32:48]).then_inc(on("gate_vec"), dve.gives("gate_vec"))
                dve.eng.wait_ge(on("gate_vec"), dve.given("gate_vec"))
                tt(gp[:, 120:128], gp[:, 96:104], gp[:, 88:96], ALU.subtract).then_inc(on("v_step"), dve.gives("v_step"))
                dve.eng.wait_ge(on("v_step"), dve.given("v_step"))
                dve.eng.wait_ge(on("gate_act"), dve.takes("gate_act"))
                dve.eng.wait_ge(on("pow_out"), dve.takes("pow_out"))
                tt(gp[:, 112:120], gp[:, 24:32], gp[:, 104:112], ALU.mult).then_inc(on("v_step"), dve.gives("v_step"))
                tsc(two_by(gp[:, 80:88]), two_by(gp[:, 64:80])[:, :, 0:4], float(P) ** -0.5, None, ALU.mult).then_inc(on("gate_vec"), dve.gives("gate_vec"))
                for t in range(NT):
                    dve.eng.wait_ge(on("grow_ps"), dve.takes("grow_ps"))
                    tt(heads(dec_y[:, t, :], HG), heads(ps[t][:, :], HG),
                                per_head(gp[:, 88 + 4 * t:92 + 4 * t], P), ALU.subtract).then_inc(on("v_step"), dve.gives("v_step"))
                    dve.eng.wait_ge(on("v_step"), dve.given("v_step"))
                    tsc(dec_y[:, t, :], dec_y[:, t, :], 0.0, -1.0, ALU.max, ALU.mult).then_inc(on("gate_vec"), dve.gives("gate_vec"))
                for t in range(NT):
                    dve.eng.wait_ge(on("gate_act"), dve.takes("gate_act"))
                    d = heads(dec_y[:, t, :], HG)
                    tt(heads(d_inc[:, t, :], HG), d, over_heads(cst[:, C_INC:C_INC + P], HG), ALU.mult).then_inc(on("v_step"), dve.gives("v_step"))
                    tt(heads(d_beta[:, t, :], HG), d, over_heads(cst[:, C_STR:C_STR + P], HG), ALU.mult).then_inc(on("v_step"), dve.gives("v_step"))
                    dve.eng.wait_ge(on("v_step"), dve.given("v_step"))
                    tt(heads(d_beta[:, t, :], HG), heads(d_beta[:, t, :], HG),
                               per_head(gp[:, 24 + 4 * t:28 + 4 * t], P), ALU.mult).then_inc(on("v_step"), dve.gives("v_step"))
            elif name == "kv":
                for t in range(NT):
                    dve.eng.wait_ge(on("kv_ps"), dve.takes("kv_ps"))
                    tt(heads(k_tok[:, t, :], HG), heads(ps[2 + t][:, :], HG),
                               per_head(gp[:, 68 + 8 * t:72 + 8 * t], P), ALU.mult).then_inc(on("v_step"), dve.gives("v_step"))
                    tt(heads(v_beta[:, t, :], HG), heads(ps[4 + t][:, :], HG),
                               per_head(gp[:, 24 + 4 * t:28 + 4 * t], P), ALU.mult).then_inc(on("kv_out"), dve.gives("kv_out"))
            elif name == "gram":
                dve.eng.wait_ge(on("v_step"), dve.given("v_step"))
                for t in range(NT):
                    dve.eng.wait_ge(on("gram_ps"), dve.takes("gram_ps"))
                    tt(a_mat[:, t, :], ps[4 + t][:, :], d_beta[:, t, :], ALU.mult).then_inc(on("v_step"), dve.gives("v_step"))
                    tt(attn[:, t, :], ps[2 + t][:, :], d_inc[:, t, :], ALU.mult).then_inc(on("gram"), dve.gives("gram"))
            elif name == "turn":
                dve.eng.wait_ge(on("v_step"), dve.given("v_step"))
                for t in range(NT):
                    id4 = over_heads(ident, HG)
                    xi, xti = heads(x_inv[:, t, :], HG), heads(xt_inv[:, t, :], HG)
                    tt(xi, heads(a_mat[:, t, :], HG), over_heads(cst[:, C_M1:C_M1 + P], HG), ALU.mult).then_inc(on("v_step"), dve.gives("v_step"))
                    dve.eng.wait_ge(on("v_step"), dve.given("v_step"))
                    tt(xi, id4, xi, ALU.subtract).then_inc(on("v_step"), dve.gives("v_step"))
                    dve.eng.wait_ge(on("turn_A"), dve.takes("turn_A"))
                    tt(xti, heads(att2[:, 0, t, :], HG), over_heads(cst[:, C_LEV:C_LEV + P], HG), ALU.mult).then_inc(on("v_step"), dve.gives("v_step"))
                    dve.eng.wait_ge(on("v_step"), dve.given("v_step"))
                    tt(xti, id4, xti, ALU.subtract).then_inc(on("x_inv"), dve.gives("x_inv"))
            elif name == "x":
                dve.eng.wait_ge(on("x_inv"), dve.given("x_inv"))
                dve.eng.wait_ge(on("v_step"), dve.given("v_step"))
                for t in range(NT):
                    dve.eng.wait_ge(on("xx_ps"), dve.takes("xx_ps"))
                    if n < 5:
                        tt(x_inv[:, t, :], x_inv[:, t, :], ps[t][:, :], ALU.subtract).then_inc(on("v_step"), dve.gives("v_step"))
                    tt(xt_inv[:, t, :], xt_inv[:, t, :], ps[4 + t][:, :], ALU.subtract).then_inc(on("x_inv"), dve.gives("x_inv"))
            elif name == "ws":
                t, lo = n // 2, CHUNK * (n % 2)
                half = slice(lo, lo + CHUNK)
                if n == 0:
                    dve.eng.wait_ge(on("uw"), dve.takes("uw", NT))
                dve.eng.wait_ge(on("ws_ps"), dve.takes("ws_ps"))
                tt(a_mat[half, t, :], d_inc[half, t, :], ps[4][half, :], ALU.subtract).then_inc(on("v_new"), dve.gives("v_new"))
            elif name == "ov":
                t, c = n // 2, 144 + 4 * n
                dve.eng.wait_ge(on("os_ps"), dve.takes("os_ps"))
                if n < N_CHUNKS - 1:
                    if n:
                        dve.eng.wait_ge(on("state"), dve.given("state"))
                    else:
                        dve.eng.wait_ge(on("state0"), dve.takes("state0"))
                    tt(heads(state[:, :], HG), heads(state[:, :], HG), per_head(gp[:, c:c + 4], P), ALU.mult).then_inc(on("v_step"), dve.gives("v_step"))
                    dve.eng.wait_ge(on("v_step"), dve.given("v_step"))
                    dve.eng.wait_ge(on("st_ps"), dve.takes("st_ps"))
                    tt(state[:, :], state[:, :], ps[5][:, :], ALU.add).then_inc(on("state"), dve.gives("state"))
            elif name == "out":
                t = n
                dve.eng.wait_ge(on("ov_ps"), dve.takes("ov_ps", 2))
                o = heads(attn[:, t, :], HG)
                tt(o, heads(ps[t][:, :], HG), per_head(gp[:, 104 + 4 * t:108 + 4 * t], P), ALU.mult).then_inc(on("v_step"), dve.gives("v_step"))
                dve.eng.wait_ge(on("v_step"), dve.given("v_step"))
                tt(attn[:, t, :], attn[:, t, :], ps[2 + t][:, :], ALU.add).then_inc(on("v_step"), dve.gives("v_step"))
                dve.eng.wait_ge(on("v_step"), dve.given("v_step"))
                tt(o, o, per_head(gp[:, 80 + 4 * t:84 + 4 * t], P), ALU.mult).then_inc(on("v_step"), dve.gives("v_step"))
                dve.eng.wait_ge(on("v_step"), dve.given("v_step"))
                tt(x_inv[:, t, :], attn[:, t, :], attn[:, t, :], ALU.mult).then_inc(on("v_step"), dve.gives("v_step"))
                dve.eng.wait_ge(on("v_step"), dve.given("v_step"))
                r = gp[:, 176 + 4 * t:180 + 4 * t]
                V.tensor_reduce(r, heads(x_inv[:, t, :], HG), AX_X, ALU.add).then_inc(on("v_step"), dve.gives("v_step"))
                dve.eng.wait_ge(on("v_step"), dve.given("v_step"))
                tsc(r, r, 1.0 / P, NORM_EPS, ALU.mult, ALU.add).then_inc(on("pow_in"), dve.gives("pow_in"))
                dve.eng.wait_ge(on("pow_out"), dve.takes("pow_out"))
                tt(o, o, per_head(r, P), ALU.mult).then_inc(on("v_step"), dve.gives("v_step"))
                dve.eng.wait_ge(on("v_step"), dve.given("v_step"))
                tt(attn[:, t, :], attn[:, t, :], silu_z[:, t, :], ALU.mult).then_inc(on("o_rule"), dve.gives("o_rule"))
                dve.eng.wait_ge(on("o_hi"), dve.takes("o_hi"))
                dst = (slice(None), slice(0, HG), slice(t * P, (t + 1) * P))
                tt(xt_lo[dst], heads(ps[t][:, :], HG), xt_hi[dst].bitcast(F32), ALU.subtract).then_inc(on("mix_rule"), dve.gives("mix_rule"))
            elif name == "mt" and n % 2 == 0:
                t = n // 2
                x1, x2 = qk_tok[:, t, :, 0:8], qk_tok[:, t, :, 8:16]
                cos = over_heads(cst[:, C_COS + 8 * t:C_COS + 8 * t + 8], 2 * HM)
                sin = over_heads(cst[:, C_SIN + 8 * t:C_SIN + 8 * t + 8], 2 * HM)
                for i, (x, w) in enumerate(((x1, cos), (x2, sin), (x2, cos), (x1, sin))):
                    tt(rot[:, i, :, :], x, w, ALU.mult).then_inc(on("v_step"), dve.gives("v_step"))
                dve.eng.wait_ge(on("v_step"), dve.given("v_step"))
                tt(x1, rot[:, 0, :, :], rot[:, 1, :, :], ALU.subtract).then_inc(on("v_step"), dve.gives("v_step"))
                tt(x2, rot[:, 2, :, :], rot[:, 3, :, :], ALU.add).then_inc(on("rot"), dve.gives("rot"))
            elif name == "ma":
                dve.eng.wait_ge(on("ma_ps"), dve.takes("ma_ps"))
                tt(pm[:, :], ps[6][:, 0:3 * P], cst[:, C_CAUSAL:C_CAUSAL + 3 * P], ALU.add).then_inc(on("v_step"), dve.gives("v_step"))
                dve.eng.wait_ge(on("v_step"), dve.given("v_step"))
                V.tensor_reduce(ms[:, 0:1], pm[:, 0:P], AX_X, ALU.max).then_inc(on("v_step"), dve.gives("v_step"))
                V.tensor_reduce(ms[:, 1:2], pm[:, P:3 * P], AX_X, ALU.max).then_inc(on("v_step"), dve.gives("v_step"))
                dve.eng.wait_ge(on("v_step"), dve.given("v_step"))
                tsc(ms[:, 2:4], ms[:, 0:2], -DH ** -0.5, None, ALU.mult).then_inc(on("p_max"), dve.gives("p_max"))
                dve.eng.wait_ge(on("p_exp"), dve.takes("p_exp"))
                V.reciprocal(ms[:, 6:8], ms[:, 4:6]).then_inc(on("v_step"), dve.gives("v_step"))
                dve.eng.wait_ge(on("v_step"), dve.given("v_step"))
                tsc(pm[:, 0:P], pm[:, 0:P], ms[:, 6:7], None, ALU.mult).then_inc(on("v_step"), dve.gives("v_step"))
                tsc(pm[:, P:3 * P], pm[:, P:3 * P], ms[:, 7:8], None, ALU.mult).then_inc(on("prob"), dve.gives("prob"))
            elif name == "mc" and n % 2:
                dve.eng.wait_ge(on("a_hi"), dve.takes("a_hi"))
                tt(xt_lo[:, 4 + n // 2, :], ps[7][:, P:3 * P], xt_hi[:, 4 + n // 2, :].bitcast(F32),
                           ALU.subtract).then_inc(on("mix_att"), dve.gives("mix_att"))

        def dve_statistics(dve, x, t):
            c = 32 * t
            for j in range(2):
                V.bn_stats(small[:, c + 6 * j:c + 6 * j + 6], x[:, 512 * j:512 * j + 512]).then_inc(on("v_step"), dve.gives("v_step"))
            dve.eng.wait_ge(on("v_step"), dve.given("v_step"))
            V.bn_aggr(small[:, c + 12:c + 14], small[:, c:c + 12]).then_inc(on("v_step"), dve.gives("v_step"))
            dve.eng.wait_ge(on("v_step"), dve.given("v_step"))
            V.tensor_scalar(small[:, c + 16:c + 17], small[:, c + 13:c + 14], LN_EPS, None, ALU.add).then_inc(on("pow_in"), dve.gives("pow_in"))

        def dve_norm(dve, halves, fine, hi, lo):
            for c in range(2):
                if c < halves:
                    dve.eng.wait_ge(on("y_ps"), dve.takes("y_ps"))
                for t in range(NT):
                    x = xs[:, t, 512 * c:512 * c + 512]
                    V.scalar_tensor_tensor(x, x, ALPHA, ps[2 * c + t][:, :], ALU.mult, ALU.add).then_inc(on("v_step"), dve.gives("v_step"))
            dve.eng.wait_ge(on("v_step"), dve.given("v_step"))
            for t in range(NT):
                dve_statistics(dve, xs[:, t, :], t)
            for t in range(NT):
                dve.eng.wait_ge(on("pow_out"), dve.takes("pow_out"))
                c = 32 * t
                V.tensor_scalar(xn1[:, t, :], xs[:, t, :], small[:, c + 12:c + 13], small[:, c + 16:c + 17],
                                        ALU.subtract, ALU.mult).then_inc(on("xn"), dve.gives("xn"))
            for t in range(NT):
                dve.eng.wait_ge(on("x_hi"), dve.takes("x_hi"))
                x = (slice(None), slice(None), slice(t * P, (t + 1) * P))
                V.tensor_tensor(lo[x], fine[:, t, :, :], hi[x].bitcast(F32), ALU.subtract).then_inc(on("xT"), dve.gives("xT"))

        def dve_ffn(dve):
            def up(j, f):
                b = ps[4 + j % 4]
                dve.eng.wait_ge(on("tap_f"), dve.takes("tap_f", 2))
                for d in (1, 2):
                    for g in range(2):
                        dst, src = hid[:, j % 4, g, :], b[:, g * SEQ:(g + 1) * SEQ]
                        w = par[:, 0, bass.ds(f + 44 * (2 - d) + FT * g, 1)]
                        sem = "conv_f" if g == 1 and d == 2 else "v_step"
                        V.scalar_tensor_tensor(dst[:, d:SEQ], src[:, 0:SEQ - d], w, dst[:, d:SEQ],
                                               ALU.mult, ALU.add).then_inc(on(sem), dve.gives(sem))
                    if d == 1:
                        dve.eng.wait_ge(on("v_step"), dve.given("v_step"))
                if j:
                    up_gate(j - 1)
                split_lo(dve)
                if j:
                    up_end(j - 1, f - 1)

            def up_gate(j):
                dve.eng.wait_ge(on("silu_f"), dve.takes("silu_f"))
                V.tensor_tensor(hid[:, j % 4, 1, :], hid[:, j % 4, 0, :], hid[:, j % 4, 1, :], ALU.mult).then_inc(
                    on("gated"), dve.gives("gated"))

            def up_end(j, f):
                dve.eng.wait_ge(on("gated"), dve.given("gated"))
                dve.eng.wait_ge(on("h_hi"), dve.takes("h_hi"))
                V.tensor_tensor(h_lo[:, bass.ds(f, 1), :], hid[:, j % 4, 1:2, :],
                                h_hi[:, bass.ds(f, 1), :].bitcast(F32), ALU.subtract).then_inc(on("h"), dve.gives("h"))

            for j in range(2):
                up(j, j)
            with dve.turns("up", (FT - 2) // 4) as i:
                for j in range(2, 6):
                    up(j, 4 * i + j)
            up_gate(FT - 1)
            up_end(FT - 1, FT - 1)
            for _ in range(FT // 2):
                split_lo(dve)

        def pe_ada(pe, l):
            def fold(b):
                pe.eng.wait_ge(on("ada_row"), pe.takes("ada_row"))
                for f in range(4):
                    ins = T.matmul(ps[6 + b][:, 2 * f:2 * f + 2], ada_row[0:4, b, hs(f)],
                                   cst[0:4, C_FOLD:C_FOLD + 2], start=True, stop=True)
                ins.then_inc(on("fold_ps"), pe.gives("fold_ps"))

            with pe.turns("ada", 6):
                for b in range(2):
                    for j in range(2):
                        hi, lo = unit_slot(pe)
                        for k in range(4):
                            w = slice(512 * k, 512 * k + 512)
                            ins = T.matmul(ps[4 + b][:, :], cs_hl[:, 4 * j + k, :], hi[:, w],
                                           start=j == k == 0, stop=False)
                            if j == k == 0:
                                ins.then_inc(on("w_used"), pe.gives("w_used"))
                            ins = T.matmul(ps[4 + b][:, :], cs_hl[:, 4 * j + k, :], lo[:, w],
                                           start=False, stop=j == 1 and k == 3)
                        if j == 0:
                            ins.then_inc(on("w_used"), pe.gives("w_used"))
                            if b == 1:
                                fold(0)
                    ins.then_inc(on("ada_ps"), pe.gives("ada_ps"))
                fold(1)

        def act_ada(act):
            with act.turns("ada", 6):
                for b in range(2):
                    split_hi(act)
                    act.eng.wait_ge(on("ada_ps"), act.takes("ada_ps"))
                    act_copy(ada_row[0:4, b, :], ps[4 + b][0:4, :]).then_inc(on("ada_row"), act.gives("ada_row"))
                    split_hi(act)

        def dve_ada(dve, l):
            with dve.turns("ada", 6) as i:
                for b in range(2):
                    for j in range(2):
                        split_lo(dve)
                        if j != b:
                            dve.eng.wait_ge(on("fold_ps"), dve.takes("fold_ps"))
                            V.tensor_copy(mod[:, l, bass.ds(8 * i + 4 * b, 4), :],
                                          ps[6 + b][:, 0:8].rearrange("p (f s) -> p f s", s=2)).then_inc(
                                              on("mod_raw"), dve.gives("mod_raw"))

        def dve_coef(dve, n, gain, bias, l, chunk, stream, sem="v_step"):
            sh = mod[:, l, 8 * chunk:8 * chunk + 8, stream]
            sc_ = mod[:, l, 8 * chunk + 8:8 * chunk + 16, stream]
            if gain is None:
                V.tensor_scalar(coef[:, n, 0, :], sc_, 1.0, None, ALU.add).then_inc(on("v_step"), dve.gives("v_step"))
                V.tensor_copy(coef[:, n, 1, :], sh).then_inc(on(sem), dve.gives(sem))
            else:
                V.scalar_tensor_tensor(coef[:, n, 0, :], sc_, 1.0, gain, ALU.add, ALU.mult).then_inc(on("v_step"), dve.gives("v_step"))
                V.scalar_tensor_tensor(coef[:, n, 1, :], sc_, 1.0, bias, ALU.add, ALU.mult).then_inc(on("v_step"), dve.gives("v_step"))
                dve.eng.wait_ge(on("v_step"), dve.given("v_step"))
                V.tensor_tensor(coef[:, n, 1, :], coef[:, n, 1, :], sh, ALU.add).then_inc(on(sem), dve.gives(sem))

        def dve_mods(dve):
            dve.eng.wait_ge(on("mod_raw"), dve.given("mod_raw"))
            for l in range(DEPTH):
                V.tensor_tensor(mod[:, l, :, :], mod[:, l, :, :], per_head(par2[:, 1, 48 * l:48 * l + 48], 2),
                                         ALU.add).then_inc(on("v_step"), dve.gives("v_step"))
                dve.eng.wait_ge(on("v_step"), dve.given("v_step"))

            def ln(i, j):
                c = 8 * (2 * i + j)
                return par2[:, 0, c:c + 8], par2[:, 0, 32 + c:40 + c]

            dve_coef(dve, 0, None, None, 0, 0, 1)
            dve_coef(dve, 2, *ln(0, 0), 0, 3, 0)
            dve_coef(dve, 3, *ln(0, 0), 0, 3, 1)
            dve_coef(dve, 4, *ln(0, 1), 1, 0, 0)
            dve_coef(dve, 5, *ln(0, 1), 1, 0, 1)
            dve_coef(dve, 6, *ln(1, 0), 1, 3, 0, "coef")

        def x_of(t):
            return xc[:, t, :] if t < NT else xs[:, t - NT, :]

        def stream_of(t):
            return 1 if t < NT else 0

        def pe_turned(pe, src, bank):
            for k in range(KT):
                ins = T.transpose(ps[bank + k // 4][:, hs(k % 4)], src[:, k * P:(k + 1) * P], ident)
            ins.then_inc(on("xnt_ps"), pe.gives("xnt_ps"))

        def act_turned(act, t, bank, n):
            act.eng.wait_ge(on("xnt_ps"), act.takes("xnt_ps"))
            if act.turned >= 2:
                act.eng.wait_ge(on("zT"), act.takes("zT"))
            fine = xf2[:, act.turned % 2, :, :]
            act.turned += 1
            for k in range(KT):
                A.activation(fine[:, k, :], ps[bank + k // 4][:, hs(k % 4)], ACT.Identity,
                                     scale=coef[:, n, 0, k:k + 1], bias=coef[:, n, 1, k:k + 1]).then_inc(on("a_step"), act.gives("a_step"))
            act.eng.wait_ge(on("a_step"), act.given("a_step"))
            act_copy(zt_hi[:, :, t * P:(t + 1) * P], fine).then_inc(on("z_hi"), act.gives("z_hi"))

        def dve_turned(dve, t):
            dve.eng.wait_ge(on("z_hi"), dve.takes("z_hi"))
            x = (slice(None), slice(None), slice(t * P, (t + 1) * P))
            V.tensor_tensor(zt_lo[x], xf2[:, t % 2, :, :], zt_hi[x].bitcast(F32), ALU.subtract).then_inc(on("zT"), dve.gives("zT"))

        def dve_gates(dve, l, chunk, tiles):
            for s in sorted({stream_of(t) for t in tiles}):
                V.tensor_tensor(xf2[:, s, :, :], over_heads(ident, KT),
                                per_head(mod[:, l, 8 * chunk:8 * chunk + 8, s], P), ALU.mult).then_inc(
                                    on("diag"), dve.gives("diag"))

        def pe_gates(pe, tiles):
            for s in sorted({stream_of(t) for t in tiles}):
                pe.eng.wait_ge(on("diag"), pe.takes("diag"))
                for k in range(KT):
                    ins = T.matmul(ps[4 + 2 * s + k // 4][:, hs(k % 4)], ones, xf2[:, s, k, :], start=True, stop=True)
                ins.then_inc(on("gate_ps"), pe.gives("gate_ps"))

        def pe_gates_end(pe, tiles):
            n = 2 * len({stream_of(t) for t in tiles})
            pe.eng.wait_ge(on("gate_b"), pe.takes("gate_b", n))

        def act_gates(act, tiles):
            for s in sorted({stream_of(t) for t in tiles}):
                act.eng.wait_ge(on("gate_ps"), act.takes("gate_ps"))
                for j in range(2):
                    act_copy(gate_b[:, s, 512 * j:512 * j + 512], ps[4 + 2 * s + j][:, :]).then_inc(
                        on("gate_b"), act.gives("gate_b"))

        def pe_norm2(pe, tiles):
            for n, t in enumerate(tiles):
                pe.eng.wait_ge(on("zn"), pe.takes("zn"))
                if n >= 2:
                    pe.eng.wait_ge(on("zT"), pe.takes("zT"))
                pe_turned(pe, y[:, t, :], 4 + 2 * (n % 2))
            pe.eng.wait_ge(on("zT"), pe.takes("zT", 2))

        def act_norm2(act, tiles, coefs):
            for n, t in enumerate(tiles):
                act_turned(act, t, 4 + 2 * (n % 2), coefs[stream_of(t)])

        def dve_norm2(dve, tiles, last, banks=None):
            def residual(t):
                if banks:
                    for c in range(2):
                        w = slice(512 * c, 512 * c + 512)
                        V.tensor_tensor(y[:, t, w], banks[2 * c + t - NT][:, :], gate_b[:, 0, w], ALU.mult).then_inc(
                            on("v_step"), dve.gives("v_step"))
                else:
                    V.tensor_tensor(y[:, t, :], y[:, t, :], gate_b[:, stream_of(t), :], ALU.mult).then_inc(
                        on("v_step"), dve.gives("v_step"))
                dve.eng.wait_ge(on("v_step"), dve.given("v_step"))
                V.scalar_tensor_tensor(x_of(t), x_of(t), ALPHA, y[:, t, :], ALU.mult, ALU.add).then_inc(
                    on("v_step"), dve.gives("v_step"))
                dve.eng.wait_ge(on("v_step"), dve.given("v_step"))
                dve_statistics(dve, x_of(t), t % 2)

            def normal(t):
                dve.eng.wait_ge(on("pow_out"), dve.takes("pow_out"))
                c = 32 * (t % 2)
                V.tensor_scalar(y[:, t, :], x_of(t), small[:, c + 12:c + 13], small[:, c + 16:c + 17],
                                ALU.subtract, ALU.mult).then_inc(on("zn"), dve.gives("zn"))

            dve.eng.wait_ge(on("y_add"), dve.given("y_add"))
            dve.eng.wait_ge(on("gate_b"), dve.takes("gate_b", 2 * len({stream_of(t) for t in tiles})))
            residual(tiles[0])
            for n in range(1, len(tiles) + 2):
                if n < len(tiles):
                    residual(tiles[n])
                if n <= len(tiles):
                    normal(tiles[n - 1])
                if n >= 2 and not last:
                    dve_turned(dve, tiles[n - 2])
            if not last:
                dve.eng.wait_ge(on("zT"), dve.given("zT"))

        def pool_norm2(pool, l, m, tiles):
            def power(t):
                pool.eng.wait_ge(on("pow_in"), pool.takes("pow_in"))
                c = 32 * (t % 2) + 16
                G.tensor_tensor(small[:, c:c + 1], small[:, c:c + 1], cst[:, C_MISC:C_MISC + 1], ALU.pow).then_inc(
                    on("pow_out"), pool.gives("pow_out"))

            pool.eng.wait_ge(on("gate_b"), pool.takes("gate_b", 2 * len({stream_of(t) for t in tiles})))
            pool.eng.wait_ge(on("zs_new"), pool.given("zs_new"))
            for j, v in enumerate(("ln_g_2", "ln_b_2")):
                pool.eng.dma_start(gn2[:, j, :], a[v][l, m].partition_broadcast(P)).then_inc(
                    on("gn2_in"), pool.gives("gn2_in", 16))
            power(tiles[0])
            for n, t in enumerate(tiles):
                if n + 1 < len(tiles):
                    power(tiles[n + 1])
                pool.eng.wait_ge(on("zn"), pool.takes("zn"))
                if n == 0:
                    pool.eng.wait_ge(on("gn2_in"), pool.takes("gn2_in", 32))
                G.tensor_tensor(x_of(t), y[:, t, :], gn2[:, 0, :], ALU.mult).then_inc(
                    on("p_step"), pool.gives("p_step"))
                pool.eng.wait_ge(on("p_step"), pool.given("p_step"))
                G.tensor_tensor(x_of(t), x_of(t), gn2[:, 1, :], ALU.add).then_inc(
                    on("zs_new"), pool.gives("zs_new"))

        def down_unit(pe, h_hi_, h_lo_, tiles, banks):
            hi, lo = unit_slot(pe)
            for n, t in enumerate(tiles):
                pe.eng.wait_ge(on("y_add"), pe.takes("y_add"))
                x = slice(n * P, (n + 1) * P)
                for k in range(4):
                    w = slice(512 * k, 512 * k + 512)
                    first, last = three(ps[banks[n]][:, :], h_hi_[:, k, x], h_lo_[:, k, x], hi[:, w], lo[:, w],
                                        k == 0, k == 3)
                    if n == k == 0:
                        begun(pe, first)
                last.then_inc(on("dn_ps"), pe.gives("dn_ps"))

        def dve_add(dve, c, tiles, banks):
            for n, t in enumerate(tiles):
                dve.eng.wait_ge(on("dn_ps"), dve.takes("dn_ps"))
                yt = y[:, t, 512 * c:512 * c + 512]
                V.tensor_tensor(yt, yt, ps[banks[n]][:, :], ALU.add).then_inc(on("y_add"), dve.gives("y_add"))

        ALL, LAT = (0, 1, 2, 3), (2, 3)

        def sp_ret(sp):
            w, w_o = a["ret_w_in_2"][0], a["ret_w_o_2"][0]
            with sp.turns("ret", RH) as h:
                for base in (0, RH * RDK):
                    fetch(sp, cols_unit(w, h * RDK + base, h * RDK + (base + P)))
                for base in (2 * RH * RDK, 2 * RH * RDK + RH * RDV):
                    for j in range(2):
                        fetch(sp, rows_unit(w, 4 * j, h * RDV + base))
                for c in range(2):
                    fetch(sp, rows_unit(w_o, h * 4, 512 * c))

        def pe_ret(pe):
            with pe.turns("ret", RH):
                for n in range(2):
                    up_unit(pe, [ps[2 * n][:, :], ps[2 * n + 1][:, :]], zt_hi, zt_lo, "proj_ps")
                for j in range(2):
                    rows_product(pe, [[ps[4 + t][:, :]] for t in ALL], zt_hi, zt_lo, range(4 * j, 4 * j + 4),
                                 j == 0, j == 1, "proj_ps" if j else None)
                pe.eng.wait_ge(on("rqk"), pe.takes("rqk", 2))
                for st in range(2):
                    for f in range(2):
                        ins = T.matmul(ps[st][:, :], rqk[:, 1, f, st * P:(st + 1) * P], rqk[:, 0, f, :],
                                       start=f == 0, stop=f == 1)
                    ins.then_inc(on("rs_ps"), pe.gives("rs_ps"))
                for st in range(2):
                    for f in range(2):
                        c = SEQ + st * P
                        ins = T.matmul(ps[2][:, st * SEQ:(st + 1) * SEQ], rqk[:, 1, f, c:c + P],
                                       rqk[:, 0, f, SEQ:2 * SEQ], start=f == 0, stop=f == 1)
                ins.then_inc(on("rs_ps"), pe.gives("rs_ps"))
                pe.eng.wait_ge(on("rv"), pe.takes("rv", 4))
                pe.eng.wait_ge(on("rs"), pe.takes("rs", 3))
                for t in ALL:
                    keys = [(rs[:, st, t * P:(t + 1) * P], st) for st in range(2)]
                    if t >= NT:
                        keys += [(rs[:, 2, st * SEQ + (t - NT) * P:st * SEQ + (t - NT + 1) * P], NT + st)
                                 for st in range(2)]
                    for n, (s_, v) in enumerate(keys):
                        ins = T.matmul(ps[4 + t][:, :], s_, rv[:, v, :], start=n == 0, stop=n == len(keys) - 1)
                    ins.then_inc(on("pv_ps"), pe.gives("pv_ps"))
                for j in range(2):
                    rows_product(pe, [[ps[t][:, :]] for t in ALL], zt_hi, zt_lo, range(4 * j, 4 * j + 4),
                                 j == 0, j == 1, "proj_ps" if j else None)
                pe.eng.wait_ge(on("ro"), pe.takes("ro", 4))
                for f in range(4):
                    for t in ALL:
                        ins = T.transpose(ps[4 + f][:, hs(t)], rv[:, t, hs(f)], ident)
                    ins.then_inc(on("rt_ps"), pe.gives("rt_ps"))
                pe.eng.wait_ge(on("rg"), pe.takes("rg", 4))
                pe.eng.wait_ge(on("rt"), pe.takes("rt", 4))
                for c in range(2):
                    down_unit(pe, rt_hi, rt_lo, ALL, ALL)
                pe.eng.wait_ge(on("y_add"), pe.beyond("y_add", 4))
                release(pe)

        def act_ret(act):
            act.eng.wait_ge(on("rdec_in"), act.takes("rdec_in", 32))
            A.activation(rsm[:, 72:80], rsm[:, 72:80], ACT.Exp).then_inc(on("r_lg"), act.gives("r_lg"))
            with act.turns("ret", RH):
                split_hi(act)
                split_hi(act)
                for st in range(2):
                    act.eng.wait_ge(on("r_arg"), act.takes("r_arg"))
                    for n, c in ((0, 80), (1, 82), (2, 80), (3, 81)):
                        A.activation(rtmp[:, n, :], rtmp[:, n, :], ACT.Exp, scale=rsm[:, c:c + 1]).then_inc(on("a_step" if n < 3 else "r_exp"), act.gives("a_step" if n < 3 else "r_exp"))
                for n in range(2):
                    act.eng.wait_ge(on("proj_ps"), act.takes("proj_ps"))
                    for f in range(2):
                        act_copy(rqk[:, n, f, 0:SEQ], ps[2 * n + f][:, 0:SEQ]).then_inc(on("rqk_c"), act.gives("rqk_c"))
                act.eng.wait_ge(on("proj_ps"), act.takes("proj_ps"))
                split_hi(act)
                for t in ALL:
                    act_copy(rv[:, t, :], ps[4 + t][:, :]).then_inc(on("rv"), act.gives("rv"))
                split_hi(act)
                split_hi(act)
                act.eng.wait_ge(on("proj_ps"), act.takes("proj_ps"))
                for t in ALL:
                    A.activation(rg[:, t, :], ps[t][:, :], ACT.Silu).then_inc(on("rg"), act.gives("rg"))
                for f in range(4):
                    act.eng.wait_ge(on("rt_ps"), act.takes("rt_ps"))
                    act_copy(rt_hi[:, f, :], ps[4 + f][:, :]).then_inc(on("rt_hi"), act.gives("rt_hi"))
                for _ in range(3):
                    split_hi(act)

        def dve_ret(dve):
            dve.eng.wait_ge(on("r_lg"), dve.takes("r_lg"))
            V.tensor_scalar(rsm[:, 84:92], rsm[:, 72:80], -1.0, None, ALU.mult).then_inc(on("v_step"), dve.gives("v_step"))
            dve.eng.wait_ge(on("v_step"), dve.given("v_step"))
            delta = rope[:, R_DEL:R_DEL + SEQ]
            stt, tsc = V.scalar_tensor_tensor, V.tensor_scalar
            for t in ALL:
                V.memset(y[:, t, :], 0.0).then_inc(on("v_step"), dve.gives("v_step"))
            with dve.turns("ret", RH) as h:
                split_lo(dve)
                V.tensor_copy(rsm[:, 80:82].unsqueeze(2),
                                       rsm[:, 84:92].rearrange("p (d h) -> p d h", d=2)[:, :, bass.ds(h, 1)]).then_inc(on("v_step"), dve.gives("v_step"))
                dve.eng.wait_ge(on("v_step"), dve.given("v_step"))
                tsc(rsm[:, 82:83], rsm[:, 81:82], -1.0, None, ALU.mult).then_inc(on("v_step"), dve.gives("v_step"))
                dve.eng.wait_ge(on("v_step"), dve.given("v_step"))
                for st in range(2):
                    o = float(P * st)
                    tsc(rtmp[:, 0, :], delta, -o, 0.0, ALU.add, ALU.max).then_inc(on("v_step"), dve.gives("v_step"))
                    tsc(rtmp[:, 1, :], delta, -o, 0.0, ALU.add, ALU.min).then_inc(on("v_step"), dve.gives("v_step"))
                    tsc(rtmp[:, 2, :], delta, SEQ - o, None, ALU.add).then_inc(on("v_step"), dve.gives("v_step"))
                    tsc(rtmp[:, 3, :], delta, -1.0, SEQ + o, ALU.mult, ALU.add).then_inc(on("r_arg"), dve.gives("r_arg"))
                    if st == 0:
                        split_lo(dve)
                    dve.eng.wait_ge(on("r_exp"), dve.takes("r_exp"))
                    stt(wd[:, st, 0:SEQ], delta, o, rtmp[:, 0, :], ALU.is_ge, ALU.mult).then_inc(on("v_step"), dve.gives("v_step"))
                    stt(rtmp[:, 1, :], delta, o, rtmp[:, 1, :], ALU.is_le, ALU.mult).then_inc(on("v_step"), dve.gives("v_step"))
                    dve.eng.wait_ge(on("v_step"), dve.given("v_step"))
                    V.tensor_tensor(wd[:, st, 0:SEQ], wd[:, st, 0:SEQ], rtmp[:, 1, :], ALU.add).then_inc(on("v_step"), dve.gives("v_step"))
                    V.tensor_tensor(wd[:, st, SEQ:2 * SEQ], rtmp[:, 2, :], rtmp[:, 3, :], ALU.add).then_inc(on("v_step"), dve.gives("v_step"))
                    dve.eng.wait_ge(on("v_step"), dve.given("v_step"))
                for n in range(2):
                    dve.eng.wait_ge(on("rqk_c"), dve.takes("rqk_c", 2))
                    for f in range(2):
                        x, out_ = ps[2 * n + f], rqk[:, n, f, SEQ:2 * SEQ]
                        cos = rope[:, R_COS + SEQ * f:R_COS + SEQ * (f + 1)]
                        sin = rope[:, R_SIN + SEQ * f:R_SIN + SEQ * (f + 1)]
                        V.tensor_tensor(out_, x[:, SEQ:2 * SEQ], cos, ALU.mult).then_inc(on("v_step"), dve.gives("v_step"))
                        for lo_, hi_ in ((0, 64), (64, 0)):
                            V.tensor_tensor(rtmp[lo_:lo_ + 64, 0, :], x[hi_:hi_ + 64, SEQ:2 * SEQ],
                                                    sin[hi_:hi_ + 64, :], ALU.mult).then_inc(on("v_step"), dve.gives("v_step"))
                        dve.eng.wait_ge(on("v_step"), dve.given("v_step"))
                        V.tensor_tensor(out_, out_, rtmp[:, 0, :], ALU.add).then_inc(on("rqk" if f else "v_step"), dve.gives("rqk" if f else "v_step"))
                        dve.eng.wait_ge(on("rqk" if f else "v_step"), dve.given("rqk" if f else "v_step"))
                split_lo(dve)
                for st in range(2):
                    dve.eng.wait_ge(on("rs_ps"), dve.takes("rs_ps"))
                    stt(rs[:, st, :], ps[st][:, :], RDK ** -0.5, wd[:, st, :], ALU.mult, ALU.mult).then_inc(on("rs"), dve.gives("rs"))
                dve.eng.wait_ge(on("rs_ps"), dve.takes("rs_ps"))
                stt(heads(rs[:, 2, :], 2), heads(ps[2][:, :], 2), RDK ** -0.5, wd[:, :, 0:SEQ],
                            ALU.mult, ALU.mult).then_inc(on("rs"), dve.gives("rs"))
                split_lo(dve)
                for t in ALL:
                    dve.eng.wait_ge(on("pv_ps"), dve.takes("pv_ps"))
                    V.bn_stats(rsm[:, 12 * t:12 * t + 6], ps[4 + t][:, :]).then_inc(on("v_step"), dve.gives("v_step"))
                dve.eng.wait_ge(on("v_step"), dve.given("v_step"))
                V.memset(rsm[:, 95:96], 0.0).then_inc(on("v_step"), dve.gives("v_step"))
                for t in ALL:
                    V.bn_aggr(rsm[:, 12 * t + 6:12 * t + 8], rsm[:, 12 * t:12 * t + 6]).then_inc(on("v_step"), dve.gives("v_step"))
                dve.eng.wait_ge(on("v_step"), dve.given("v_step"))
                tsc(r_stat[:, :, 8:9], r_stat[:, :, 7:8], LN_EPS, None, ALU.add).then_inc(on("pow_in"), dve.gives("pow_in"))
                split_lo(dve)
                dve.eng.wait_ge(on("pow_out"), dve.takes("pow_out"))
                for t in ALL:
                    c = 12 * t
                    tsc(rv[:, t, :], ps[4 + t][:, :], rsm[:, c + 6:c + 7], rsm[:, c + 8:c + 9],
                                ALU.subtract, ALU.mult).then_inc(on("v_step"), dve.gives("v_step"))
                dve.eng.wait_ge(on("v_step"), dve.given("v_step"))
                for t in ALL:
                    dve.eng.wait_ge(on("rg"), dve.takes("rg"))
                    V.tensor_tensor(rv[:, t, :], rv[:, t, :], rg[:, t, :], ALU.mult).then_inc(on("ro"), dve.gives("ro"))
                for f in range(4):
                    dve.eng.wait_ge(on("rt_hi"), dve.takes("rt_hi"))
                    V.tensor_tensor(rt_lo[:, f, :], ps[4 + f][:, :], rt_hi[:, f, :].bitcast(F32),
                                            ALU.subtract).then_inc(on("rt"), dve.gives("rt"))
                for c in range(2):
                    split_lo(dve)
                    dve.eng.wait_ge(on("y_add"), dve.given("y_add"))
                    dve_add(dve, c, ALL, ALL)
                split_lo(dve)

        def pool_ret(pool):
            with pool.turns("ret", RH):
                pool.eng.wait_ge(on("pow_in"), pool.takes("pow_in"))
                G.tensor_tensor(r_stat[:, :, 8], r_stat[:, :, 8],
                                         cst[:, C_MISC:C_MISC + 1].to_broadcast([P, 4]), ALU.pow).then_inc(on("pow_out"), pool.gives("pow_out"))

        def mlp_order():
            return (("up", 0),), (("up", 1), ("down", 0), ("up", 0), ("down", 1)), \
                (("up", 1), ("down", 0), ("down", 1))

        MLP_TURNS = MLP // 512 // 2 - 1
        last_down = "last"


        def mlp_program(lane, key, step):
            first, turn, last = mlp_order()
            chunk = {"up": 0, "down": 0}

            def run(steps, i):
                for what, b in steps:
                    step(what, b, i + chunk[what])
                    chunk[what] += 1

            run(first, 0)
            with lane.turns(key, MLP_TURNS) as i:
                run(turn, i * 2)
            for what in chunk:
                chunk[what] += 2 * (MLP_TURNS - 1)
            run(last[:-1], 0)
            step(*last[-1], last_down)

        def sp_mlp(sp, l):
            w1, w2 = a["mlp_w1_2"][l], a["mlp_w2_2"][l]

            def step(what, b, c):
                c = MLP // 512 - 1 if c is last_down else c
                for j in range(2):
                    if what == "up":
                        fetch(sp, cols_unit(w1, c * 512 + 256 * j, c * 512 + (256 * j + P)))
                    else:
                        fetch(sp, rows_unit(w2, c * 4, 512 * j))

            mlp_program(sp, "mlp", step)

        def down_banks(j, tiles):
            return (4, 5, 6, 7) if len(tiles) == 4 else (4 + 2 * j, 5 + 2 * j)

        def pe_mlp(pe, tiles):
            tok = slice(tiles[0] * P, 2 * SEQ)
            n_tok = len(tiles) * P

            def up(j):
                pe.eng.wait_ge(on("hh"), pe.takes("hh", 2))
                up_unit(pe, [ps[2 * j][:, 0:n_tok], ps[2 * j + 1][:, 0:n_tok]], zt_hi, zt_lo, "up_ps", (tok, tok))

            def step(what, b, c):
                for j in range(2):
                    if what == "up":
                        up(j)
                        if j == 0 and pe.loop is None and c == 0:
                            pe_gates(pe, tiles)
                    else:
                        if j == 0 and c is last_down:
                            pe.eng.wait_ge(on("hh"), pe.takes("hh", 4))
                        down_unit(pe, hh_hi[:, b, :, :], hh_lo[:, b, :, :], tiles, down_banks(j, tiles))
                if what == "up" and pe.loop is None and c == 0:
                    pe_gates_end(pe, tiles)

            mlp_program(pe, f"mlp{len(tiles)}", step)
            pe.eng.wait_ge(on("y_add"), pe.beyond("y_add", 4))
            release(pe)

        def act_mlp(act, tiles, final=False):
            n_tok = len(tiles) * P

            def step(what, b, c):
                for j in range(2):
                    if what == "up":
                        act.eng.wait_ge(on("up_ps"), act.takes("up_ps"))
                        act.eng.wait_ge(on("hh"), act.takes("hh", 2))
                        for f in range(2):
                            A.activation(hm[:, 2 * j + f, 0:n_tok], ps[2 * j + f][:, 0:n_tok], ACT.Relu).then_inc(on("relu"), act.gives("relu"))
                        for f in range(2):
                            act.eng.wait_ge(on("hm"), act.takes("hm"))
                            act_copy(hh_hi[:, b, 2 * j + f, 0:n_tok], hm[:, 2 * j + f, 0:n_tok]).then_inc(on("hh_hi"), act.gives("hh_hi"))
                    if not (final and c is last_down):
                        split_hi(act)
                    if what == "up" and j == 0 and act.loop is None and c == 0:
                        act_gates(act, tiles)

            mlp_program(act, f"mlp{len(tiles)}", step)
            act.eng.wait_ge(on("hh"), act.takes("hh", 4))

        def dve_mlp(dve, tiles, final=False):
            n_tok = len(tiles) * P

            def step(what, b, c):
                for j in range(2):
                    if what == "up":
                        for f in range(2):
                            dve.eng.wait_ge(on("relu"), dve.takes("relu"))
                            r2 = hm[:, 2 * j + f, 0:n_tok]
                            V.tensor_tensor(r2, r2, ps[2 * j + f][:, 0:n_tok], ALU.mult).then_inc(on("hm"), dve.gives("hm"))
                        dve.eng.wait_ge(on("hm"), dve.given("hm"))
                        split_lo(dve)
                        for f in range(2):
                            dve.eng.wait_ge(on("hh_hi"), dve.takes("hh_hi"))
                            V.tensor_tensor(hh_lo[:, b, 2 * j + f, 0:n_tok], hm[:, 2 * j + f, 0:n_tok],
                                                    hh_hi[:, b, 2 * j + f, 0:n_tok].bitcast(F32), ALU.subtract).then_inc(on("hh"), dve.gives("hh"))
                    else:
                        dve.eng.wait_ge(on("y_add"), dve.given("y_add"))
                        dve_add(dve, j, tiles, down_banks(j, tiles))
                        if not (final and c is last_down):
                            split_lo(dve)

            dve.eng.wait_ge(on("zs_new"), dve.takes("zs_new", len(tiles)))
            dve.eng.sem_inc(on("hh"), 4)
            dve.made["hh"] = dve.made.get("hh", 0) + 4
            for t in tiles:
                V.memset(y[:, t, :], 0.0).then_inc(on("y_zero"), dve.gives("y_zero"))
            dve.eng.wait_ge(on("y_zero"), dve.given("y_zero"))
            mlp_program(dve, f"mlp{len(tiles)}", step)

        NF = D // P
        NAT_TURN = 4
        NAT_STEPS = NAT_TURN * 8
        S_BANK = (2, 3, 6)

        def sp_nat(sp):
            w, w_o = a["nat_w_in_2"][0], a["nat_w_o_2"][0]
            for c in range(2):
                for j in range(2):
                    fetch(sp, rows_unit(w, 4 * j, 2 * D + 512 * c))
            with sp.turns("nat", NF // NAT_TURN) as i:
                for j in range(NAT_TURN):
                    f = i * (NAT_TURN * P) + j * P
                    fetch(sp, cols_unit(w, f, f + D))
            for c in range(2):
                for j in range(2):
                    fetch(sp, rows_unit(w_o, 4 * j, 512 * c))

        def pool_nat(pool):
            pool.eng.wait_ge(on("zT"), pool.takes("zT", 2 * len(ALL)))
            pool.eng.wait_ge(on("zs_new"), pool.given("zs_new"))
            G.memset(nq[:, :, :, :], 0.0).then_inc(on("nq_zero"), pool.gives("nq_zero"))
            rpb = a["nat_rpb_2"]
            for f in range(NF):
                b = f % 2
                if f >= 2:
                    pool.eng.wait_ge(on("n_biased"), pool.takes("n_biased", 8))
                for half in range(2):
                    for h in range(4):
                        src = bass.AP(rpb.tensor, (4 * f + h) * 15 * 31 + (5 - half) * 31 + 15 - (GRID_W - 1),
                                        [[1, GRID_W], [31, 6], [1, GRID_W]])
                        pool.eng.dma_start(nb[half * GRID_W:(half + 1) * GRID_W, b, h, :, :], src).then_inc(on("nb_in"), pool.gives("nb_in", 16))
                pool.eng.wait_ge(on("nb_in"), pool.takes("nb_in", 128))
                for h in range(4):
                    ins = G.tensor_tensor(nb[:, b, h, :, :], nb[:, b, h, :, :],
                                          over_heads(cst[:, C_NAT:C_NAT + GRID_W], 6), ALU.add)
                ins.then_inc(on("n_bias"), pool.gives("n_bias"))
                if f == 0:
                    pool.eng.wait_ge(on("nv"), pool.takes("nv", 8))
                G.tensor_copy(nvf[:, f % NAT_TURN, :, :], nv[:, :, f * P:(f + 1) * P]).then_inc(on("n_v"), pool.gives("n_v"))

        def up_nat(pe):
            up_unit(pe, [ps[0][:, 0:SEQ], ps[1][:, :]], zt_hi, zt_lo, "nqk_ps", (slice(SEQ, 2 * SEQ), slice(None)))

        def pe_nat(pe):
            for c in range(2):
                for j in range(2):
                    rows_product(pe, [[ps[4 * c + t][:, :]] for t in ALL], zt_hi, zt_lo, range(4 * j, 4 * j + 4),
                                 j == 0, j == 1, "proj_ps" if j else None)
            pe.eng.wait_ge(on("nv"), pe.takes("nv", 8))
            pe.eng.wait_ge(on("nq_zero"), pe.takes("nq_zero"))
            with pe.turns("nat", NF // NAT_TURN):
                up_nat(pe)
                for g in range(NAT_STEPS + 2):
                    if g < NAT_STEPS:
                        j, h, t = g // 8, g % 8 // 2, g % 2
                        if g % 8 == 0:
                            pe.eng.wait_ge(on("n_q"), pe.takes("n_q", 4))
                            pe.eng.wait_ge(on("n_k"), pe.takes("n_k"))
                        if g % 8 == 4 and j + 1 < NAT_TURN:
                            up_nat(pe)
                        T.matmul(ps[S_BANK[g % 3]][:, :], nq[:, j % 2, h, t * P:(t + 1) * P], nk[:, j % 2, :],
                                 start=True, stop=True).then_inc(on("ns_ps"), pe.gives("ns_ps"))
                    if g < 2:
                        continue
                    j, h, t, b = (g - 2) // 8, (g - 2) % 8 // 2, g % 2, (g - 2) % 3
                    pe.eng.wait_ge(on("n_diag"), pe.takes("n_diag"))
                    for k in range(4):
                        ins = T.matmul(ps[4 + t][:, hs(k)], npr[:, b, hs(k)], nd[:, b, :], start=True, stop=True)
                    ins.then_inc(on("nt_ps"), pe.gives("nt_ps"))
                    if t == 1:
                        if h == 0:
                            pe.eng.wait_ge(on("nt"), pe.takes("nt"))
                            pe.eng.wait_ge(on("n_v"), pe.takes("n_v"))
                        pe.eng.wait_ge(on("n_pt"), pe.takes("n_pt", 2))
                        r = slice(ND * h, ND * h + ND)
                        for k in range(4):
                            ins = T.matmul(ps[7][r, 0:SEQ], nvf[:, j, k, r],
                                           npt[:, k, :, :].rearrange("p t q -> p (t q)"), start=k == 0, stop=k == 3)
                        if h == 3:
                            ins.then_inc(on("no_ps"), pe.gives("no_ps"))
            pe.eng.wait_ge(on("nt"), pe.takes("nt"))
            for c in range(2):
                for j in range(2):
                    rows_product(pe, [[ps[2 * c + t][:, :]] for t in range(NT)], nt_hi, nt_lo,
                                 range(4 * j, 4 * j + 4), j == 0, j == 1, "ny_ps" if j else None)
            release(pe)

        def act_q(act, j):
            act.eng.wait_ge(on("nqk_ps"), act.takes("nqk_ps"))
            for h in range(4):
                r = slice(ND * h, ND * h + ND)
                src = ps[0][r, 0:SEQ].rearrange("p (g c) -> p g c", c=GRID_W)[:, :, ::-1]
                A.activation(nq[r, j % 2, h, :].rearrange("p (g c) -> p g c", c=GRID_W), src, ACT.Copy,
                             scale=ND ** -0.5).then_inc(on("n_q"), act.gives("n_q"))

        def act_nat(act):
            act.eng.wait_ge(on("zs_new"), act.takes("zs_new", 2 * len(ALL)))
            for c in range(2):
                split_hi(act)
                if c == 0:
                    split_hi(act)
                act.eng.wait_ge(on("proj_ps"), act.takes("proj_ps"))
                for t in ALL:
                    act_copy(nv[:, t, 512 * c:512 * c + 512], ps[4 * c + t][:, :]).then_inc(on("nv"), act.gives("nv"))
            act.eng.wait_ge(on("nq_zero"), act.takes("nq_zero"))
            with act.turns("nat", NF // NAT_TURN) as i:
                split_hi(act)
                act_q(act, 0)
                for g in range(NAT_STEPS + 2):
                    if g >= 2:
                        t = g % 2
                        act.eng.wait_ge(on("nt_ps"), act.takes("nt_ps"))
                        act_copy(npt[:, :, t, :], heads(ps[4 + t][:, :], 4)).then_inc(on("n_pt"), act.gives("n_pt"))
                    if g < NAT_STEPS:
                        b = g % 3
                        act.eng.wait_ge(on("n_max"), act.takes("n_max"))
                        A.activation(npr[:, b, :], ps[S_BANK[b]][:, :], ACT.Exp, bias=nsm[:, 3 + b:4 + b],
                                     accum_out=nsm[:, 6 + b:7 + b]).then_inc(on("n_exp"), act.gives("n_exp"))
                        if g % 8 == 4 and g // 8 + 1 < NAT_TURN:
                            act_q(act, g // 8 + 1)
                            split_hi(act)
                    if g >= 9 and g % 8 == 1:
                        j = (g - 9) // 8
                        act.eng.wait_ge(on("no_ps"), act.takes("no_ps"))
                        act_copy(nt_hi[:, bass.ds(NAT_TURN * i + j, 1), :],
                                 ps[7][:, 0:SEQ].unsqueeze(1)).then_inc(on("nt_hi"), act.gives("nt_hi"))
            for _ in range(5):
                split_hi(act)

        def dve_k(dve, j):
            dve.eng.wait_ge(on("nqk_ps"), dve.takes("nqk_ps"))
            V.tensor_copy(nk[:, j % 2, :], ps[1][:, :]).then_inc(on("n_k"), dve.gives("n_k"))

        def dve_nat(dve):
            dve.eng.wait_ge(on("zs_new"), dve.takes("zs_new", len(ALL)))
            dve.eng.sem_inc(on("nt"), 1)
            dve.made["nt"] = 1
            split_lo(dve)
            split_lo(dve)
            split_lo(dve)
            with dve.turns("nat", NF // NAT_TURN) as i:
                split_lo(dve)
                dve_k(dve, 0)
                for g in range(NAT_STEPS + 2):
                    if g < NAT_STEPS:
                        j, h, t, b = g // 8, g % 8 // 2, g % 2, g % 3
                        if g % 8 == 0:
                            dve.eng.wait_ge(on("n_bias"), dve.takes("n_bias"))
                        dve.eng.wait_ge(on("ns_ps"), dve.takes("ns_ps"))
                        s_, slots = heads(ps[S_BANK[b]][:, SEQ:2 * SEQ], 4), slice(2 - 2 * t, 6 - 2 * t)
                        V.tensor_tensor(s_, s_, nb[:, j % 2, h, slots, :], ALU.add).then_inc(
                            on("n_biased"), dve.gives("n_biased"))
                        dve.eng.wait_ge(on("n_biased"), dve.given("n_biased"))
                        V.tensor_reduce(nsm[:, b:b + 1], ps[S_BANK[b]][:, :], AX_X, ALU.max).then_inc(
                            on("v_step"), dve.gives("v_step"))
                        dve.eng.wait_ge(on("v_step"), dve.given("v_step"))
                        V.tensor_scalar(nsm[:, 3 + b:4 + b], nsm[:, b:b + 1], -1.0, None, ALU.mult).then_inc(
                            on("n_max"), dve.gives("n_max"))
                    if 1 <= g <= NAT_STEPS:
                        b = (g - 1) % 3
                        dve.eng.wait_ge(on("n_exp"), dve.takes("n_exp"))
                        V.reciprocal(nsm[:, 9 + b:10 + b], nsm[:, 6 + b:7 + b]).then_inc(
                            on("v_step"), dve.gives("v_step"))
                        dve.eng.wait_ge(on("v_step"), dve.given("v_step"))
                        V.tensor_scalar(nd[:, b, :], cst[:, C_REV:C_REV + P], nsm[:, 9 + b:10 + b], None,
                                        ALU.mult).then_inc(on("n_diag"), dve.gives("n_diag"))
                    if g % 8 == 4 and g // 8 + 1 < NAT_TURN:
                        dve_k(dve, g // 8 + 1)
                        split_lo(dve)
                    if g >= 9 and g % 8 == 1:
                        j = (g - 9) // 8
                        dve.eng.wait_ge(on("nt_hi"), dve.takes("nt_hi"))
                        V.tensor_tensor(nt_lo[:, bass.ds(NAT_TURN * i + j, 1), :], ps[7][:, 0:SEQ].unsqueeze(1),
                                        nt_hi[:, bass.ds(NAT_TURN * i + j, 1), :].bitcast(F32),
                                        ALU.subtract).then_inc(on("nt"), dve.gives("nt"))
            for _ in range(5):
                split_lo(dve)

        block = ctx.enter_context(nc.Block())

        @block.sync
        def _(eng):
            sp = Lane("sync", eng)
            eng.dma_start(xs[:, :, :], a["x"].rearrange("b (t p) d -> p (b t) d", p=P)).then_inc(on("x_in"), sp.gives("x_in", 16))
            for l in range(DEPTH):
                w = a["ada_w_2"][l]
                with sp.turns("ada", 6) as i:
                    for b in range(2):
                        for j in range(2):
                            fetch(sp, rows_unit(w, 4 * j, i * 1024 + 512 * b))
            for l in range(DEPTH):
                sp_layer(sp, l)
            sp_ret(sp)
            sp_mlp(sp, 0)
            sp_nat(sp)
            sp_mlp(sp, 1)
            sp.eng.wait_ge(on("zs_new"), sp.takes("zs_new", 4 * len(ALL) - 4))
            eng.dma_start(out.rearrange("b (t p) d -> p (b t) d", p=P), xs[:, :, :]).then_inc(on("stored"), sp.gives("stored", 16))
            sp.eng.wait_ge(on("stored"), sp.given("stored"))

        @block.gpsimd
        def _(eng):
            pool = Lane("gpsimd", eng)
            pool_start(pool)
            pool_params(pool, 0)
            for l in range(DEPTH):
                pool_mixer(pool, l)
                pool_gains(pool, l)
                if l + 1 < DEPTH:
                    pool_params(pool, l + 1)
                pool_norm(pool, lambda t: xn1[:, t, :], 0)
                pool.eng.wait_ge(on("y_ps"), pool.takes("y_ps"))
                if l + 1 == DEPTH:
                    eng.dma_start(xc[:, :, :], a["ctx_2"].rearrange("b (t p) d -> p (b t) d", p=P)).then_inc(on("xc_in"), pool.gives("xc_in", 16))
                pool_norm(pool, lambda t: xn1[:, t, :], 1)
            pool.eng.wait_ge(on("xT"), pool.takes("xT", 3 * NT))
            pool.eng.wait_ge(on("xs_new"), pool.given("xs_new"))
            eng.dma_start(rope[:, :], a["table_2"]).then_inc(on("rdec_in"), pool.gives("rdec_in", 16))
            eng.dma_start(rsm[:, 72:80], a["ret_decay_2"].rearrange("a d h -> (a d h)").partition_broadcast(P)).then_inc(on("rdec_in"), pool.gives("rdec_in", 16))
            pool_ret(pool)
            pool_norm2(pool, 0, 0, ALL)
            pool_norm2(pool, 0, 1, ALL)
            pool_nat(pool)
            pool_norm2(pool, 1, 0, LAT)
            pool_norm2(pool, 1, 1, LAT)

        @block.scalar
        def _(eng):
            act = Lane("scalar", eng)
            act_start(act)
            for l in range(DEPTH):
                act_ada(act)
            for l in range(DEPTH):
                act_mixer(act, l)
                act_norm(act, par[:, 0, 88:96], par[:, 0, 96:104], xf1, xt_hi)
                act_ffn(act)
                if l + 1 < DEPTH:
                    act_norm(act, par[:, 0, 104:112], par[:, 0, 112:120], xf1, xt_hi)
            act.eng.wait_ge(on("coef"), act.takes("coef", 2))
            act_norm(act, coef[:, 1, 0, :], coef[:, 1, 1, :], xf1, zt_hi[:, :, SEQ:2 * SEQ])
            act.eng.wait_ge(on("xT"), act.takes("xT", 4 * DEPTH))
            for t in range(NT):
                act.eng.wait_ge(on("xnt_ps"), act.takes("xnt_ps"))
                for k in range(KT):
                    A.activation(xf1[:, t, k, :], ps[2 * t + k // 4][:, hs(k % 4)], ACT.Identity,
                                         scale=coef[:, 0, 0, k:k + 1], bias=coef[:, 0, 1, k:k + 1]).then_inc(on("a_step"), act.gives("a_step"))
                act.eng.wait_ge(on("a_step"), act.given("a_step"))
                act_copy(zt_hi[:, :, t * P:(t + 1) * P], xf1[:, t, :, :]).then_inc(on("x_hi"), act.gives("x_hi"))
            act_ret(act)
            act.turned = 0
            act_gates(act, ALL)
            act_norm2(act, ALL, (2, 3))
            act_mlp(act, ALL)
            act_norm2(act, ALL, (4, 5))
            act_nat(act)
            act_gates(act, LAT)
            act_norm2(act, LAT, (6,))
            act_mlp(act, LAT, final=True)

        @block.vector
        def _(eng):
            dve = Lane("vector", eng)
            dve_start(dve)
            for l in range(DEPTH):
                dve_ada(dve, l)
            dve_mods(dve)
            dve.eng.wait_ge(on("x_in"), dve.takes("x_in", 16))
            for l in range(DEPTH):
                if l:
                    dve.eng.wait_ge(on("xs_new"), dve.takes("xs_new", NT))
                dve_mixer(dve, l)
                dve_norm(dve, 2, xf1, xt_hi, xt_lo)
                dve_ffn(dve)
                dve.eng.wait_ge(on("xs_new"), dve.takes("xs_new", NT))
                if l + 1 < DEPTH:
                    dve_norm(dve, 1, xf1, xt_hi, xt_lo)
            dve_coef(dve, 1, par[:, 0, 104:112], par[:, 0, 112:120], 0, 0, 0, "coef")
            dve_norm(dve, 1, xf1, zt_hi[:, :, SEQ:2 * SEQ], zt_lo[:, :, SEQ:2 * SEQ])
            for t in range(NT):
                dve.eng.wait_ge(on("x_hi"), dve.takes("x_hi"))
                x = (slice(None), slice(None), slice(t * P, (t + 1) * P))
                V.tensor_tensor(zt_lo[x], xf1[:, t, :, :], zt_hi[x].bitcast(F32), ALU.subtract).then_inc(on("xT"), dve.gives("xT"))
            dve.eng.sem_inc(on("y_add"), 4)
            dve.made["y_add"] = 4
            dve_ret(dve)
            dve_gates(dve, 0, 2, ALL)
            dve_norm2(dve, ALL, False)
            dve_gates(dve, 0, 5, ALL)
            dve_mlp(dve, ALL)
            dve_norm2(dve, ALL, False)
            dve_nat(dve)
            dve_gates(dve, 1, 2, LAT)
            for c in range(2):
                dve.eng.wait_ge(on("ny_ps"), dve.takes("ny_ps"))
            dve_norm2(dve, LAT, False, ps)
            dve_gates(dve, 1, 5, LAT)
            dve_mlp(dve, LAT, final=True)
            dve_norm2(dve, LAT, True)

        @block.tensor
        def _(eng):
            pe = Lane("tensor", eng)
            pe.used["w_split"] = RAW_SLOTS
            pe.released = True
            pe_start(pe)
            pe.eng.wait_ge(on("c_lo"), pe.takes("c_lo", 2))
            for l in range(DEPTH):
                pe_ada(pe, l)
            pe.released = False
            for l in range(DEPTH):
                pe_mixer(pe, l)
                pe_norm(pe, lambda t: xn1[:, t, :])
                pe_ffn(pe)
                pe_norm(pe, lambda t: xn1[:, t, :])
            pe.eng.wait_ge(on("xc_in"), pe.takes("xc_in", 16))
            for t in range(NT):
                pe_turned(pe, xc[:, t, :], 2 * t)
            pe.eng.wait_ge(on("xT"), pe.takes("xT", NT))
            pe_ret(pe)
            pe_gates(pe, ALL)
            pe_gates_end(pe, ALL)
            pe_norm2(pe, ALL)
            pe_mlp(pe, ALL)
            pe_norm2(pe, ALL)
            pe_nat(pe)
            pe_gates(pe, LAT)
            pe_gates_end(pe, LAT)
            pe_norm2(pe, LAT)
            pe_mlp(pe, LAT)


_INS = ["x", "w_in", "gdn_conv_w", "gdn_a_log", "gdn_dt_bias", "gdn_norm_g", "w_out", "ln1_g", "ln1_b", "w_up",
        "ffn_conv_w", "ffn_conv_b", "w_down", "ln2_g", "ln2_b", "c_2", "ctx_2", "c_ctx_2", "ada_w_2", "ada_b_2",
        "ret_w_in_2", "ret_w_o_2", "ret_decay_2", "nat_w_in_2", "nat_w_o_2", "nat_rpb_2", "mlp_w1_2", "mlp_w2_2",
        "ln_g_2", "ln_b_2"]


def make(arrays, bacc):
    nc = bacc.Bacc("TRN2", target_bir_lowering=False, num_devices=1)
    aps = {n: nc.dram_tensor(f"in_{n}", v.shape, mybir.dt.from_np(v.dtype), kind="ExternalInput").ap()
           for n, v in arrays.items()}
    out = nc.dram_tensor("out", (1, SEQ, D), F32, kind="ExternalOutput").ap()
    build(nc, aps, out)
    return nc


def kernel(**inputs):
    import numpy as np
    import concourse.bacc as bacc
    from concourse.bass_utils import run_bass_kernel_spmd

    arrays = {n: np.ascontiguousarray(inputs[n]) for n in _INS}
    arrays["table_1"], arrays["table_2"] = constants()
    nc = make(arrays, bacc)
    r = run_bass_kernel_spmd(nc, [{f"in_{n}": v for n, v in arrays.items()}], core_ids=[0])
    return r.results[0]["out"]
```

```python
from contextlib import ExitStack, contextmanager

import concourse.bass as bass
from concourse import mybir

F32 = mybir.dt.float32
F32R = mybir.dt.float32r
ALU = mybir.AluOpType
ACT = mybir.ActivationFunctionType
AX_X = mybir.AxisListType.X

P = 128
D = 1024
KT = D // P
SEQ = 256
NT = SEQ // P
DEPTH = 2
ALPHA = (2 * DEPTH) ** 0.25
LN_EPS, NORM_EPS = 1e-5, 1e-6
HG, CHUNK = 4, 64
N_CHUNKS = SEQ // CHUNK
HM, DH = 8, 64
D_FF = 2816
FT = D_FF // P
COL_A, COL_Z, COL_QB = 1536, 1544, 2056
RH, RDK, RDV = 4, 256, 512
MLP = 4096
NH, ND = 32, 32
GRID_W = 64
RAW_SLOTS, SPLIT_SLOTS, UNIT = 4, 2, 2048
NEG = -1e30

C_ID, C_TRI, C_BD, C_ONE, C_INC, C_STR, C_M1, C_LEV = (P * i for i in range(8))
C_CAUSAL = C_LEV + 6 * P
C_COS = C_CAUSAL + 3 * P
C_SIN = C_COS + NT * 8
C_HALF = C_SIN + NT * 8
C_NAT = C_HALF + 2
C_MISC = C_NAT + GRID_W
C_FOLD = C_MISC + 2
C_REV = C_FOLD + 2
C_END = C_REV + P
R_DEL, R_COS, R_SIN, R_END = 0, 256, 768, 1280


def constants():
    import numpy as np
    p = np.arange(P)
    c, m = p[:, None], p[None, :]
    same = c // CHUNK == m // CHUNK
    t = np.zeros((P, C_END), np.float32)
    t[:, C_ID:C_ID + P] = c == m
    t[:, C_TRI:C_TRI + P] = same & (c <= m)
    t[:, C_BD:C_BD + P] = same
    t[:, C_ONE:C_ONE + P] = 1
    t[:, C_INC:C_INC + P] = same & (c >= m)
    t[:, C_STR:C_STR + P] = same & (c > m)
    for n in range(6):
        s = 2 ** n
        lev = (c // (2 * s) == m // (2 * s)) & ((c // s) % 2 == 1) & ((m // s) % 2 == 0)
        if n == 0:
            t[:, C_M1:C_M1 + P] = lev
        t[:, C_LEV + n * P:C_LEV + (n + 1) * P] = lev.T
    tri = np.where(c >= m, 0.0, NEG)
    t[:, C_CAUSAL:C_CAUSAL + P] = tri
    t[:, C_CAUSAL + 2 * P:C_CAUSAL + 3 * P] = tri
    inv = np.float32(500000.0) ** (-np.arange(8, dtype=np.float32) / np.float32(8))
    ang = (np.arange(SEQ, dtype=np.float32)[:, None] * inv).reshape(NT, P, 8).transpose(1, 0, 2)
    t[:, C_COS:C_COS + 16] = np.cos(ang).reshape(P, 16)
    t[:, C_SIN:C_SIN + 16] = np.sin(ang).reshape(P, 16)
    t[:, C_HALF] = p < CHUNK
    t[:, C_HALF + 1] = p >= CHUNK
    cq = (GRID_W - 1 - p % GRID_W)[:, None]
    t[:, C_REV:C_REV + P] = (c // GRID_W == m // GRID_W) & (m % GRID_W == cq)
    ck = np.arange(GRID_W)[None, :]
    start = np.clip(cq - 8, 0, GRID_W - 16)
    t[:, C_NAT:C_NAT + GRID_W] = np.where((ck >= start) & (ck < start + 16), 0.0, NEG)
    t[:, C_MISC] = -0.5
    t[:, C_MISC + 1] = 0.0

    t[0:4, C_FOLD:C_FOLD + 2] = np.arange(4)[:, None] % 2 == np.arange(2)[None, :]

    r = np.zeros((P, R_END), np.float32)
    r[:, R_DEL:R_DEL + SEQ] = np.arange(SEQ)[None, :] - p[:, None]
    inv = (1.0 / (np.float32(10000.0) ** (np.arange(0, P, 2, dtype=np.float32) / np.float32(P)))).astype(np.float32)
    tok = np.arange(SEQ)
    for n, pos in enumerate((tok // GRID_W, tok % GRID_W)):
        ang = (pos.astype(np.float32)[:, None] * inv).T
        r[:, R_COS + SEQ * n:R_COS + SEQ * (n + 1)] = np.tile(np.cos(ang), (2, 1))
        r[:, R_SIN + SEQ * n:R_SIN + SEQ * (n + 1)] = np.concatenate([np.sin(ang), -np.sin(ang)], 0)
    return t, r


TURNS = {
    "sync.ada": {"made raw_full0": 32, "made raw_full1": 32, "made raw_full2": 32, "made raw_full3": 32,
        "used w_split": 4},
    "sync.up": {"made raw_full0": 32, "made raw_full1": 32, "made raw_full2": 32, "made raw_full3": 32,
        "used w_split": 4},
    "sync.ret": {"made raw_full0": 64, "made raw_full1": 64, "made raw_full2": 64, "made raw_full3": 64,
        "used w_split": 8},
    "sync.mlp": {"made raw_full0": 64, "made raw_full1": 64, "made raw_full2": 64, "made raw_full3": 64,
        "used w_split": 8},
    "sync.nat": {"made raw_full0": 32, "made raw_full1": 32, "made raw_full2": 32, "made raw_full3": 32,
        "used w_split": 4},
    "gpsimd.ret": {"made pow_out": 1, "used pow_in": 1},
    "scalar.ada": {"made w_hi": 8, "made ada_row": 2, "used w_used": 4, "used raw_full0": 32, "used raw_full1": 32,
        "used raw_full2": 32, "used ada_ps": 2, "used raw_full3": 32},
    "scalar.up": {"made w_hi": 8, "made tap_f": 8, "made silu_f": 4, "made h_hi": 4, "used w_used": 4,
        "used raw_full0": 32, "used raw_full1": 32, "used raw_full2": 32, "used raw_full3": 32, "used up_ps": 4,
        "used conv_f": 4, "used gated": 4},
    "scalar.ret": {"made w_hi": 16, "made a_step": 6, "made r_exp": 2, "made rqk_c": 4, "made rv": 4, "made rg": 4,
        "made rt_hi": 4, "used w_used": 8, "used raw_full0": 64, "used raw_full1": 64, "used raw_full2": 64,
        "used raw_full3": 64, "used proj_ps": 4, "used r_arg": 2, "used rt_ps": 4},
    "scalar.mlp4": {"made w_hi": 16, "made relu": 8, "made hh_hi": 8, "used w_used": 8, "used raw_full0": 64,
        "used raw_full1": 64, "used raw_full2": 64, "used raw_full3": 64, "used up_ps": 4, "used hh": 8,
        "used hm": 8},
    "scalar.nat": {"made w_hi": 8, "made n_q": 16, "made n_exp": 32, "made n_pt": 32, "made nt_hi": 4,
        "used w_used": 4, "used raw_full0": 32, "used raw_full1": 32, "used raw_full2": 32, "used raw_full3": 32,
        "used nqk_ps": 4, "used n_max": 32, "used nt_ps": 32, "used no_ps": 4},
    "scalar.mlp2": {"made w_hi": 16, "made relu": 8, "made hh_hi": 8, "used w_used": 8, "used raw_full0": 64,
        "used raw_full1": 64, "used raw_full2": 64, "used raw_full3": 64, "used up_ps": 4, "used hh": 8,
        "used hm": 8},
    "vector.ada": {"made w_split": 4, "made mod_raw": 2, "used w_hi": 8, "used fold_ps": 2},
    "vector.up": {"made w_split": 4, "made v_step": 12, "made conv_f": 4, "made gated": 4, "made h": 4,
        "used w_hi": 8, "used tap_f": 8, "used silu_f": 4, "used h_hi": 4},
    "vector.ret": {"made w_split": 8, "made v_step": 43, "made pow_in": 1, "made y_add": 8, "made r_arg": 2,
        "made rqk": 2, "made rs": 3, "made ro": 4, "made rt": 4, "used w_hi": 16, "used pow_out": 1,
        "used r_exp": 2, "used rqk_c": 4, "used rs_ps": 3, "used pv_ps": 4, "used rg": 4, "used rt_hi": 4,
        "used dn_ps": 8},
    "vector.mlp4": {"made w_split": 8, "made y_add": 16, "made hh": 8, "made hm": 8, "used w_hi": 16,
        "used dn_ps": 16, "used relu": 8, "used hh_hi": 8},
    "vector.nat": {"made w_split": 4, "made v_step": 64, "made nt": 4, "made n_k": 4, "made n_biased": 32,
        "made n_max": 32, "made n_diag": 32, "used w_hi": 8, "used nqk_ps": 4, "used n_bias": 4, "used ns_ps": 32,
        "used n_exp": 32, "used nt_hi": 4},
    "vector.mlp2": {"made w_split": 8, "made y_add": 8, "made hh": 8, "made hm": 8, "used w_hi": 16,
        "used dn_ps": 8, "used relu": 8, "used hh_hi": 8},
    "tensor.ada": {"made w_used": 4, "made ada_ps": 2, "made fold_ps": 2, "used w_split": 4, "used ada_row": 2},
    "tensor.up": {"made w_used": 4, "made up_ps": 4, "used w_split": 4, "used conv_f": 4},
    "tensor.ret": {"made w_used": 8, "made proj_ps": 4, "made rs_ps": 3, "made pv_ps": 4, "made rt_ps": 4,
        "made dn_ps": 8, "used w_split": 8, "used rqk": 2, "used rv": 4, "used rs": 3, "used ro": 4, "used rg": 4,
        "used rt": 4, "used y_add": 8},
    "tensor.mlp4": {"made w_used": 8, "made up_ps": 4, "made dn_ps": 16, "used w_split": 8, "used y_add": 16,
        "used hh": 8},
    "tensor.nat": {"made w_used": 4, "made nqk_ps": 4, "made ns_ps": 32, "made nt_ps": 32, "made no_ps": 4,
        "used w_split": 4, "used n_q": 16, "used n_k": 4, "used n_diag": 32, "used nt": 4, "used n_v": 4,
        "used n_pt": 32},
    "tensor.mlp2": {"made w_used": 8, "made up_ps": 4, "made dn_ps": 8, "used w_split": 8, "used y_add": 8,
        "used hh": 8},
}


class Lane:

    def __init__(self, name, eng):
        self.name, self.eng = name, eng
        self.made, self.used, self.loop, self.unit = {}, {}, None, 0

    def _value(self, kind, counts, sem):
        counts.setdefault(sem, 0)
        if self.loop is None:
            return counts[sem]
        i, per = self.loop
        step = per.get(f"{kind} {sem}", 0)
        return counts[sem] + i * step if step else counts[sem]

    def gives(self, sem, by=1):
        self.made[sem] = self.made.get(sem, 0) + by
        return by

    def takes(self, sem, by=1):
        self.used[sem] = self.used.get(sem, 0) + by
        return self._value("used", self.used, sem)

    def beyond(self, sem, ahead):
        return self._value("used", self.used, sem) + ahead

    def given(self, sem):
        return self._value("made", self.made, sem)

    @contextmanager
    def turns(self, key, n):
        key = f"{self.name}.{key}"
        per = TURNS.get(key, {})
        kinds = (("made", self.made), ("used", self.used))
        before = {f"{kind} {sem}": v for kind, counts in kinds for sem, v in counts.items()}
        with self.eng.Fori(0, n) as i:
            self.loop = (i, per)
            yield i
            self.loop = None
        found = {}
        for kind, counts in kinds:
            for sem, v in counts.items():
                if v != before.get(f"{kind} {sem}", 0):
                    found[f"{kind} {sem}"] = v - before.get(f"{kind} {sem}", 0)
                    counts[sem] += (n - 1) * found[f"{kind} {sem}"]
        assert found == per, (key, found)


def build(nc, a, out):
    with ExitStack() as ctx:
        held = {}

        def on(name):
            if name not in held:
                held[name] = ctx.enter_context(nc.semaphore(name))
            return held[name]

        def tensors(scope):
            return lambda name, shape, dt=F32: scope.enter_context(nc.sbuf_tensor(name, [P] + shape, dt))

        sb = tensors(ctx)
        cst = sb("cst", [C_END])
        raw = sb("raw", [RAW_SLOTS, UNIT])
        w_hi = sb("w_hi", [SPLIT_SLOTS, UNIT], F32R)
        w_lo = sb("w_lo", [SPLIT_SLOTS, UNIT], F32R)
        xs = sb("xs", [NT, D])
        rows = sb("rows", [3, P])
        par = sb("par", [3, P])
        rows2 = sb("rows2", [2, P])
        par2 = sb("par2", [2, P])
        mod = sb("mod", [DEPTH, 48, 2])
        coef = sb("coef", [7, 2, KT])
        small = sb("small", [64])
        one = ExitStack()
        sb1 = tensors(one)
        lay = sb1("lay", [200])
        xt_hi = sb1("xt_hi", [KT, SEQ], F32R)
        xt_lo = sb1("xt_lo", [KT, SEQ], F32R)
        pa = ExitStack()
        sa = tensors(pa)
        qkv = sa("qkv", [12, SEQ])
        ab_hi = sa("ab_hi", [KT, 8], F32R)
        ab_lo = sa("ab_lo", [KT, 8], F32R)
        k_tok = sa("k_tok", [NT, 512])
        v_beta = sa("v_beta", [NT, 512])
        k_bg = sa("k_bg", [NT, 512])
        k_dec = sa("k_dec", [NT, 512])
        kn = sa("kn", [HG, SEQ])
        dec_y = sa("dec_y", [NT, 512])
        d_inc = sa("d_inc", [NT, 512])
        d_beta = sa("d_beta", [NT, 512])
        a_mat = sa("a_mat", [NT, 512])
        attn = sa("attn", [NT, 512])
        att2 = sa("att2", [2, NT, 512])
        x_inv = sa("x_inv", [NT, 512])
        xt_inv = sa("xt_inv", [NT, 512])
        state = sa("state", [512])
        silu_z = sa("silu_z", [NT, 512])
        gp = sa("gp", [320])
        qk_tok = sa("qk_tok", [NT, 2 * HM, DH])
        v_tok = sa("v_tok", [NT, 512])
        qk_t = sa("qk_t", [2 * HM // 2, SEQ])
        pm = sa("pm", [2, 384])
        pm_t = sa("pm_t", [2, 384])
        rot = pm_t[:, :, :].rearrange("p b c -> p (b c)")[:, 0:512].rearrange("p (i h c) -> p i h c", i=4, h=2 * HM)
        ms = sa("ms", [16])
        w_t = d_beta[:, :, :].rearrange("p t (h c) -> p (t h c)", h=4).rearrange("p (h c) -> p h c", h=HG)
        squares = att2[:, :, :, :].rearrange("p a t n -> p (a t n)").rearrange("p (f c) -> p f c", f=8)
        m_lev = [qkv[:, 4:8, :].rearrange("p f c -> p (f c)").rearrange("p (t n) -> p t n", t=NT),
                 qkv[:, 8:12, :].rearrange("p f c -> p (f c)").rearrange("p (t n) -> p t n", t=NT)]
        pa.close()
        pb = ExitStack()
        sbb = tensors(pb)
        pz = ExitStack()
        sz = tensors(pz)
        cs_hl = sz("cs_hl", [KT, P], F32R)
        ada_row = sz("ada_row", [2, 512])
        pz.close()
        h_hi = sbb("h_hi", [FT, SEQ], F32R)
        h_lo = sbb("h_lo", [FT, SEQ], F32R)
        ln_gb = sbb("ln_gb", [2, 2, D])
        xn1 = sbb("xn1", [NT, D])
        xf1 = sbb("xf1", [NT, KT, P])
        hid = sbb("hid", [4, 2, SEQ])
        pb.close()
        one.close()
        two = ExitStack()
        s2 = tensors(two)
        zt_hi = s2("zt_hi", [KT, 2 * SEQ], F32R)
        zt_lo = s2("zt_lo", [KT, 2 * SEQ], F32R)
        xc = s2("xc", [NT, D])
        pc = ExitStack()
        sc = tensors(pc)
        y = sc("y", [2 * NT, D])
        pr = ExitStack()
        sr = tensors(pr)
        rqk = sr("rqk", [2, 2, 2 * SEQ])
        rv = sr("rv", [2 * NT, RDV])
        rg = sr("rg", [2 * NT, RDV])
        rs = sr("rs", [3, 2 * SEQ])
        rt_hi = sr("rt_hi", [4, 2 * SEQ], F32R)
        rt_lo = sr("rt_lo", [4, 2 * SEQ], F32R)
        wd = sr("wd", [2, 2 * SEQ])
        rope = sr("rope", [R_END])
        rtmp = sr("rtmp", [4, SEQ])
        rsm = sr("rsm", [96])
        r_stat = rsm[:, 0:48].rearrange("p (t c) -> p t c", t=4)
        pr.close()
        pm2 = ExitStack()
        sm = tensors(pm2)
        gate_b = sm("gate_b", [2, D])
        gn2 = sm("gn2", [2, D])
        xf2 = sm("xf2", [2, KT, P])
        hm = sm("hm", [4, 2 * SEQ])
        hh_hi = sm("hh_hi", [2, 4, 2 * SEQ], F32R)
        hh_lo = sm("hh_lo", [2, 4, 2 * SEQ], F32R)
        pm2.close()
        pc.close()
        pn = ExitStack()
        sn = tensors(pn)
        nv = sn("nv", [2 * NT, D])
        nq = sn("nq", [2, 4, SEQ])
        nk = xc[:, 0, :].rearrange("p (b c) -> p b c", b=2)
        nb = sn("nb", [2, 4, 6, GRID_W])
        npr = sn("npr", [3, 2 * SEQ])
        npt = xc[:, 1, :].rearrange("p (k t q) -> p k t q", k=4, t=NT)
        nvf = sn("nvf", [2, 4, 4, P])
        nd = sn("nd", [3, P])
        nt_hi = sn("nt_hi", [KT, SEQ], F32R)
        nt_lo = sn("nt_lo", [KT, SEQ], F32R)
        nsm = sn("nsm", [64])
        pn.close()
        two.close()

        ps = [ctx.enter_context(nc.psum_tensor(f"ps{i}", [P, 512], F32)) for i in range(8)]

        V, A, G, T = nc.vector, nc.scalar, nc.gpsimd, nc.tensor
        ident = cst[:, C_ID:C_ID + P]
        ones = cst[:, C_ONE:C_ONE + P]

        def heads(ap, n):
            return ap.rearrange("p (h c) -> p h c", h=n)

        def per_head(ap, width):
            return ap.unsqueeze(2).to_broadcast([P, ap.shape[1], width])

        def over_heads(ap, n):
            return ap.unsqueeze(1).to_broadcast([P, n, ap.shape[1]])

        def fetch(sp, halves):
            s = sp.unit % RAW_SLOTS
            sp.unit += 1
            sp.eng.wait_ge(on("w_split"), sp.takes("w_split"))
            for n, src in enumerate(halves):
                dst = raw[:, s, n * 1024:(n + 1) * 1024].rearrange("p (k c) -> p k c", k=src.shape[1])
                sp.eng.dma_start(dst, src).then_inc(on(f"raw_full{s}"), sp.gives(f"raw_full{s}", 16))

        def cols_unit(w, c0, c1):
            v = w.rearrange("(k p) n -> p k n", p=P)
            return [v[:, :, bass.ds(c, P)] for c in (c0, c1)]

        def rows_unit(w, k0, c0, n_k=4, width=512):
            v = w.rearrange("(k p) n -> p k n", p=P)
            h = n_k // 2
            return [v[:, bass.ds(k0 + h * j, h), bass.ds(c0, width)] for j in range(2)]

        def split_hi(act):
            s, t = act.unit % RAW_SLOTS, act.unit % SPLIT_SLOTS
            act.unit += 1
            act.eng.wait_ge(on(f"raw_full{s}"), act.takes(f"raw_full{s}", 32))
            if act.started >= SPLIT_SLOTS:
                act.eng.wait_ge(on("w_used"), act.takes("w_used"))
            act.started += 1
            for h in range(2):
                w = slice(h * UNIT // 2, (h + 1) * UNIT // 2)
                nc.scalar.activation(w_hi[:, t, w], raw[:, s, w], ACT.Copy).then_inc(on("w_hi"), act.gives("w_hi"))

        def split_lo(dve):
            s, t = dve.unit % RAW_SLOTS, dve.unit % SPLIT_SLOTS
            dve.unit += 1
            for h in range(2):
                w = slice(h * UNIT // 2, (h + 1) * UNIT // 2)
                dve.eng.wait_ge(on("w_hi"), dve.takes("w_hi"))
                ins = nc.vector.tensor_tensor(w_lo[:, t, w], raw[:, s, w], w_hi[:, t, w].bitcast(F32), ALU.subtract)
            ins.then_inc(on("w_split"), dve.gives("w_split"))

        def unit_slot(pe):
            t = pe.unit % SPLIT_SLOTS
            pe.unit += 1
            pe.eng.wait_ge(on("w_split"), pe.takes("w_split"))
            return w_hi[:, t, :], w_lo[:, t, :]

        def three(out_ap, l_hi, l_lo, r_hi, r_lo, start, stop):
            first = nc.tensor.matmul(out_ap, l_hi, r_hi, start=start, stop=False)
            nc.tensor.matmul(out_ap, l_hi, r_lo, start=False, stop=False)
            return first, nc.tensor.matmul(out_ap, l_lo, r_hi, start=False, stop=stop)

        def begun(pe, first):
            if not pe.released:
                first.then_inc(on("w_used"), pe.gives("w_used"))
            pe.released = False

        def release(pe, bank=7):
            t = (pe.unit - 1) % SPLIT_SLOTS
            T.matmul(ps[bank][:, 508:510], w_hi[:, t, 0:P], w_hi[:, t, 0:2], start=True, stop=True).then_inc(
                on("w_used"), pe.gives("w_used"))
            pe.released = True

        def up_unit(pe, outs, x_hi, x_lo, sem, toks=(slice(None), slice(None))):
            hi, lo = unit_slot(pe)
            for f in range(2):
                for k in range(KT):
                    c = f * 1024 + k * P
                    first, last = three(outs[f], hi[:, c:c + P], lo[:, c:c + P], x_hi[:, k, toks[f]],
                                        x_lo[:, k, toks[f]], k == 0, k == KT - 1)
                    if f == k == 0:
                        begun(pe, first)
            last.then_inc(on(sem), pe.gives(sem))

        def rows_product(pe, outs, x_hi, x_lo, ks, first_k, last_k, sem, n_k=4, width=512):
            hi, lo = unit_slot(pe)
            for j in range(n_k):
                for t in range(len(outs)):
                    for c in range(len(outs[t])):
                        w = slice(j * width + c * 512, j * width + (c + 1) * 512)
                        x = slice(t * P, (t + 1) * P)
                        first, last = three(outs[t][c], x_hi[:, ks[j], x], x_lo[:, ks[j], x], hi[:, w], lo[:, w],
                                            first_k and j == 0, last_k and j == n_k - 1)
                        if j == t == c == 0:
                            begun(pe, first)
            if sem:
                last.then_inc(on(sem), pe.gives(sem))

        EARLY = ("ss", "gate", "gsum")
        PROJ_BANK = (0, 2, 4, 2)

        def mixer_steps():
            rule = ["kv", "kn", "gram", "turn"]
            for n in range(1, 6):
                rule += [("y", n), ("x", n)]
            rule += ["uw"]
            for n in range(N_CHUNKS):
                rule += [("ws", n), ("ov", n)]
                if n % 2:
                    rule += [("out", n // 2)]
            att = [("mt", n) for n in range(4)]
            for g in range(HM // 2):
                att += [("ma", g), ("mb", g), ("mc", g)]
            order = []
            while rule or att:
                order += rule[:1] + att[:1]
                rule, att = rule[1:], att[1:]
            return order

        def hs(h):
            return slice(h * P, (h + 1) * P)

        def pe_start(pe):
            pe.eng.wait_ge(on("cst_in"), pe.takes("cst_in", 16))
            pe.eng.wait_ge(on("rows2_in"), pe.takes("rows2_in", 80))
            for n in range(2):
                ins = T.transpose(ps[6][:, hs(n)], rows2[:, n, :], ident)
            ins.then_inc(on("par2_ps"), pe.gives("par2_ps"))
            pe.eng.wait_ge(on("x_in"), pe.takes("x_in", 16))
            for t in range(NT):
                for k in range(KT):
                    ins = T.transpose(ps[2 * t + k // 4][:, hs(k % 4)], xs[:, t, k * P:(k + 1) * P], ident)
            ins.then_inc(on("x0_ps"), pe.gives("x0_ps"))

        def pe_params(pe):
            pe.eng.wait_ge(on("rows_in"), pe.takes("rows_in", 16 * 8))
            for n in range(3):
                ins = T.transpose(ps[6][:, hs(n)], rows[:, n, :], ident)
            ins.then_inc(on("par_ps"), pe.gives("par_ps"))

        def pe_mixer(pe, l):
            for u in range(6):
                if u >= 3:
                    pe.eng.wait_ge(on("conv"), pe.takes("conv"))
                b = ps[4 + u % 3] if u % 3 < 2 else ps[0]
                if u == 0 and l == 0:
                    pe.eng.wait_ge(on("x0"), pe.takes("x0", 4))
                up_unit(pe, [b[:, 0:SEQ], b[:, SEQ:2 * SEQ]], xt_hi, xt_lo, "qkv_ps")
                if u == 0:
                    if l == 0:
                        pe.eng.wait_ge(on("mod_raw"), pe.takes("mod_raw", 12 * DEPTH))
                    pe_params(pe)
            pe.eng.wait_ge(on("ab_split"), pe.takes("ab_split"))
            for t in range(NT):
                for k in range(KT):
                    _, ins = three(ps[7][:, 8 * t:8 * t + 8], xt_hi[:, k, t * P:(t + 1) * P],
                                   xt_lo[:, k, t * P:(t + 1) * P], ab_hi[:, k, :], ab_lo[:, k, :],
                                   k == 0, k == KT - 1)
            ins.then_inc(on("ab_ps"), pe.gives("ab_ps"))
            pe.eng.wait_ge(on("conv"), pe.takes("conv", 3))
            for n in range(4):
                if n == 3:
                    pe.eng.wait_ge(on("tok_out"), pe.takes("tok_out", 2))
                for j in range(2):
                    rows_product(pe, [[ps[PROJ_BANK[n] + t][:, :]] for t in range(NT)], xt_hi, xt_lo,
                                 range(4 * j, 4 * j + 4), j == 0, j == 1, "proj_ps" if j else None)
                if n == 2:
                    pe.eng.wait_ge(on("tok_out"), pe.takes("tok_out", 2))
                if n < 3:
                    pe_step(pe, EARLY[n])
            release(pe, 6)
            pe.eng.wait_ge(on("tok_out"), pe.takes("tok_out", 4))
            for step in mixer_steps():
                pe_step(pe, step)
            pe.eng.wait_ge(on("mix_rule"), pe.takes("mix_rule", 2))
            pe.eng.wait_ge(on("mix_att"), pe.takes("mix_att"))
            for c in range(2):
                for j in range(2):
                    rows_product(pe, [[ps[2 * c + t][:, :]] for t in range(NT)], xt_hi, xt_lo,
                                 range(4 * j, 4 * j + 4), j == 0, j == 1, "y_ps" if j else None)
            release(pe)

        def pe_step(pe, step):
            name, n = step if isinstance(step, tuple) else (step, 0)
            if name == "ss":
                pe.eng.wait_ge(on("sq"), pe.takes("sq", 4))
                for t in range(NT):
                    for f in range(8):
                        c = 16 + 8 * t + f
                        ins = T.matmul(ps[7][:, c:c + 1], squares[:, f, t * P:(t + 1) * P], ones[:, 0:1],
                                       start=True, stop=True)
                ins.then_inc(on("ss_ps"), pe.gives("ss_ps"))
            elif name == "gsum":
                pe.eng.wait_ge(on("gates"), pe.takes("gates"))
                for t in range(NT):
                    raw_g = gp[:, 16 + 4 * t:20 + 4 * t]
                    T.matmul(ps[7][:, 32 + 4 * t:36 + 4 * t], cst[:, C_TRI:C_TRI + P], raw_g, start=True, stop=True)
                    T.matmul(ps[7][:, 40 + 4 * t:44 + 4 * t], cst[:, C_BD:C_BD + P], raw_g, start=True, stop=True)
                    ins = T.matmul(ps[7][:, 48 + 8 * t:56 + 8 * t], ones, gp[:, 128 + 8 * t:136 + 8 * t],
                                   start=True, stop=True)
                ins.then_inc(on("gs_ps"), pe.gives("gs_ps"))
                for t in range(NT):
                    for h in range(HG):
                        ins = T.matmul(ps[t][:, hs(h)], dec_y[:, t, hs(h)], cst[:, C_TRI:C_TRI + P],
                                       start=True, stop=True)
                    ins.then_inc(on("grow_ps"), pe.gives("grow_ps"))
            elif name == "kv":
                pe.eng.wait_ge(on("silu"), pe.takes("silu", 6))
                for t in range(NT):
                    for h in range(HG):
                        T.transpose(ps[2 + t][:, hs(h)], qkv[:, 4 + h, t * P:(t + 1) * P], ident)
                    for h in range(HG):
                        ins = T.transpose(ps[4 + t][:, hs(h)], qkv[:, 8 + h, t * P:(t + 1) * P], ident)
                    ins.then_inc(on("kv_ps"), pe.gives("kv_ps"))
            elif name == "kn":
                for t in range(NT):
                    pe.eng.wait_ge(on("kv_out"), pe.takes("kv_out"))
                    for h in range(HG):
                        ins = T.transpose(ps[2 + t][:, hs(h)], k_tok[:, t, hs(h)], ident)
                    ins.then_inc(on("rule_ps"), pe.gives("rule_ps"))
            elif name == "gram":
                for t in range(NT):
                    pe.eng.wait_ge(on("kn"), pe.takes("kn"))
                    tok = slice(t * P, (t + 1) * P)
                    for h in range(HG):
                        T.matmul(ps[4 + t][:, hs(h)], kn[:, h, tok], kn[:, h, tok], start=True, stop=True)
                    for h in range(HG):
                        ins = T.matmul(ps[2 + t][:, hs(h)], qkv[:, h, tok], kn[:, h, tok], start=True, stop=True)
                    ins.then_inc(on("gram_ps"), pe.gives("gram_ps"))
            elif name == "turn":
                for t in range(NT):
                    pe.eng.wait_ge(on("gram"), pe.takes("gram"))
                    for h in range(HG):
                        T.transpose(ps[t][:, hs(h)], a_mat[:, t, hs(h)], ident)
                    for h in range(HG):
                        ins = T.transpose(ps[4 + t][:, hs(h)], attn[:, t, hs(h)], ident)
                    ins.then_inc(on("rule_ps"), pe.gives("rule_ps"))
            elif name == "y":
                for t in range(NT):
                    pe.eng.wait_ge(on("x_inv"), pe.takes("x_inv"))
                    pe.eng.wait_ge(on("m_lev"), pe.takes("m_lev"))
                    for h in range(HG):
                        ins = T.matmul(ps[2 + t][:, hs(h)], m_lev[n % 2][:, t, hs(h)], x_inv[:, t, hs(h)],
                                       start=True, stop=True)
                    ins.then_inc(on("yy_ps"), pe.gives("yy_ps"))
            elif name == "x":
                for t in range(NT):
                    pe.eng.wait_ge(on("yy"), pe.takes("yy"))
                    if n < 5:
                        for h in range(HG):
                            T.matmul(ps[t][:, hs(h)], xt_inv[:, t, hs(h)], dec_y[:, t, hs(h)], start=True, stop=True)
                    for h in range(HG):
                        ins = T.matmul(ps[4 + t][:, hs(h)], dec_y[:, t, hs(h)], xt_inv[:, t, hs(h)],
                                       start=True, stop=True)
                    ins.then_inc(on("xx_ps"), pe.gives("xx_ps"))
            elif name == "uw":
                for t in range(NT):
                    pe.eng.wait_ge(on("x_inv"), pe.takes("x_inv"))
                    if t == 0:
                        pe.eng.wait_ge(on("k_bg"), pe.takes("k_bg", 2))
                    for h in range(HG):
                        T.matmul(ps[2 + t][:, hs(h)], xt_inv[:, t, hs(h)], v_beta[:, t, hs(h)], start=True, stop=True)
                    for h in range(HG):
                        ins = T.matmul(ps[t][:, hs(h)], k_bg[:, t, hs(h)], xt_inv[:, t, hs(h)], start=True, stop=True)
                    ins.then_inc(on("rule_ps"), pe.gives("rule_ps"))
                pe.eng.wait_ge(on("uw"), pe.takes("uw", 2))
            elif name == "ws":
                t, lo = n // 2, CHUNK * (n % 2)
                half, tok = slice(lo, lo + CHUNK), slice(n * CHUNK, (n + 1) * CHUNK)
                pe.eng.wait_ge(on("state" if n else "state0"), pe.takes("state" if n else "state0"))
                for h in range(HG):
                    ins = T.matmul(ps[4][half, hs(h)], w_t[:, h, tok], state[:, hs(h)], start=True, stop=True)
                ins.then_inc(on("ws_ps"), pe.gives("ws_ps"))
                for h in range(HG):
                    ins = T.matmul(ps[t][half, hs(h)], qkv[:, h, tok], state[:, hs(h)], start=True, stop=True)
                ins.then_inc(on("os_ps"), pe.gives("os_ps"))
            elif name == "ov":
                t, lo = n // 2, CHUNK * (n % 2)
                half = slice(lo, lo + CHUNK)
                pe.eng.wait_ge(on("v_new"), pe.takes("v_new"))
                if n < N_CHUNKS - 1:
                    for h in range(HG):
                        ins = T.matmul(ps[5][:, hs(h)], k_dec[half, t, hs(h)], a_mat[half, t, hs(h)],
                                       start=True, stop=True)
                    ins.then_inc(on("st_ps"), pe.gives("st_ps"))
                for h in range(HG):
                    ins = T.matmul(ps[2 + t][half, hs(h)], att2[half, 1, t, h * P + lo:h * P + lo + CHUNK],
                                   a_mat[half, t, hs(h)], start=True, stop=True)
                ins.then_inc(on("ov_ps"), pe.gives("ov_ps"))
            elif name == "out":
                pe.eng.wait_ge(on("o_rule"), pe.takes("o_rule"))
                for h in range(HG):
                    ins = T.transpose(ps[n][:, hs(h)], attn[:, n, hs(h)], ident)
                ins.then_inc(on("rule_ps"), pe.gives("rule_ps"))
            elif name == "mt":
                t, g = n // 2, n % 2
                if g == 0:
                    pe.eng.wait_ge(on("rot"), pe.takes("rot"))
                if n:
                    pe.eng.wait_ge(on("qk_t"), pe.takes("qk_t"))
                for j in range(4):
                    f = 4 * g + j
                    ins = T.transpose(ps[6][:, hs(j)], qk_tok[:, t, 2 * f:2 * f + 2, :].rearrange("p h d -> p (h d)"),
                                      ident)
                ins.then_inc(on("att_ps"), pe.gives("att_ps"))
            elif name == "ma":
                if n == 0:
                    pe.eng.wait_ge(on("qk_t"), pe.takes("qk_t"))
                else:
                    pe.eng.wait_ge(on("mix_att"), pe.takes("mix_att"))
                for b in range(2):
                    r, s_ = slice(DH * b, DH * b + DH), ps[6 + b]
                    T.matmul(s_[:, 0:P], qk_t[r, n, 0:P], qk_t[r, 4 + n, 0:P], start=True, stop=True)
                    T.matmul(s_[:, P:3 * P], qk_t[r, n, P:2 * P], qk_t[r, 4 + n, 0:2 * P],
                             start=True, stop=True).then_inc(on("ma_ps"), pe.gives("ma_ps"))
            elif name == "mb":
                for b in range(2):
                    pe.eng.wait_ge(on("prob"), pe.takes("prob"))
                    for j in range(3):
                        ins = T.transpose(ps[6 + b][:, hs(j)], pm[:, b, hs(j)], ident)
                    ins.then_inc(on("att_ps"), pe.gives("att_ps"))
            elif name == "mc":
                for b in range(2):
                    pe.eng.wait_ge(on("prob_t"), pe.takes("prob_t"))
                    r, c = slice(DH * b, DH * b + DH), slice((2 * n + b) * DH, (2 * n + b + 1) * DH)
                    o = ps[6 + b]
                    T.matmul(o[r, 0:P], v_tok[:, 0, c], pm_t[:, b, 0:P], start=True, stop=True)
                    T.matmul(o[r, P:2 * P], v_tok[:, 0, c], pm_t[:, b, P:2 * P], start=True, stop=False)
                    T.matmul(o[r, P:2 * P], v_tok[:, 1, c], pm_t[:, b, 2 * P:3 * P],
                             start=False, stop=True).then_inc(on("att_ps"), pe.gives("att_ps"))

        def pe_norm(pe, src):
            for t in range(NT):
                pe.eng.wait_ge(on("xn"), pe.takes("xn"))
                for k in range(KT):
                    ins = T.transpose(ps[4 + 2 * t + k // 4][:, hs(k % 4)], src(t)[:, k * P:(k + 1) * P], ident)
                ins.then_inc(on("xnt_ps"), pe.gives("xnt_ps"))
            pe.eng.wait_ge(on("xT"), pe.takes("xT", NT))

        def pe_ffn(pe):
            def up(j):
                up_unit(pe, [ps[4 + j % 4][:, 0:SEQ], ps[4 + j % 4][:, SEQ:2 * SEQ]], xt_hi, xt_lo, "up_ps")

            for j in range(2):
                up(j)
            with pe.turns("up", (FT - 2) // 4):
                for j in range(2, 6):
                    pe.eng.wait_ge(on("conv_f"), pe.takes("conv_f"))
                    up(j)
            release(pe)
            pe.eng.wait_ge(on("conv_f"), pe.takes("conv_f", 2))
            pe.eng.wait_ge(on("h"), pe.takes("h", FT))
            for j in range(FT // 2):
                rows_product(pe, [[ps[t][:, :], ps[2 + t][:, :]] for t in range(NT)], h_hi, h_lo,
                             (2 * j, 2 * j + 1), j == 0, j == FT // 2 - 1,
                             "y_ps" if j == FT // 2 - 1 else None, n_k=2, width=D)
            release(pe)

        def sp_layer(sp, l):
            w_in, w_out, w_up, w_down = a["w_in"][l], a["w_out"][l], a["w_up"][l], a["w_down"][l]
            for u in range(6):
                fetch(sp, cols_unit(w_in, 256 * u, 256 * u + P))
            for c0 in (COL_Z, COL_QB, COL_QB + 512, COL_QB + 1024):
                for j in range(2):
                    fetch(sp, rows_unit(w_in, 4 * j, c0))
            for c in range(2):
                for j in range(2):
                    fetch(sp, rows_unit(w_out, 4 * j, 512 * c))
            for j in range(2):
                fetch(sp, cols_unit(w_up, j * P, D_FF + j * P))
            with sp.turns("up", (FT - 2) // 4) as i:
                for j in range(2, 6):
                    c = i * (4 * P) + j * P
                    fetch(sp, cols_unit(w_up, c, c + D_FF))
            for j in range(FT // 2):
                fetch(sp, rows_unit(w_down, 2 * j, 0, n_k=2, width=D))

        def pool_start(pool):
            pool.eng.dma_start(cst[:, :], a["table_1"]).then_inc(on("cst_in"), pool.gives("cst_in", 16))
            G.memset(rows[:, :, :], 0.0).then_inc(on("p_step"), pool.gives("p_step"))
            G.memset(rows2[:, :, :], 0.0).then_inc(on("p_step"), pool.gives("p_step"))
            G.memset(cs_hl[:, :, :].bitcast(F32), 0.0).then_inc(on("cs_zero"), pool.gives("cs_zero"))
            pool.eng.wait_ge(on("p_step"), pool.given("p_step"))

            def as_rows(v):
                return v.rearrange("(r c) -> r c", c=P)

            r = 0
            for v in ("ln_g_2", "ln_b_2"):
                pool.eng.dma_start(rows2[r:r + 32, 0, :], a[v].rearrange("l n (r c) -> (l n r) c", c=P)).then_inc(
                    on("rows2_in"), pool.gives("rows2_in", 16))
                r += 32
            pool.eng.dma_start(rows2[64:72, 0, :], a["c_2"].rearrange("a (r c) -> (a r) c", c=P)).then_inc(
                on("rows2_in"), pool.gives("rows2_in", 16))
            pool.eng.dma_start(rows2[72:80, 0, :], as_rows(a["c_ctx_2"])).then_inc(
                on("rows2_in"), pool.gives("rows2_in", 16))
            pool.eng.dma_start(rows2[0:96, 1, :], a["ada_b_2"].rearrange("l (r c) -> (l r) c", c=P)).then_inc(
                on("rows2_in"), pool.gives("rows2_in", 16))

        def pool_params(pool, l):
            if l:
                pool.eng.wait_ge(on("par_ps"), pool.takes("par_ps"))
            e = pool.eng

            def as_rows(v):
                return v.rearrange("(r c) -> r c", c=P)

            def load(dst, src, sem="rows_in"):
                e.dma_start(dst, src).then_inc(on(sem), pool.gives(sem, 16))

            load(rows[0:48, 2, :], a["gdn_conv_w"][l].rearrange("j (r c) -> (j r) c", c=P))
            load(rows[0:88, 0, :], a["ffn_conv_w"][l, 0:2].rearrange("j (r c) -> (j r) c", c=P))
            for n, v in enumerate(("ln1_g", "ln1_b", "ln2_g", "ln2_b")):
                load(rows[88 + 8 * n:96 + 8 * n, 0, :], as_rows(a[v][l]))
            load(rows[0:44, 1, :], as_rows(a["ffn_conv_w"][l, 2]))
            load(rows[44:88, 1, :], as_rows(a["ffn_conv_b"][l]))
            load(lay[:, 0:4], a["gdn_a_log"][l].partition_broadcast(P), "lay_in")
            load(lay[:, 4:8], a["gdn_dt_bias"][l].partition_broadcast(P), "lay_in")
            load(lay[:, 8:136], a["gdn_norm_g"][l].partition_broadcast(P), "lay_in")
            load(lay[:, 136:200].rearrange("p (k n) -> p k n", n=8),
                 a["w_in"][l].rearrange("(k p) n -> p k n", p=P)[:, :, COL_A:COL_A + 8], "lay_in")

        def pool_gains(pool, l):
            pool.eng.wait_ge(on("y_ps"), pool.takes("y_ps", 2))
            for n in range(2):
                for m, v in enumerate((("ln1_g", "ln1_b"), ("ln2_g", "ln2_b"))[n]):
                    pool.eng.dma_start(ln_gb[:, n, m, :], a[v][l].partition_broadcast(P)).then_inc(
                        on("gains_in"), pool.gives("gains_in", 16))

        def pool_mixer(pool, l):
            if l:
                pool.eng.wait_ge(on("xT"), pool.takes("xT", 2 * NT))
            G.memset(state[:, :], 0.0).then_inc(on("state0"), pool.gives("state0"))
            for step in [*EARLY, *mixer_steps()]:
                name, n = step if isinstance(step, tuple) else (step, 0)
                if name == "ss":
                    pool.eng.wait_ge(on("pow_in"), pool.takes("pow_in"))
                    G.tensor_tensor(gp[:, 64:80], gp[:, 64:80],
                                             cst[:, C_MISC:C_MISC + 1].to_broadcast([P, 16]), ALU.pow).then_inc(
                                                 on("pow_out"), pool.gives("pow_out"))
                elif name == "kv":
                    pool.eng.wait_ge(on("gate_x"), pool.takes("gate_x"))
                    for t in range(NT):
                        pool.eng.wait_ge(on("kv_out"), pool.takes("kv_out"))
                        for dst, at in ((k_bg, 112), (k_dec, 120)):
                            ins = G.tensor_tensor(heads(dst[:, t, :], HG), heads(k_tok[:, t, :], HG),
                                                  per_head(gp[:, at + 4 * t:at + 4 * t + 4], P), ALU.mult)
                        ins.then_inc(on("k_bg"), pool.gives("k_bg"))
                elif name == "turn":
                    for t in range(NT):
                        pool.eng.wait_ge(on("turn_A"), pool.takes("turn_A"))
                        pool_level(pool, 1, t)
                    for t in range(NT):
                        pool_level(pool, 2, t)
                elif name == "x":
                    pool.eng.wait_ge(on("yy_ps"), pool.takes("yy_ps", NT))
                    for t in range(NT if n < 4 else 0):
                        pool_level(pool, n + 2, t)
                elif name == "out":
                    pool.eng.wait_ge(on("pow_in"), pool.takes("pow_in"))
                    at = 176 + 4 * n
                    G.tensor_tensor(gp[:, at:at + 4], gp[:, at:at + 4],
                                             cst[:, C_MISC:C_MISC + 1].to_broadcast([P, 4]), ALU.pow).then_inc(
                                                 on("pow_out"), pool.gives("pow_out"))

        def pool_level(pool, n, t):
            lev = cst[:, C_LEV + n * P:C_LEV + (n + 1) * P]
            G.tensor_tensor(heads(m_lev[n % 2][:, t, :], HG), heads(att2[:, 0, t, :], HG),
                                     over_heads(lev, HG), ALU.mult).then_inc(on("m_lev"), pool.gives("m_lev"))

        def pool_norm(pool, src, n):
            for t in range(NT):
                pool.eng.wait_ge(on("pow_in"), pool.takes("pow_in"))
                c = 32 * t + 16
                G.tensor_tensor(small[:, c:c + 1], small[:, c:c + 1],
                                         cst[:, C_MISC:C_MISC + 1], ALU.pow).then_inc(
                                             on("pow_out"), pool.gives("pow_out"))
            if n == 0:
                pool.eng.wait_ge(on("gains_in"), pool.takes("gains_in", 64))
            for t in range(NT):
                pool.eng.wait_ge(on("xn"), pool.takes("xn"))
                G.tensor_tensor(xs[:, t, :], src(t), ln_gb[:, n, 0, :], ALU.mult).then_inc(
                    on("p_step"), pool.gives("p_step"))
                pool.eng.wait_ge(on("p_step"), pool.given("p_step"))
                G.tensor_tensor(xs[:, t, :], xs[:, t, :], ln_gb[:, n, 1, :], ALU.add).then_inc(
                    on("xs_new"), pool.gives("xs_new"))

        def act_copy(dst, src):
            return A.activation(dst, src, ACT.Copy)

        def act_start(act):
            act.started = 0
            act.used["w_used"] = 1
            for _ in range(SPLIT_SLOTS):
                split_hi(act)
            act.eng.wait_ge(on("par2_ps"), act.takes("par2_ps"))
            act_copy(par2[:, :, :], ps[6][:, 0:2 * P]).then_inc(on("a_step"), act.gives("a_step"))
            act.eng.wait_ge(on("a_step"), act.given("a_step"))
            silu_c = small[:, 0:16]
            A.activation(silu_c, par2[:, 0, 64:80], ACT.Silu).then_inc(on("a_step"), act.gives("a_step"))
            act.eng.wait_ge(on("a_step"), act.given("a_step"))
            act.eng.wait_ge(on("cs_zero"), act.takes("cs_zero"))
            for n in range(2):
                act_copy(cs_hl[:, :, n], small[:, 8 * n:8 * n + 8]).then_inc(on("start_hi"), act.gives("start_hi"))
            act.eng.wait_ge(on("x0_ps"), act.takes("x0_ps"))
            for t in range(NT):
                for g in range(2):
                    act_copy(xt_hi[:, 4 * g:4 * g + 4, t * P:(t + 1) * P], heads(ps[2 * t + g][:, :], 4)).then_inc(
                        on("start_hi"), act.gives("start_hi"))

        def act_mixer(act, l):
            act.eng.wait_ge(on("par_ps"), act.takes("par_ps"))
            act_copy(par[:, :, :], ps[6][:, 0:3 * P]).then_inc(on("par"), act.gives("par"))
            act.eng.wait_ge(on("lay_in"), act.takes("lay_in", 64))
            act_copy(ab_hi[:, :, :], lay[:, 136:200].rearrange("p (k n) -> p k n", n=8)).then_inc(
                on("ab_hi"), act.gives("ab_hi"))
            act.eng.wait_ge(on("par"), act.given("par"))
            for u in range(6):
                act.eng.wait_ge(on("qkv_ps"), act.takes("qkv_ps"))
                b = ps[4 + u % 3] if u % 3 < 2 else ps[0]
                for g in range(2):
                    f = 2 * u + g
                    A.activation(qkv[:, f, :], b[:, g * SEQ:(g + 1) * SEQ], ACT.Copy,
                                         scale=par[:, 2, 36 + f:37 + f]).then_inc(on("tap"), act.gives("tap"))
                split_hi(act)
                act.eng.wait_ge(on("conv"), act.takes("conv"))
                A.activation(qkv[:, 2 * u:2 * u + 2, :], qkv[:, 2 * u:2 * u + 2, :], ACT.Silu).then_inc(
                    on("silu"), act.gives("silu"))
                if u < 4:
                    act.eng.wait_ge(on("silu"), act.given("silu"))
                    A.activation(squares[:, 2 * u:2 * u + 2, :], qkv[:, 2 * u:2 * u + 2, :], ACT.Square).then_inc(
                        on("sq"), act.gives("sq"))
            for n in range(4):
                split_hi(act)
                act.eng.wait_ge(on("proj_ps"), act.takes("proj_ps"))
                for t in range(NT):
                    src = ps[PROJ_BANK[n] + t][:, :]
                    if n == 0:
                        ins = A.activation(silu_z[:, t, :], src, ACT.Silu)
                    elif n == 3:
                        ins = act_copy(v_tok[:, t, :], src)
                    else:
                        ins = act_copy(qk_tok[:, t, HM * (n - 1):HM * n, :], heads(src, HM))
                    ins.then_inc(on("tok_out"), act.gives("tok_out"))
                split_hi(act)
                if n < 3:
                    act_step(act, EARLY[n])
            for step in mixer_steps():
                act_step(act, step)
            for _ in range(4):
                split_hi(act)

        def act_step(act, step):
            name, n = step if isinstance(step, tuple) else (step, 0)
            if name == "gate":
                act.eng.wait_ge(on("gate_vec"), act.takes("gate_vec"))
                A.activation(gp[:, 56:64], gp[:, 40:48], ACT.Exp, scale=-1.0).then_inc(
                    on("a_step"), act.gives("a_step"))
                act.eng.wait_ge(on("a_step"), act.given("a_step"))
                A.activation(gp[:, 56:64], gp[:, 56:64], ACT.Ln, bias=ones[:, 0:1]).then_inc(
                    on("a_step"), act.gives("a_step"))
                A.activation(gp[:, 168:172], lay[:, 0:4], ACT.Exp).then_inc(on("a_step"), act.gives("a_step"))
                A.activation(gp[:, 24:32].rearrange("p (t h) -> p t h", t=NT),
                                     gp[:, 0:16].rearrange("p (t h) -> p t h", t=NT)[:, :, 4:8], ACT.Exp,
                                     scale=-1.0).then_inc(on("gate_act"), act.gives("gate_act"))
            elif name == "gsum":
                act.eng.wait_ge(on("gate_vec"), act.takes("gate_vec"))
                A.activation(gp[:, 104:112], gp[:, 88:96], ACT.Exp).then_inc(on("a_step"), act.gives("a_step"))
                A.activation(gp[:, 144:160], ps[7][:, 48:64], ACT.Exp).then_inc(
                    on("gate_act"), act.gives("gate_act"))
                act.eng.wait_ge(on("gate_vec"), act.takes("gate_vec"))
                A.activation(gp[:, 120:128], gp[:, 120:128], ACT.Exp).then_inc(on("gate_x"), act.gives("gate_x"))
                for t in range(NT):
                    act.eng.wait_ge(on("gate_vec"), act.takes("gate_vec"))
                    A.activation(dec_y[:, t, :], dec_y[:, t, :], ACT.Exp).then_inc(
                        on("gate_act"), act.gives("gate_act"))
            elif name == "kn":
                for t in range(NT):
                    act.eng.wait_ge(on("rule_ps"), act.takes("rule_ps"))
                    act_copy(kn[:, :, t * P:(t + 1) * P], heads(ps[2 + t][:, :], HG)).then_inc(
                        on("kn"), act.gives("kn"))
            elif name == "turn":
                for t in range(NT):
                    act.eng.wait_ge(on("rule_ps"), act.takes("rule_ps"))
                    act_copy(att2[:, 0, t, :], ps[t][:, :]).then_inc(on("turn_A"), act.gives("turn_A"))
                    act_copy(att2[:, 1, t, :], ps[4 + t][:, :]).then_inc(on("turn_q"), act.gives("turn_q"))
            elif name == "y":
                for t in range(NT):
                    act.eng.wait_ge(on("yy_ps"), act.takes("yy_ps"))
                    act_copy(dec_y[:, t, :], ps[2 + t][:, :]).then_inc(on("yy"), act.gives("yy"))
            elif name == "uw":
                for t in range(NT):
                    act.eng.wait_ge(on("rule_ps"), act.takes("rule_ps"))
                    act_copy(d_inc[:, t, :], ps[2 + t][:, :]).then_inc(on("a_step"), act.gives("a_step"))
                    act_copy(w_t[:, :, t * P:(t + 1) * P], heads(ps[t][:, :], HG)).then_inc(
                        on("uw"), act.gives("uw"))
            elif name == "out":
                act.eng.wait_ge(on("rule_ps"), act.takes("rule_ps"))
                act_copy(xt_hi[:, 0:HG, n * P:(n + 1) * P], heads(ps[n][:, :], HG)).then_inc(
                    on("o_hi"), act.gives("o_hi"))
            elif name == "mt":
                act.eng.wait_ge(on("att_ps"), act.takes("att_ps"))
                act_copy(qk_t[:, 4 * (n % 2):4 * (n % 2) + 4, (n // 2) * P:(n // 2 + 1) * P],
                                 heads(ps[6][:, :], 4)).then_inc(on("qk_t"), act.gives("qk_t"))
            elif name == "ma":
                for b in range(2):
                    act.eng.wait_ge(on("p_max"), act.takes("p_max"))
                    m = 8 * b
                    A.activation(pm[:, b, 0:P], pm[:, b, 0:P], ACT.Exp, bias=ms[:, m + 2:m + 3], scale=DH ** -0.5,
                                 accum_out=ms[:, m + 4:m + 5]).then_inc(on("a_step"), act.gives("a_step"))
                    A.activation(pm[:, b, P:3 * P], pm[:, b, P:3 * P], ACT.Exp, bias=ms[:, m + 3:m + 4],
                                 scale=DH ** -0.5, accum_out=ms[:, m + 5:m + 6]).then_inc(
                                     on("p_exp"), act.gives("p_exp"))
            elif name == "mb":
                for b in range(2):
                    act.eng.wait_ge(on("att_ps"), act.takes("att_ps"))
                    act_copy(pm_t[:, b, :], ps[6 + b][:, 0:3 * P]).then_inc(on("prob_t"), act.gives("prob_t"))
            elif name == "mc":
                for b in range(2):
                    r = slice(DH * b, DH * b + DH)
                    act.eng.wait_ge(on("att_ps"), act.takes("att_ps"))
                    act_copy(xt_hi[r, 4 + n, :], ps[6 + b][r, 0:2 * P]).then_inc(on("a_hi"), act.gives("a_hi"))

        def act_norm(act, gain, bias, fine, hi):
            for t in range(NT):
                act.eng.wait_ge(on("xnt_ps"), act.takes("xnt_ps"))
                for g in range(2):
                    for k in range(4 * g, 4 * g + 4):
                        A.activation(fine[:, t, k, :], ps[4 + 2 * t + g][:, hs(k % 4)], ACT.Identity,
                                     scale=gain[:, k:k + 1], bias=bias[:, k:k + 1]).then_inc(
                                         on("a_step"), act.gives("a_step"))
                    act.eng.wait_ge(on("a_step"), act.given("a_step"))
                    act_copy(hi[:, 4 * g:4 * g + 4, t * P:(t + 1) * P], fine[:, t, 4 * g:4 * g + 4, :]).then_inc(
                        on("x_hi"), act.gives("x_hi"))

        def act_ffn(act):
            def up(j, f):
                act.eng.wait_ge(on("up_ps"), act.takes("up_ps"))
                b = ps[4 + j % 4]
                for g in range(2):
                    A.activation(hid[:, j % 4, g, :], b[:, g * SEQ:(g + 1) * SEQ], ACT.Identity,
                                 scale=par[:, 1, bass.ds(f + FT * g, 1)],
                                 bias=par[:, 1, bass.ds(f + 44 + FT * g, 1)]).then_inc(
                                     on("tap_f"), act.gives("tap_f"))
                split_hi(act)
                if j:
                    up_end(j - 1, f - 1)
                act.eng.wait_ge(on("conv_f"), act.takes("conv_f"))
                A.activation(hid[:, j % 4, 0, :], hid[:, j % 4, 0, :], ACT.Silu).then_inc(
                    on("silu_f"), act.gives("silu_f"))

            def up_end(j, f):
                act.eng.wait_ge(on("gated"), act.takes("gated"))
                act_copy(h_hi[:, bass.ds(f, 1), :], hid[:, j % 4, 1:2, :]).then_inc(on("h_hi"), act.gives("h_hi"))

            for j in range(2):
                up(j, j)
            with act.turns("up", (FT - 2) // 4) as i:
                for j in range(2, 6):
                    up(j, 4 * i + j)
            up_end(FT - 1, FT - 1)
            for _ in range(FT // 2):
                split_hi(act)

        def dve_start(dve):
            dve.eng.sem_inc(on("w_split"), RAW_SLOTS)
            for _ in range(SPLIT_SLOTS):
                split_lo(dve)
            dve.eng.wait_ge(on("start_hi"), dve.takes("start_hi", 2))
            for n in range(2):
                V.tensor_tensor(cs_hl[:, :, 2 + n], small[:, 8 * n:8 * n + 8],
                                        cs_hl[:, :, n].bitcast(F32), ALU.subtract).then_inc(
                                            on("c_lo"), dve.gives("c_lo"))
            dve.eng.wait_ge(on("x0_ps"), dve.takes("x0_ps"))
            for t in range(NT):
                for g in range(2):
                    dve.eng.wait_ge(on("start_hi"), dve.takes("start_hi"))
                    x = (slice(None), slice(4 * g, 4 * g + 4), slice(t * P, (t + 1) * P))
                    V.tensor_tensor(xt_lo[x], heads(ps[2 * t + g][:, :], 4), xt_hi[x].bitcast(F32),
                                            ALU.subtract).then_inc(on("x0"), dve.gives("x0"))

        def taps(dve, dst, src, weights):
            for d, w in enumerate(weights, 1):
                V.scalar_tensor_tensor(dst[:, d:SEQ], src[:, 0:SEQ - d], w, dst[:, d:SEQ], ALU.mult, ALU.add).then_inc(
                    on("v_step"), dve.gives("v_step"))
                dve.eng.wait_ge(on("v_step"), dve.given("v_step"))

        def dve_mixer(dve, l):
            dve.eng.wait_ge(on("ab_hi"), dve.takes("ab_hi"))
            V.tensor_tensor(ab_lo[:, :, :], lay[:, 136:200].rearrange("p (k n) -> p k n", n=8),
                                    ab_hi[:, :, :].bitcast(F32), ALU.subtract).then_inc(
                                        on("ab_split"), dve.gives("ab_split"))
            dve.eng.wait_ge(on("par"), dve.takes("par"))
            for u in range(6):
                b = ps[4 + u % 3] if u % 3 < 2 else ps[0]
                dve.eng.wait_ge(on("tap"), dve.takes("tap", 2))
                for g in range(2):
                    f = 2 * u + g
                    dst, src = qkv[:, f, :], b[:, g * SEQ:(g + 1) * SEQ]
                    w = [par[:, 2, 12 * j + f:12 * j + f + 1] for j in (2, 1, 0)]
                    taps(dve, dst, src, w if g == 0 else w[:2])
                V.scalar_tensor_tensor(dst[:, 3:SEQ], src[:, 0:SEQ - 3], w[2], dst[:, 3:SEQ],
                                               ALU.mult, ALU.add).then_inc(on("conv"), dve.gives("conv"))
                split_lo(dve)
            for n in range(4):
                split_lo(dve)
                split_lo(dve)
                if n == 1:
                    dve.eng.wait_ge(on("tok_out"), dve.takes("tok_out", 2))
                if n < 3:
                    dve_step(dve, EARLY[n])
            dve.eng.wait_ge(on("tok_out"), dve.takes("tok_out", 6))
            for step in mixer_steps():
                dve_step(dve, step)
            for _ in range(4):
                split_lo(dve)

        def dve_step(dve, step):
            name, n = step if isinstance(step, tuple) else (step, 0)
            tt, tsc = V.tensor_tensor, V.tensor_scalar

            def two_by(ap):
                return ap.rearrange("p (t h) -> p t h", t=NT)

            if name == "ss":
                dve.eng.wait_ge(on("ss_ps"), dve.takes("ss_ps"))
                tsc(gp[:, 64:80], ps[7][:, 16:32], NORM_EPS, None, ALU.add).then_inc(
                    on("pow_in"), dve.gives("pow_in"))
            elif name == "gate":
                dve.eng.wait_ge(on("ab_ps"), dve.takes("ab_ps"))
                V.tensor_copy(gp[:, 0:16], ps[7][:, 0:16]).then_inc(on("v_step"), dve.gives("v_step"))
                dve.eng.wait_ge(on("v_step"), dve.given("v_step"))
                tt(two_by(gp[:, 32:40]), two_by(gp[:, 0:16])[:, :, 0:4], over_heads(lay[:, 4:8], NT), ALU.add).then_inc(
                    on("v_step"), dve.gives("v_step"))
                dve.eng.wait_ge(on("v_step"), dve.given("v_step"))
                x = gp[:, 32:40]
                V.scalar_tensor_tensor(gp[:, 40:48], x, -1.0, x, ALU.mult, ALU.max).then_inc(
                    on("gate_vec"), dve.gives("gate_vec"))
                dve.eng.wait_ge(on("gate_act"), dve.takes("gate_act"))
                V.scalar_tensor_tensor(x, x, 0.0, gp[:, 56:64], ALU.max, ALU.add).then_inc(
                    on("v_step"), dve.gives("v_step"))
                dve.eng.wait_ge(on("v_step"), dve.given("v_step"))
                V.scalar_tensor_tensor(two_by(gp[:, 16:24]), two_by(x), -1.0, over_heads(gp[:, 168:172], NT),
                                               ALU.mult, ALU.mult).then_inc(on("v_step"), dve.gives("v_step"))
                tsc(gp[:, 24:32], gp[:, 24:32], 1.0, None, ALU.add).then_inc(on("v_step"), dve.gives("v_step"))
                dve.eng.wait_ge(on("v_step"), dve.given("v_step"))
                V.reciprocal(gp[:, 24:32], gp[:, 24:32]).then_inc(on("v_step"), dve.gives("v_step"))
                dve.eng.wait_ge(on("v_step"), dve.given("v_step"))
                gm = gp[:, 128:144].rearrange("p (t a h) -> p t a h", t=NT, a=2)
                for half in range(2):
                    tsc(gm[:, :, half, :], two_by(gp[:, 16:24]), cst[:, C_HALF + half:C_HALF + half + 1], None,
                                ALU.mult).then_inc(on("v_step"), dve.gives("v_step"))
                for t in range(NT):
                    ins = tt(heads(dec_y[:, t, :], HG), over_heads(ones, HG),
                             per_head(gp[:, 16 + 4 * t:20 + 4 * t], P), ALU.mult)
                    ins.then_inc(on("v_step" if t == 0 else "gates"), dve.gives("v_step" if t == 0 else "gates"))
                for t in range(NT):
                    tt(heads(silu_z[:, t, :], HG), heads(silu_z[:, t, :], HG), over_heads(lay[:, 8:136], HG),
                               ALU.mult).then_inc(on("v_step"), dve.gives("v_step"))
            elif name == "gsum":
                dve.eng.wait_ge(on("gs_ps"), dve.takes("gs_ps"))
                V.tensor_copy(gp[:, 88:104], ps[7][:, 32:48]).then_inc(on("gate_vec"), dve.gives("gate_vec"))
                dve.eng.wait_ge(on("gate_vec"), dve.given("gate_vec"))
                tt(gp[:, 120:128], gp[:, 96:104], gp[:, 88:96], ALU.subtract).then_inc(
                    on("v_step"), dve.gives("v_step"))
                dve.eng.wait_ge(on("v_step"), dve.given("v_step"))
                dve.eng.wait_ge(on("gate_act"), dve.takes("gate_act"))
                dve.eng.wait_ge(on("pow_out"), dve.takes("pow_out"))
                tt(gp[:, 112:120], gp[:, 24:32], gp[:, 104:112], ALU.mult).then_inc(
                    on("v_step"), dve.gives("v_step"))
                tsc(two_by(gp[:, 80:88]), two_by(gp[:, 64:80])[:, :, 0:4], float(P) ** -0.5, None, ALU.mult).then_inc(
                    on("gate_vec"), dve.gives("gate_vec"))
                for t in range(NT):
                    dve.eng.wait_ge(on("grow_ps"), dve.takes("grow_ps"))
                    tt(heads(dec_y[:, t, :], HG), heads(ps[t][:, :], HG),
                                per_head(gp[:, 88 + 4 * t:92 + 4 * t], P), ALU.subtract).then_inc(
                                    on("v_step"), dve.gives("v_step"))
                    dve.eng.wait_ge(on("v_step"), dve.given("v_step"))
                    tsc(dec_y[:, t, :], dec_y[:, t, :], 0.0, -1.0, ALU.max, ALU.mult).then_inc(
                        on("gate_vec"), dve.gives("gate_vec"))
                for t in range(NT):
                    dve.eng.wait_ge(on("gate_act"), dve.takes("gate_act"))
                    d = heads(dec_y[:, t, :], HG)
                    tt(heads(d_inc[:, t, :], HG), d, over_heads(cst[:, C_INC:C_INC + P], HG), ALU.mult).then_inc(
                        on("v_step"), dve.gives("v_step"))
                    tt(heads(d_beta[:, t, :], HG), d, over_heads(cst[:, C_STR:C_STR + P], HG), ALU.mult).then_inc(
                        on("v_step"), dve.gives("v_step"))
                    dve.eng.wait_ge(on("v_step"), dve.given("v_step"))
                    tt(heads(d_beta[:, t, :], HG), heads(d_beta[:, t, :], HG),
                               per_head(gp[:, 24 + 4 * t:28 + 4 * t], P), ALU.mult).then_inc(
                                   on("v_step"), dve.gives("v_step"))
            elif name == "kv":
                for t in range(NT):
                    dve.eng.wait_ge(on("kv_ps"), dve.takes("kv_ps"))
                    tt(heads(k_tok[:, t, :], HG), heads(ps[2 + t][:, :], HG),
                               per_head(gp[:, 68 + 8 * t:72 + 8 * t], P), ALU.mult).then_inc(
                                   on("v_step"), dve.gives("v_step"))
                    tt(heads(v_beta[:, t, :], HG), heads(ps[4 + t][:, :], HG),
                               per_head(gp[:, 24 + 4 * t:28 + 4 * t], P), ALU.mult).then_inc(
                                   on("kv_out"), dve.gives("kv_out"))
            elif name == "gram":
                dve.eng.wait_ge(on("v_step"), dve.given("v_step"))
                for t in range(NT):
                    dve.eng.wait_ge(on("gram_ps"), dve.takes("gram_ps"))
                    tt(a_mat[:, t, :], ps[4 + t][:, :], d_beta[:, t, :], ALU.mult).then_inc(
                        on("v_step"), dve.gives("v_step"))
                    tt(attn[:, t, :], ps[2 + t][:, :], d_inc[:, t, :], ALU.mult).then_inc(
                        on("gram"), dve.gives("gram"))
            elif name == "turn":
                dve.eng.wait_ge(on("v_step"), dve.given("v_step"))
                for t in range(NT):
                    id4 = over_heads(ident, HG)
                    xi, xti = heads(x_inv[:, t, :], HG), heads(xt_inv[:, t, :], HG)
                    tt(xi, heads(a_mat[:, t, :], HG), over_heads(cst[:, C_M1:C_M1 + P], HG), ALU.mult).then_inc(
                        on("v_step"), dve.gives("v_step"))
                    dve.eng.wait_ge(on("v_step"), dve.given("v_step"))
                    tt(xi, id4, xi, ALU.subtract).then_inc(on("v_step"), dve.gives("v_step"))
                    dve.eng.wait_ge(on("turn_A"), dve.takes("turn_A"))
                    tt(xti, heads(att2[:, 0, t, :], HG), over_heads(cst[:, C_LEV:C_LEV + P], HG), ALU.mult).then_inc(
                        on("v_step"), dve.gives("v_step"))
                    dve.eng.wait_ge(on("v_step"), dve.given("v_step"))
                    tt(xti, id4, xti, ALU.subtract).then_inc(on("x_inv"), dve.gives("x_inv"))
            elif name == "x":
                dve.eng.wait_ge(on("x_inv"), dve.given("x_inv"))
                dve.eng.wait_ge(on("v_step"), dve.given("v_step"))
                for t in range(NT):
                    dve.eng.wait_ge(on("xx_ps"), dve.takes("xx_ps"))
                    if n < 5:
                        tt(x_inv[:, t, :], x_inv[:, t, :], ps[t][:, :], ALU.subtract).then_inc(
                            on("v_step"), dve.gives("v_step"))
                    tt(xt_inv[:, t, :], xt_inv[:, t, :], ps[4 + t][:, :], ALU.subtract).then_inc(
                        on("x_inv"), dve.gives("x_inv"))
            elif name == "ws":
                t, lo = n // 2, CHUNK * (n % 2)
                half = slice(lo, lo + CHUNK)
                if n == 0:
                    dve.eng.wait_ge(on("uw"), dve.takes("uw", NT))
                dve.eng.wait_ge(on("ws_ps"), dve.takes("ws_ps"))
                tt(a_mat[half, t, :], d_inc[half, t, :], ps[4][half, :], ALU.subtract).then_inc(
                    on("v_new"), dve.gives("v_new"))
            elif name == "ov":
                t, c = n // 2, 144 + 4 * n
                dve.eng.wait_ge(on("os_ps"), dve.takes("os_ps"))
                if n < N_CHUNKS - 1:
                    if n:
                        dve.eng.wait_ge(on("state"), dve.given("state"))
                    else:
                        dve.eng.wait_ge(on("state0"), dve.takes("state0"))
                    tt(heads(state[:, :], HG), heads(state[:, :], HG), per_head(gp[:, c:c + 4], P), ALU.mult).then_inc(
                        on("v_step"), dve.gives("v_step"))
                    dve.eng.wait_ge(on("v_step"), dve.given("v_step"))
                    dve.eng.wait_ge(on("st_ps"), dve.takes("st_ps"))
                    tt(state[:, :], state[:, :], ps[5][:, :], ALU.add).then_inc(on("state"), dve.gives("state"))
            elif name == "out":
                t = n
                dve.eng.wait_ge(on("ov_ps"), dve.takes("ov_ps", 2))
                o = heads(attn[:, t, :], HG)
                tt(o, heads(ps[t][:, :], HG), per_head(gp[:, 104 + 4 * t:108 + 4 * t], P), ALU.mult).then_inc(
                    on("v_step"), dve.gives("v_step"))
                dve.eng.wait_ge(on("v_step"), dve.given("v_step"))
                tt(attn[:, t, :], attn[:, t, :], ps[2 + t][:, :], ALU.add).then_inc(
                    on("v_step"), dve.gives("v_step"))
                dve.eng.wait_ge(on("v_step"), dve.given("v_step"))
                tt(o, o, per_head(gp[:, 80 + 4 * t:84 + 4 * t], P), ALU.mult).then_inc(
                    on("v_step"), dve.gives("v_step"))
                dve.eng.wait_ge(on("v_step"), dve.given("v_step"))
                tt(x_inv[:, t, :], attn[:, t, :], attn[:, t, :], ALU.mult).then_inc(
                    on("v_step"), dve.gives("v_step"))
                dve.eng.wait_ge(on("v_step"), dve.given("v_step"))
                r = gp[:, 176 + 4 * t:180 + 4 * t]
                V.tensor_reduce(r, heads(x_inv[:, t, :], HG), AX_X, ALU.add).then_inc(
                    on("v_step"), dve.gives("v_step"))
                dve.eng.wait_ge(on("v_step"), dve.given("v_step"))
                tsc(r, r, 1.0 / P, NORM_EPS, ALU.mult, ALU.add).then_inc(on("pow_in"), dve.gives("pow_in"))
                dve.eng.wait_ge(on("pow_out"), dve.takes("pow_out"))
                tt(o, o, per_head(r, P), ALU.mult).then_inc(on("v_step"), dve.gives("v_step"))
                dve.eng.wait_ge(on("v_step"), dve.given("v_step"))
                tt(attn[:, t, :], attn[:, t, :], silu_z[:, t, :], ALU.mult).then_inc(
                    on("o_rule"), dve.gives("o_rule"))
                dve.eng.wait_ge(on("o_hi"), dve.takes("o_hi"))
                dst = (slice(None), slice(0, HG), slice(t * P, (t + 1) * P))
                tt(xt_lo[dst], heads(ps[t][:, :], HG), xt_hi[dst].bitcast(F32), ALU.subtract).then_inc(
                    on("mix_rule"), dve.gives("mix_rule"))
            elif name == "mt" and n % 2 == 0:
                t = n // 2
                x1, x2 = qk_tok[:, t, :, 0:8], qk_tok[:, t, :, 8:16]
                cos = over_heads(cst[:, C_COS + 8 * t:C_COS + 8 * t + 8], 2 * HM)
                sin = over_heads(cst[:, C_SIN + 8 * t:C_SIN + 8 * t + 8], 2 * HM)
                for i, (x, w) in enumerate(((x1, cos), (x2, sin), (x2, cos), (x1, sin))):
                    tt(rot[:, i, :, :], x, w, ALU.mult).then_inc(on("v_step"), dve.gives("v_step"))
                dve.eng.wait_ge(on("v_step"), dve.given("v_step"))
                tt(x1, rot[:, 0, :, :], rot[:, 1, :, :], ALU.subtract).then_inc(on("v_step"), dve.gives("v_step"))
                tt(x2, rot[:, 2, :, :], rot[:, 3, :, :], ALU.add).then_inc(on("rot"), dve.gives("rot"))
            elif name == "ma":
                for b in range(2):
                    m = 8 * b
                    dve.eng.wait_ge(on("ma_ps"), dve.takes("ma_ps"))
                    tt(pm[:, b, :], ps[6 + b][:, 0:3 * P], cst[:, C_CAUSAL:C_CAUSAL + 3 * P], ALU.add).then_inc(
                        on("v_step"), dve.gives("v_step"))
                    dve.eng.wait_ge(on("v_step"), dve.given("v_step"))
                    V.tensor_reduce(ms[:, m:m + 1], pm[:, b, 0:P], AX_X, ALU.max).then_inc(
                        on("v_step"), dve.gives("v_step"))
                    V.tensor_reduce(ms[:, m + 1:m + 2], pm[:, b, P:3 * P], AX_X, ALU.max).then_inc(
                        on("v_step"), dve.gives("v_step"))
                    dve.eng.wait_ge(on("v_step"), dve.given("v_step"))
                    tsc(ms[:, m + 2:m + 4], ms[:, m:m + 2], -DH ** -0.5, None, ALU.mult).then_inc(
                        on("p_max"), dve.gives("p_max"))
            elif name == "mb":
                for b in range(2):
                    m = 8 * b
                    dve.eng.wait_ge(on("p_exp"), dve.takes("p_exp"))
                    V.reciprocal(ms[:, m + 6:m + 8], ms[:, m + 4:m + 6]).then_inc(on("v_step"), dve.gives("v_step"))
                    dve.eng.wait_ge(on("v_step"), dve.given("v_step"))
                    tsc(pm[:, b, 0:P], pm[:, b, 0:P], ms[:, m + 6:m + 7], None, ALU.mult).then_inc(
                        on("v_step"), dve.gives("v_step"))
                    tsc(pm[:, b, P:3 * P], pm[:, b, P:3 * P], ms[:, m + 7:m + 8], None, ALU.mult).then_inc(
                        on("prob"), dve.gives("prob"))
            elif name == "mc":
                for b in range(2):
                    r = slice(DH * b, DH * b + DH)
                    dve.eng.wait_ge(on("a_hi"), dve.takes("a_hi"))
                    sem = "mix_att" if b else "v_step"
                    tt(xt_lo[r, 4 + n, :], ps[6 + b][r, 0:2 * P], xt_hi[r, 4 + n, :].bitcast(F32),
                       ALU.subtract).then_inc(on(sem), dve.gives(sem))

        def dve_statistics(dve, x, t):
            c = 32 * t
            for j in range(2):
                V.bn_stats(small[:, c + 6 * j:c + 6 * j + 6], x[:, 512 * j:512 * j + 512]).then_inc(
                    on("v_step"), dve.gives("v_step"))
            dve.eng.wait_ge(on("v_step"), dve.given("v_step"))
            V.bn_aggr(small[:, c + 12:c + 14], small[:, c:c + 12]).then_inc(on("v_step"), dve.gives("v_step"))
            dve.eng.wait_ge(on("v_step"), dve.given("v_step"))
            V.tensor_scalar(small[:, c + 16:c + 17], small[:, c + 13:c + 14], LN_EPS, None, ALU.add).then_inc(
                on("pow_in"), dve.gives("pow_in"))

        def dve_norm(dve, halves, fine, hi, lo):
            def residual(c, t):
                x = xs[:, t, 512 * c:512 * c + 512]
                V.scalar_tensor_tensor(x, x, ALPHA, ps[2 * c + t][:, :], ALU.mult, ALU.add).then_inc(
                    on("v_step"), dve.gives("v_step"))

            dve.eng.wait_ge(on("y_ps"), dve.takes("y_ps"))
            if halves == 2:
                for t in range(NT):
                    residual(0, t)
                dve.eng.wait_ge(on("y_ps"), dve.takes("y_ps"))
            for t in range(NT):
                for c in range(halves - 1, 2):
                    residual(c, t)
                dve.eng.wait_ge(on("v_step"), dve.given("v_step"))
                dve_statistics(dve, xs[:, t, :], t)
            for t in range(NT):
                dve.eng.wait_ge(on("pow_out"), dve.takes("pow_out"))
                c = 32 * t
                V.tensor_scalar(xn1[:, t, :], xs[:, t, :], small[:, c + 12:c + 13], small[:, c + 16:c + 17],
                                        ALU.subtract, ALU.mult).then_inc(on("xn"), dve.gives("xn"))
            for t in range(NT):
                for g in range(2):
                    dve.eng.wait_ge(on("x_hi"), dve.takes("x_hi"))
                    x = (slice(None), slice(4 * g, 4 * g + 4), slice(t * P, (t + 1) * P))
                    ins = V.tensor_tensor(lo[x], fine[:, t, 4 * g:4 * g + 4, :], hi[x].bitcast(F32), ALU.subtract)
                ins.then_inc(on("xT"), dve.gives("xT"))

        def dve_ffn(dve):
            def up(j, f):
                b = ps[4 + j % 4]
                dve.eng.wait_ge(on("tap_f"), dve.takes("tap_f", 2))
                for d in (1, 2):
                    for g in range(2):
                        dst, src = hid[:, j % 4, g, :], b[:, g * SEQ:(g + 1) * SEQ]
                        w = par[:, 0, bass.ds(f + 44 * (2 - d) + FT * g, 1)]
                        sem = "conv_f" if g == 1 and d == 2 else "v_step"
                        V.scalar_tensor_tensor(dst[:, d:SEQ], src[:, 0:SEQ - d], w, dst[:, d:SEQ],
                                               ALU.mult, ALU.add).then_inc(on(sem), dve.gives(sem))
                    if d == 1:
                        dve.eng.wait_ge(on("v_step"), dve.given("v_step"))
                if j:
                    up_gate(j - 1)
                split_lo(dve)
                if j:
                    up_end(j - 1, f - 1)

            def up_gate(j):
                dve.eng.wait_ge(on("silu_f"), dve.takes("silu_f"))
                V.tensor_tensor(hid[:, j % 4, 1, :], hid[:, j % 4, 0, :], hid[:, j % 4, 1, :], ALU.mult).then_inc(
                    on("gated"), dve.gives("gated"))

            def up_end(j, f):
                dve.eng.wait_ge(on("gated"), dve.given("gated"))
                dve.eng.wait_ge(on("h_hi"), dve.takes("h_hi"))
                V.tensor_tensor(h_lo[:, bass.ds(f, 1), :], hid[:, j % 4, 1:2, :],
                                h_hi[:, bass.ds(f, 1), :].bitcast(F32), ALU.subtract).then_inc(
                                    on("h"), dve.gives("h"))

            for j in range(2):
                up(j, j)
            with dve.turns("up", (FT - 2) // 4) as i:
                for j in range(2, 6):
                    up(j, 4 * i + j)
            up_gate(FT - 1)
            up_end(FT - 1, FT - 1)
            for _ in range(FT // 2):
                split_lo(dve)

        def pe_ada(pe, l):
            def fold(b):
                pe.eng.wait_ge(on("ada_row"), pe.takes("ada_row"))
                for f in range(4):
                    ins = T.matmul(ps[6 + b][:, 2 * f:2 * f + 2], ada_row[0:4, b, hs(f)],
                                   cst[0:4, C_FOLD:C_FOLD + 2], start=True, stop=True)
                ins.then_inc(on("fold_ps"), pe.gives("fold_ps"))

            with pe.turns("ada", 6):
                for b in range(2):
                    for j in range(2):
                        hi, lo = unit_slot(pe)
                        for k in range(4):
                            w = slice(512 * k, 512 * k + 512)
                            ins = T.matmul(ps[4 + b][:, :], cs_hl[:, 4 * j + k, :], hi[:, w],
                                           start=j == k == 0, stop=False)
                            if j == k == 0:
                                ins.then_inc(on("w_used"), pe.gives("w_used"))
                            ins = T.matmul(ps[4 + b][:, :], cs_hl[:, 4 * j + k, :], lo[:, w],
                                           start=False, stop=j == 1 and k == 3)
                        if j == 0:
                            ins.then_inc(on("w_used"), pe.gives("w_used"))
                            if b == 1:
                                fold(0)
                    ins.then_inc(on("ada_ps"), pe.gives("ada_ps"))
                fold(1)

        def act_ada(act):
            with act.turns("ada", 6):
                for b in range(2):
                    split_hi(act)
                    act.eng.wait_ge(on("ada_ps"), act.takes("ada_ps"))
                    act_copy(ada_row[0:4, b, :], ps[4 + b][0:4, :]).then_inc(on("ada_row"), act.gives("ada_row"))
                    split_hi(act)

        def dve_ada(dve, l):
            with dve.turns("ada", 6) as i:
                for b in range(2):
                    for j in range(2):
                        split_lo(dve)
                        if j != b:
                            dve.eng.wait_ge(on("fold_ps"), dve.takes("fold_ps"))
                            V.tensor_copy(mod[:, l, bass.ds(8 * i + 4 * b, 4), :],
                                          ps[6 + b][:, 0:8].rearrange("p (f s) -> p f s", s=2)).then_inc(
                                              on("mod_raw"), dve.gives("mod_raw"))

        def dve_coef(dve, n, gain, bias, l, chunk, stream, sem="v_step"):
            sh = mod[:, l, 8 * chunk:8 * chunk + 8, stream]
            sc_ = mod[:, l, 8 * chunk + 8:8 * chunk + 16, stream]
            if gain is None:
                V.tensor_scalar(coef[:, n, 0, :], sc_, 1.0, None, ALU.add).then_inc(
                    on("v_step"), dve.gives("v_step"))
                V.tensor_copy(coef[:, n, 1, :], sh).then_inc(on(sem), dve.gives(sem))
            else:
                V.scalar_tensor_tensor(coef[:, n, 0, :], sc_, 1.0, gain, ALU.add, ALU.mult).then_inc(
                    on("v_step"), dve.gives("v_step"))
                V.scalar_tensor_tensor(coef[:, n, 1, :], sc_, 1.0, bias, ALU.add, ALU.mult).then_inc(
                    on("v_step"), dve.gives("v_step"))
                dve.eng.wait_ge(on("v_step"), dve.given("v_step"))
                V.tensor_tensor(coef[:, n, 1, :], coef[:, n, 1, :], sh, ALU.add).then_inc(on(sem), dve.gives(sem))

        def dve_mods(dve):
            dve.eng.wait_ge(on("mod_raw"), dve.given("mod_raw"))
            for l in range(DEPTH):
                V.tensor_tensor(mod[:, l, :, :], mod[:, l, :, :], per_head(par2[:, 1, 48 * l:48 * l + 48], 2),
                                         ALU.add).then_inc(on("v_step"), dve.gives("v_step"))
                dve.eng.wait_ge(on("v_step"), dve.given("v_step"))

            def ln(i, j):
                c = 8 * (2 * i + j)
                return par2[:, 0, c:c + 8], par2[:, 0, 32 + c:40 + c]

            dve_coef(dve, 0, None, None, 0, 0, 1)
            dve_coef(dve, 2, *ln(0, 0), 0, 3, 0)
            dve_coef(dve, 3, *ln(0, 0), 0, 3, 1)
            dve_coef(dve, 4, *ln(0, 1), 1, 0, 0)
            dve_coef(dve, 5, *ln(0, 1), 1, 0, 1)
            dve_coef(dve, 6, *ln(1, 0), 1, 3, 0, "coef")

        def x_of(t):
            return xc[:, t, :] if t < NT else xs[:, t - NT, :]

        def stream_of(t):
            return 1 if t < NT else 0

        def pe_turned(pe, src, bank):
            for k in range(KT):
                ins = T.transpose(ps[bank + k // 4][:, hs(k % 4)], src[:, k * P:(k + 1) * P], ident)
            ins.then_inc(on("xnt_ps"), pe.gives("xnt_ps"))

        def act_turned(act, t, bank, n):
            act.eng.wait_ge(on("xnt_ps"), act.takes("xnt_ps"))
            if act.turned >= 2:
                act.eng.wait_ge(on("zT"), act.takes("zT"))
            fine = xf2[:, act.turned % 2, :, :]
            act.turned += 1
            for g in range(2):
                for k in range(4 * g, 4 * g + 4):
                    A.activation(fine[:, k, :], ps[bank + g][:, hs(k % 4)], ACT.Identity,
                                 scale=coef[:, n, 0, k:k + 1], bias=coef[:, n, 1, k:k + 1]).then_inc(
                                     on("a_step"), act.gives("a_step"))
                act.eng.wait_ge(on("a_step"), act.given("a_step"))
                act_copy(zt_hi[:, 4 * g:4 * g + 4, t * P:(t + 1) * P], fine[:, 4 * g:4 * g + 4, :]).then_inc(
                    on("z_hi"), act.gives("z_hi"))

        def dve_turned(dve, t):
            for g in range(2):
                dve.eng.wait_ge(on("z_hi"), dve.takes("z_hi"))
                x = (slice(None), slice(4 * g, 4 * g + 4), slice(t * P, (t + 1) * P))
                ins = V.tensor_tensor(zt_lo[x], xf2[:, t % 2, 4 * g:4 * g + 4, :], zt_hi[x].bitcast(F32),
                                      ALU.subtract)
            ins.then_inc(on("zT"), dve.gives("zT"))

        def dve_gates(dve, l, chunk, tiles):
            for s in sorted({stream_of(t) for t in tiles}):
                V.tensor_tensor(xf2[:, s, :, :], over_heads(ident, KT),
                                per_head(mod[:, l, 8 * chunk:8 * chunk + 8, s], P), ALU.mult).then_inc(
                                    on("diag"), dve.gives("diag"))

        def pe_gates(pe, tiles):
            for s in sorted({stream_of(t) for t in tiles}):
                pe.eng.wait_ge(on("diag"), pe.takes("diag"))
                for k in range(KT):
                    ins = T.matmul(ps[4 + 2 * s + k // 4][:, hs(k % 4)], ones, xf2[:, s, k, :], start=True, stop=True)
                ins.then_inc(on("gate_ps"), pe.gives("gate_ps"))

        def pe_gates_end(pe, tiles):
            n = 2 * len({stream_of(t) for t in tiles})
            pe.eng.wait_ge(on("gate_b"), pe.takes("gate_b", n))

        def act_gates(act, tiles):
            for s in sorted({stream_of(t) for t in tiles}):
                act.eng.wait_ge(on("gate_ps"), act.takes("gate_ps"))
                for j in range(2):
                    act_copy(gate_b[:, s, 512 * j:512 * j + 512], ps[4 + 2 * s + j][:, :]).then_inc(
                        on("gate_b"), act.gives("gate_b"))

        def pe_norm2(pe, tiles):
            for n, t in enumerate(tiles):
                pe.eng.wait_ge(on("zn"), pe.takes("zn"))
                if n >= 2:
                    pe.eng.wait_ge(on("zT"), pe.takes("zT"))
                pe_turned(pe, y[:, t, :], 4 + 2 * (n % 2))
            pe.eng.wait_ge(on("zT"), pe.takes("zT", 2))

        def act_norm2(act, tiles, coefs):
            for n, t in enumerate(tiles):
                act_turned(act, t, 4 + 2 * (n % 2), coefs[stream_of(t)])

        def dve_norm2(dve, tiles, last, banks=None):
            def residual(t):
                if banks:
                    for c in range(2):
                        w = slice(512 * c, 512 * c + 512)
                        V.tensor_tensor(y[:, t, w], banks[2 * c + t - NT][:, :], gate_b[:, 0, w], ALU.mult).then_inc(
                            on("v_step"), dve.gives("v_step"))
                else:
                    V.tensor_tensor(y[:, t, :], y[:, t, :], gate_b[:, stream_of(t), :], ALU.mult).then_inc(
                        on("v_step"), dve.gives("v_step"))
                dve.eng.wait_ge(on("v_step"), dve.given("v_step"))
                V.scalar_tensor_tensor(x_of(t), x_of(t), ALPHA, y[:, t, :], ALU.mult, ALU.add).then_inc(
                    on("v_step"), dve.gives("v_step"))
                dve.eng.wait_ge(on("v_step"), dve.given("v_step"))
                dve_statistics(dve, x_of(t), t % 2)

            def normal(t):
                dve.eng.wait_ge(on("pow_out"), dve.takes("pow_out"))
                c = 32 * (t % 2)
                V.tensor_scalar(y[:, t, :], x_of(t), small[:, c + 12:c + 13], small[:, c + 16:c + 17],
                                ALU.subtract, ALU.mult).then_inc(on("zn"), dve.gives("zn"))

            dve.eng.wait_ge(on("y_add"), dve.given("y_add"))
            dve.eng.wait_ge(on("gate_b"), dve.takes("gate_b", 2 * len({stream_of(t) for t in tiles})))
            residual(tiles[0])
            for n in range(1, len(tiles) + 2):
                if n < len(tiles):
                    residual(tiles[n])
                if n <= len(tiles):
                    normal(tiles[n - 1])
                if n >= 2 and not last:
                    dve_turned(dve, tiles[n - 2])
            if not last:
                dve.eng.wait_ge(on("zT"), dve.given("zT"))

        def pool_norm2(pool, l, m, tiles):
            def power(t):
                pool.eng.wait_ge(on("pow_in"), pool.takes("pow_in"))
                c = 32 * (t % 2) + 16
                G.tensor_tensor(small[:, c:c + 1], small[:, c:c + 1], cst[:, C_MISC:C_MISC + 1], ALU.pow).then_inc(
                    on("pow_out"), pool.gives("pow_out"))

            pool.eng.wait_ge(on("gate_b"), pool.takes("gate_b", 2 * len({stream_of(t) for t in tiles})))
            pool.eng.wait_ge(on("zs_new"), pool.given("zs_new"))
            for j, v in enumerate(("ln_g_2", "ln_b_2")):
                pool.eng.dma_start(gn2[:, j, :], a[v][l, m].partition_broadcast(P)).then_inc(
                    on("gn2_in"), pool.gives("gn2_in", 16))
            power(tiles[0])
            for n, t in enumerate(tiles):
                if n + 1 < len(tiles):
                    power(tiles[n + 1])
                pool.eng.wait_ge(on("zn"), pool.takes("zn"))
                if n == 0:
                    pool.eng.wait_ge(on("gn2_in"), pool.takes("gn2_in", 32))
                G.tensor_tensor(x_of(t), y[:, t, :], gn2[:, 0, :], ALU.mult).then_inc(
                    on("p_step"), pool.gives("p_step"))
                pool.eng.wait_ge(on("p_step"), pool.given("p_step"))
                G.tensor_tensor(x_of(t), x_of(t), gn2[:, 1, :], ALU.add).then_inc(
                    on("zs_new"), pool.gives("zs_new"))

        def down_unit(pe, h_hi_, h_lo_, tiles, banks):
            hi, lo = unit_slot(pe)
            for n, t in enumerate(tiles):
                pe.eng.wait_ge(on("y_add"), pe.takes("y_add"))
                x = slice(n * P, (n + 1) * P)
                for k in range(4):
                    w = slice(512 * k, 512 * k + 512)
                    first, last = three(ps[banks[n]][:, :], h_hi_[:, k, x], h_lo_[:, k, x], hi[:, w], lo[:, w],
                                        k == 0, k == 3)
                    if n == k == 0:
                        begun(pe, first)
                last.then_inc(on("dn_ps"), pe.gives("dn_ps"))

        def dve_add(dve, c, tiles, banks):
            for n, t in enumerate(tiles):
                dve.eng.wait_ge(on("dn_ps"), dve.takes("dn_ps"))
                yt = y[:, t, 512 * c:512 * c + 512]
                V.tensor_tensor(yt, yt, ps[banks[n]][:, :], ALU.add).then_inc(on("y_add"), dve.gives("y_add"))

        ALL, LAT = (0, 1, 2, 3), (2, 3)

        def sp_ret(sp):
            w, w_o = a["ret_w_in_2"][0], a["ret_w_o_2"][0]
            with sp.turns("ret", RH) as h:
                for base in (0, RH * RDK):
                    fetch(sp, cols_unit(w, h * RDK + base, h * RDK + (base + P)))
                for base in (2 * RH * RDK, 2 * RH * RDK + RH * RDV):
                    for j in range(2):
                        fetch(sp, rows_unit(w, 4 * j, h * RDV + base))
                for c in range(2):
                    fetch(sp, rows_unit(w_o, h * 4, 512 * c))

        def pe_ret(pe):
            with pe.turns("ret", RH):
                for n in range(2):
                    up_unit(pe, [ps[2 * n][:, :], ps[2 * n + 1][:, :]], zt_hi, zt_lo, "proj_ps")
                for j in range(2):
                    rows_product(pe, [[ps[4 + t][:, :]] for t in ALL], zt_hi, zt_lo, range(4 * j, 4 * j + 4),
                                 j == 0, j == 1, "proj_ps" if j else None)
                pe.eng.wait_ge(on("rqk"), pe.takes("rqk", 2))
                for st in range(2):
                    for f in range(2):
                        ins = T.matmul(ps[st][:, :], rqk[:, 1, f, st * P:(st + 1) * P], rqk[:, 0, f, :],
                                       start=f == 0, stop=f == 1)
                    ins.then_inc(on("rs_ps"), pe.gives("rs_ps"))
                for st in range(2):
                    for f in range(2):
                        c = SEQ + st * P
                        ins = T.matmul(ps[2][:, st * SEQ:(st + 1) * SEQ], rqk[:, 1, f, c:c + P],
                                       rqk[:, 0, f, SEQ:2 * SEQ], start=f == 0, stop=f == 1)
                ins.then_inc(on("rs_ps"), pe.gives("rs_ps"))
                pe.eng.wait_ge(on("rv"), pe.takes("rv", 4))
                pe.eng.wait_ge(on("rs"), pe.takes("rs", 3))
                for t in ALL:
                    keys = [(rs[:, st, t * P:(t + 1) * P], st) for st in range(2)]
                    if t >= NT:
                        keys += [(rs[:, 2, st * SEQ + (t - NT) * P:st * SEQ + (t - NT + 1) * P], NT + st)
                                 for st in range(2)]
                    for n, (s_, v) in enumerate(keys):
                        ins = T.matmul(ps[4 + t][:, :], s_, rv[:, v, :], start=n == 0, stop=n == len(keys) - 1)
                    ins.then_inc(on("pv_ps"), pe.gives("pv_ps"))
                for j in range(2):
                    rows_product(pe, [[ps[t][:, :]] for t in ALL], zt_hi, zt_lo, range(4 * j, 4 * j + 4),
                                 j == 0, j == 1, "proj_ps" if j else None)
                pe.eng.wait_ge(on("ro"), pe.takes("ro", 4))
                for f in range(4):
                    for t in ALL:
                        ins = T.transpose(ps[4 + f][:, hs(t)], rv[:, t, hs(f)], ident)
                    ins.then_inc(on("rt_ps"), pe.gives("rt_ps"))
                pe.eng.wait_ge(on("rg"), pe.takes("rg", 4))
                pe.eng.wait_ge(on("rt"), pe.takes("rt", 4))
                for c in range(2):
                    down_unit(pe, rt_hi, rt_lo, ALL, ALL)
                pe.eng.wait_ge(on("y_add"), pe.beyond("y_add", 4))
                release(pe)

        def act_ret(act):
            act.eng.wait_ge(on("rdec_in"), act.takes("rdec_in", 32))
            A.activation(rsm[:, 72:80], rsm[:, 72:80], ACT.Exp).then_inc(on("r_lg"), act.gives("r_lg"))
            with act.turns("ret", RH):
                split_hi(act)
                split_hi(act)
                for st in range(2):
                    act.eng.wait_ge(on("r_arg"), act.takes("r_arg"))
                    for n, c in ((0, 80), (1, 82), (2, 80), (3, 81)):
                        A.activation(rtmp[:, n, :], rtmp[:, n, :], ACT.Exp, scale=rsm[:, c:c + 1]).then_inc(
                            on("a_step" if n < 3 else "r_exp"), act.gives("a_step" if n < 3 else "r_exp"))
                for n in range(2):
                    act.eng.wait_ge(on("proj_ps"), act.takes("proj_ps"))
                    for f in range(2):
                        act_copy(rqk[:, n, f, 0:SEQ], ps[2 * n + f][:, 0:SEQ]).then_inc(
                            on("rqk_c"), act.gives("rqk_c"))
                act.eng.wait_ge(on("proj_ps"), act.takes("proj_ps"))
                split_hi(act)
                for t in ALL:
                    act_copy(rv[:, t, :], ps[4 + t][:, :]).then_inc(on("rv"), act.gives("rv"))
                split_hi(act)
                split_hi(act)
                act.eng.wait_ge(on("proj_ps"), act.takes("proj_ps"))
                for t in ALL:
                    A.activation(rg[:, t, :], ps[t][:, :], ACT.Silu).then_inc(on("rg"), act.gives("rg"))
                for f in range(4):
                    act.eng.wait_ge(on("rt_ps"), act.takes("rt_ps"))
                    act_copy(rt_hi[:, f, :], ps[4 + f][:, :]).then_inc(on("rt_hi"), act.gives("rt_hi"))
                for _ in range(3):
                    split_hi(act)

        def dve_ret(dve):
            dve.eng.wait_ge(on("r_lg"), dve.takes("r_lg"))
            V.tensor_scalar(rsm[:, 84:92], rsm[:, 72:80], -1.0, None, ALU.mult).then_inc(
                on("v_step"), dve.gives("v_step"))
            dve.eng.wait_ge(on("v_step"), dve.given("v_step"))
            delta = rope[:, R_DEL:R_DEL + SEQ]
            stt, tsc = V.scalar_tensor_tensor, V.tensor_scalar
            for t in ALL:
                V.memset(y[:, t, :], 0.0).then_inc(on("v_step"), dve.gives("v_step"))
            with dve.turns("ret", RH) as h:
                split_lo(dve)
                V.tensor_copy(rsm[:, 80:82].unsqueeze(2),
                                       rsm[:, 84:92].rearrange("p (d h) -> p d h", d=2)[:, :, bass.ds(h, 1)]).then_inc(
                                           on("v_step"), dve.gives("v_step"))
                dve.eng.wait_ge(on("v_step"), dve.given("v_step"))
                tsc(rsm[:, 82:83], rsm[:, 81:82], -1.0, None, ALU.mult).then_inc(on("v_step"), dve.gives("v_step"))
                dve.eng.wait_ge(on("v_step"), dve.given("v_step"))
                for st in range(2):
                    o = float(P * st)
                    tsc(rtmp[:, 0, :], delta, -o, 0.0, ALU.add, ALU.max).then_inc(on("v_step"), dve.gives("v_step"))
                    tsc(rtmp[:, 1, :], delta, -o, 0.0, ALU.add, ALU.min).then_inc(on("v_step"), dve.gives("v_step"))
                    tsc(rtmp[:, 2, :], delta, SEQ - o, None, ALU.add).then_inc(on("v_step"), dve.gives("v_step"))
                    tsc(rtmp[:, 3, :], delta, -1.0, SEQ + o, ALU.mult, ALU.add).then_inc(
                        on("r_arg"), dve.gives("r_arg"))
                    if st == 0:
                        split_lo(dve)
                    dve.eng.wait_ge(on("r_exp"), dve.takes("r_exp"))
                    stt(wd[:, st, 0:SEQ], delta, o, rtmp[:, 0, :], ALU.is_ge, ALU.mult).then_inc(
                        on("v_step"), dve.gives("v_step"))
                    stt(rtmp[:, 1, :], delta, o, rtmp[:, 1, :], ALU.is_le, ALU.mult).then_inc(
                        on("v_step"), dve.gives("v_step"))
                    dve.eng.wait_ge(on("v_step"), dve.given("v_step"))
                    V.tensor_tensor(wd[:, st, 0:SEQ], wd[:, st, 0:SEQ], rtmp[:, 1, :], ALU.add).then_inc(
                        on("v_step"), dve.gives("v_step"))
                    V.tensor_tensor(wd[:, st, SEQ:2 * SEQ], rtmp[:, 2, :], rtmp[:, 3, :], ALU.add).then_inc(
                        on("v_step"), dve.gives("v_step"))
                    dve.eng.wait_ge(on("v_step"), dve.given("v_step"))
                for n in range(2):
                    dve.eng.wait_ge(on("rqk_c"), dve.takes("rqk_c", 2))
                    for f in range(2):
                        x, out_ = ps[2 * n + f], rqk[:, n, f, SEQ:2 * SEQ]
                        cos = rope[:, R_COS + SEQ * f:R_COS + SEQ * (f + 1)]
                        sin = rope[:, R_SIN + SEQ * f:R_SIN + SEQ * (f + 1)]
                        V.tensor_tensor(out_, x[:, SEQ:2 * SEQ], cos, ALU.mult).then_inc(
                            on("v_step"), dve.gives("v_step"))
                        for lo_, hi_ in ((0, 64), (64, 0)):
                            V.tensor_tensor(rtmp[lo_:lo_ + 64, 0, :], x[hi_:hi_ + 64, SEQ:2 * SEQ],
                                                    sin[hi_:hi_ + 64, :], ALU.mult).then_inc(
                                                        on("v_step"), dve.gives("v_step"))
                        dve.eng.wait_ge(on("v_step"), dve.given("v_step"))
                        V.tensor_tensor(out_, out_, rtmp[:, 0, :], ALU.add).then_inc(
                            on("rqk" if f else "v_step"), dve.gives("rqk" if f else "v_step"))
                        dve.eng.wait_ge(on("rqk" if f else "v_step"), dve.given("rqk" if f else "v_step"))
                split_lo(dve)
                for st in range(2):
                    dve.eng.wait_ge(on("rs_ps"), dve.takes("rs_ps"))
                    stt(rs[:, st, :], ps[st][:, :], RDK ** -0.5, wd[:, st, :], ALU.mult, ALU.mult).then_inc(
                        on("rs"), dve.gives("rs"))
                dve.eng.wait_ge(on("rs_ps"), dve.takes("rs_ps"))
                stt(heads(rs[:, 2, :], 2), heads(ps[2][:, :], 2), RDK ** -0.5, wd[:, :, 0:SEQ],
                            ALU.mult, ALU.mult).then_inc(on("rs"), dve.gives("rs"))
                split_lo(dve)
                for t in ALL:
                    dve.eng.wait_ge(on("pv_ps"), dve.takes("pv_ps"))
                    V.bn_stats(rsm[:, 12 * t:12 * t + 6], ps[4 + t][:, :]).then_inc(
                        on("v_step"), dve.gives("v_step"))
                dve.eng.wait_ge(on("v_step"), dve.given("v_step"))
                V.memset(rsm[:, 95:96], 0.0).then_inc(
                    on("v_step"), dve.gives("v_step"))
                for t in ALL:
                    V.bn_aggr(rsm[:, 12 * t + 6:12 * t + 8], rsm[:, 12 * t:12 * t + 6]).then_inc(
                        on("v_step"), dve.gives("v_step"))
                dve.eng.wait_ge(on("v_step"), dve.given("v_step"))
                tsc(r_stat[:, :, 8:9], r_stat[:, :, 7:8], LN_EPS, None, ALU.add).then_inc(
                    on("pow_in"), dve.gives("pow_in"))
                split_lo(dve)
                dve.eng.wait_ge(on("pow_out"), dve.takes("pow_out"))
                for t in ALL:
                    c = 12 * t
                    tsc(rv[:, t, :], ps[4 + t][:, :], rsm[:, c + 6:c + 7], rsm[:, c + 8:c + 9],
                                ALU.subtract, ALU.mult).then_inc(on("v_step"), dve.gives("v_step"))
                dve.eng.wait_ge(on("v_step"), dve.given("v_step"))
                for t in ALL:
                    dve.eng.wait_ge(on("rg"), dve.takes("rg"))
                    V.tensor_tensor(rv[:, t, :], rv[:, t, :], rg[:, t, :], ALU.mult).then_inc(
                        on("ro"), dve.gives("ro"))
                for f in range(4):
                    dve.eng.wait_ge(on("rt_hi"), dve.takes("rt_hi"))
                    V.tensor_tensor(rt_lo[:, f, :], ps[4 + f][:, :], rt_hi[:, f, :].bitcast(F32),
                                            ALU.subtract).then_inc(on("rt"), dve.gives("rt"))
                for c in range(2):
                    split_lo(dve)
                    dve.eng.wait_ge(on("y_add"), dve.given("y_add"))
                    dve_add(dve, c, ALL, ALL)
                split_lo(dve)

        def pool_ret(pool):
            with pool.turns("ret", RH):
                pool.eng.wait_ge(on("pow_in"), pool.takes("pow_in"))
                G.tensor_tensor(r_stat[:, :, 8], r_stat[:, :, 8],
                                         cst[:, C_MISC:C_MISC + 1].to_broadcast([P, 4]), ALU.pow).then_inc(
                                             on("pow_out"), pool.gives("pow_out"))

        def mlp_order():
            return (("up", 0),), (("up", 1), ("down", 0), ("up", 0), ("down", 1)), \
                (("up", 1), ("down", 0), ("down", 1))

        MLP_TURNS = MLP // 512 // 2 - 1
        last_down = "last"

        def mlp_program(lane, key, step):
            first, turn, last = mlp_order()
            chunk = {"up": 0, "down": 0}

            def run(steps, i):
                for what, b in steps:
                    step(what, b, i + chunk[what])
                    chunk[what] += 1

            run(first, 0)
            with lane.turns(key, MLP_TURNS) as i:
                run(turn, i * 2)
            for what in chunk:
                chunk[what] += 2 * (MLP_TURNS - 1)
            run(last[:-1], 0)
            step(*last[-1], last_down)

        def sp_mlp(sp, l):
            w1, w2 = a["mlp_w1_2"][l], a["mlp_w2_2"][l]

            def step(what, b, c):
                c = MLP // 512 - 1 if c is last_down else c
                for j in range(2):
                    if what == "up":
                        fetch(sp, cols_unit(w1, c * 512 + 256 * j, c * 512 + (256 * j + P)))
                    else:
                        fetch(sp, rows_unit(w2, c * 4, 512 * j))

            mlp_program(sp, "mlp", step)

        def down_banks(j, tiles):
            return (4, 5, 6, 7) if len(tiles) == 4 else (4 + 2 * j, 5 + 2 * j)

        def pe_mlp(pe, tiles):
            tok = slice(tiles[0] * P, 2 * SEQ)
            n_tok = len(tiles) * P

            def up(j):
                pe.eng.wait_ge(on("hh"), pe.takes("hh", 2))
                up_unit(pe, [ps[2 * j][:, 0:n_tok], ps[2 * j + 1][:, 0:n_tok]], zt_hi, zt_lo, "up_ps", (tok, tok))

            def step(what, b, c):
                for j in range(2):
                    if what == "up":
                        up(j)
                        if j == 0 and pe.loop is None and c == 0:
                            pe_gates(pe, tiles)
                    else:
                        if j == 0 and c is last_down:
                            pe.eng.wait_ge(on("hh"), pe.takes("hh", 4))
                        down_unit(pe, hh_hi[:, b, :, :], hh_lo[:, b, :, :], tiles, down_banks(j, tiles))
                if what == "up" and pe.loop is None and c == 0:
                    pe_gates_end(pe, tiles)

            mlp_program(pe, f"mlp{len(tiles)}", step)
            pe.eng.wait_ge(on("y_add"), pe.beyond("y_add", 4))
            release(pe)

        def act_mlp(act, tiles, final=False):
            n_tok = len(tiles) * P

            def step(what, b, c):
                for j in range(2):
                    if what == "up":
                        act.eng.wait_ge(on("up_ps"), act.takes("up_ps"))
                        act.eng.wait_ge(on("hh"), act.takes("hh", 2))
                        for f in range(2):
                            A.activation(hm[:, 2 * j + f, 0:n_tok], ps[2 * j + f][:, 0:n_tok], ACT.Relu).then_inc(
                                on("relu"), act.gives("relu"))
                        for f in range(2):
                            act.eng.wait_ge(on("hm"), act.takes("hm"))
                            act_copy(hh_hi[:, b, 2 * j + f, 0:n_tok], hm[:, 2 * j + f, 0:n_tok]).then_inc(
                                on("hh_hi"), act.gives("hh_hi"))
                    if not (final and c is last_down):
                        split_hi(act)
                    if what == "up" and j == 0 and act.loop is None and c == 0:
                        act_gates(act, tiles)

            mlp_program(act, f"mlp{len(tiles)}", step)
            act.eng.wait_ge(on("hh"), act.takes("hh", 4))

        def dve_mlp(dve, tiles, final=False):
            n_tok = len(tiles) * P

            def step(what, b, c):
                for j in range(2):
                    if what == "up":
                        for f in range(2):
                            dve.eng.wait_ge(on("relu"), dve.takes("relu"))
                            r2 = hm[:, 2 * j + f, 0:n_tok]
                            V.tensor_tensor(r2, r2, ps[2 * j + f][:, 0:n_tok], ALU.mult).then_inc(
                                on("hm"), dve.gives("hm"))
                        dve.eng.wait_ge(on("hm"), dve.given("hm"))
                        split_lo(dve)
                        for f in range(2):
                            dve.eng.wait_ge(on("hh_hi"), dve.takes("hh_hi"))
                            V.tensor_tensor(hh_lo[:, b, 2 * j + f, 0:n_tok], hm[:, 2 * j + f, 0:n_tok],
                                                    hh_hi[:, b, 2 * j + f, 0:n_tok].bitcast(F32), ALU.subtract).then_inc(
                                                        on("hh"), dve.gives("hh"))
                    else:
                        dve.eng.wait_ge(on("y_add"), dve.given("y_add"))
                        dve_add(dve, j, tiles, down_banks(j, tiles))
                        if not (final and c is last_down):
                            split_lo(dve)

            dve.eng.wait_ge(on("zs_new"), dve.takes("zs_new", len(tiles)))
            dve.eng.sem_inc(on("hh"), 4)
            dve.made["hh"] = dve.made.get("hh", 0) + 4
            for t in tiles:
                V.memset(y[:, t, :], 0.0).then_inc(on("y_zero"), dve.gives("y_zero"))
            dve.eng.wait_ge(on("y_zero"), dve.given("y_zero"))
            mlp_program(dve, f"mlp{len(tiles)}", step)

        NF = D // P
        NAT_TURN = 4
        NAT_STEPS = NAT_TURN * 8
        S_BANK = (2, 3, 6)

        def sp_nat(sp):
            w, w_o = a["nat_w_in_2"][0], a["nat_w_o_2"][0]
            for c in range(2):
                for j in range(2):
                    fetch(sp, rows_unit(w, 4 * j, 2 * D + 512 * c))
            with sp.turns("nat", NF // NAT_TURN) as i:
                for j in range(NAT_TURN):
                    f = i * (NAT_TURN * P) + j * P
                    fetch(sp, cols_unit(w, f, f + D))
            for c in range(2):
                for j in range(2):
                    fetch(sp, rows_unit(w_o, 4 * j, 512 * c))

        def pool_nat(pool):
            pool.eng.wait_ge(on("zT"), pool.takes("zT", 2 * len(ALL)))
            pool.eng.wait_ge(on("zs_new"), pool.given("zs_new"))
            G.memset(nvf[:, :, :, :, :], 0.0).then_inc(on("p_step"), pool.gives("p_step"))
            pool.eng.wait_ge(on("p_step"), pool.given("p_step"))
            G.memset(nq[:, :, :, :], 0.0).then_inc(on("nq_zero"), pool.gives("nq_zero"))
            rpb = a["nat_rpb_2"]
            for f in range(NF):
                b = f % 2
                if f >= 2:
                    pool.eng.wait_ge(on("n_biased"), pool.takes("n_biased", 8))
                for half in range(2):
                    for h in range(4):
                        src = bass.AP(rpb.tensor, (4 * f + h) * 15 * 31 + (5 - half) * 31 + 15 - (GRID_W - 1),
                                        [[1, GRID_W], [31, 6], [1, GRID_W]])
                        pool.eng.dma_start(nb[half * GRID_W:(half + 1) * GRID_W, b, h, :, :], src).then_inc(
                            on("nb_in"), pool.gives("nb_in", 16))
                pool.eng.wait_ge(on("nb_in"), pool.takes("nb_in", 128))
                for h in range(4):
                    ins = G.tensor_tensor(nb[:, b, h, :, :], nb[:, b, h, :, :],
                                          over_heads(cst[:, C_NAT:C_NAT + GRID_W], 6), ALU.add)
                ins.then_inc(on("n_bias"), pool.gives("n_bias"))
                if f == 0:
                    pool.eng.wait_ge(on("nv"), pool.takes("nv", 8))
                if f >= 2:
                    pool.eng.wait_ge(on("no_ps"), pool.takes("no_ps"))
                for h in range(4):
                    r = slice(ND * h, ND * h + ND)
                    ins = G.tensor_copy(nvf[:, b, :, h, r], nv[:, :, f * P + ND * h:f * P + ND * h + ND])
                ins.then_inc(on("n_v"), pool.gives("n_v"))

        def up_nat(pe):
            up_unit(pe, [ps[0][:, 0:SEQ], ps[1][:, :]], zt_hi, zt_lo, "nqk_ps", (slice(SEQ, 2 * SEQ), slice(None)))

        def pe_nat(pe):
            for c in range(2):
                for j in range(2):
                    rows_product(pe, [[ps[4 * c + t][:, :]] for t in ALL], zt_hi, zt_lo, range(4 * j, 4 * j + 4),
                                 j == 0, j == 1, "proj_ps" if j else None)
            pe.eng.wait_ge(on("nv"), pe.takes("nv", 8))
            pe.eng.wait_ge(on("nq_zero"), pe.takes("nq_zero"))
            with pe.turns("nat", NF // NAT_TURN):
                up_nat(pe)
                for g in range(NAT_STEPS + 3):
                    if g < NAT_STEPS:
                        j, h, t = g // 8, g % 8 // 2, g % 2
                        if g % 8 == 0:
                            pe.eng.wait_ge(on("n_q"), pe.takes("n_q", 4))
                            pe.eng.wait_ge(on("n_k"), pe.takes("n_k"))
                        if g % 8 == 4 and j + 1 < NAT_TURN:
                            up_nat(pe)
                        T.matmul(ps[S_BANK[g % 3]][:, :], nq[:, j % 2, h, t * P:(t + 1) * P], nk[:, j % 2, :],
                                 start=True, stop=True).then_inc(on("ns_ps"), pe.gives("ns_ps"))
                    if g >= 4 and g % 2 == 0:
                        j, h = (g - 4) // 8, (g - 4) % 8 // 2
                        if h == 0:
                            pe.eng.wait_ge(on("nt"), pe.takes("nt"))
                            pe.eng.wait_ge(on("n_v"), pe.takes("n_v"))
                        pe.eng.wait_ge(on("n_pt"), pe.takes("n_pt", 2))
                        for k in range(4):
                            ins = T.matmul(ps[7][:, 0:SEQ], nvf[:, j % 2, k, h, :],
                                           npt[:, k, :, :].rearrange("p t q -> p (t q)"),
                                           start=h == k == 0, stop=h == k == 3)
                        if h == 3:
                            ins.then_inc(on("no_ps"), pe.gives("no_ps"))
                    if 2 <= g < NAT_STEPS + 2:
                        t, b = g % 2, (g - 2) % 3
                        pe.eng.wait_ge(on("n_diag"), pe.takes("n_diag"))
                        for k in range(4):
                            ins = T.matmul(ps[4 + t][:, hs(k)], npr[:, b, hs(k)], nd[:, b, :], start=True, stop=True)
                        ins.then_inc(on("nt_ps"), pe.gives("nt_ps"))
            pe.eng.wait_ge(on("nt"), pe.takes("nt"))
            for c in range(2):
                for j in range(2):
                    rows_product(pe, [[ps[2 * c + t][:, :]] for t in range(NT)], nt_hi, nt_lo,
                                 range(4 * j, 4 * j + 4), j == 0, j == 1, "ny_ps" if j else None)
            release(pe)

        def act_q(act, j):
            act.eng.wait_ge(on("nqk_ps"), act.takes("nqk_ps"))
            for h in range(4):
                r = slice(ND * h, ND * h + ND)
                src = ps[0][r, 0:SEQ].rearrange("p (g c) -> p g c", c=GRID_W)[:, :, ::-1]
                A.activation(nq[r, j % 2, h, :].rearrange("p (g c) -> p g c", c=GRID_W), src, ACT.Copy,
                             scale=ND ** -0.5).then_inc(on("n_q"), act.gives("n_q"))

        def act_nat(act):
            act.eng.wait_ge(on("zs_new"), act.takes("zs_new", 2 * len(ALL)))
            for c in range(2):
                split_hi(act)
                if c == 0:
                    split_hi(act)
                act.eng.wait_ge(on("proj_ps"), act.takes("proj_ps"))
                for t in ALL:
                    act_copy(nv[:, t, 512 * c:512 * c + 512], ps[4 * c + t][:, :]).then_inc(
                        on("nv"), act.gives("nv"))
            act.eng.wait_ge(on("nq_zero"), act.takes("nq_zero"))
            with act.turns("nat", NF // NAT_TURN) as i:
                split_hi(act)
                act_q(act, 0)
                for g in range(NAT_STEPS + 3):
                    if 2 <= g < NAT_STEPS + 2:
                        t = g % 2
                        act.eng.wait_ge(on("nt_ps"), act.takes("nt_ps"))
                        act_copy(npt[:, :, t, :], heads(ps[4 + t][:, :], 4)).then_inc(on("n_pt"), act.gives("n_pt"))
                    if g < NAT_STEPS:
                        b = g % 3
                        act.eng.wait_ge(on("n_max"), act.takes("n_max"))
                        A.activation(npr[:, b, :], ps[S_BANK[b]][:, :], ACT.Exp, bias=nsm[:, 3 + b:4 + b],
                                     accum_out=nsm[:, 6 + b:7 + b]).then_inc(on("n_exp"), act.gives("n_exp"))
                        if g % 8 == 4 and g // 8 + 1 < NAT_TURN:
                            act_q(act, g // 8 + 1)
                        if g % 8 == 6 and g // 8 + 1 < NAT_TURN:
                            split_hi(act)
                    if g >= 10 and g % 8 == 2:
                        j = (g - 10) // 8
                        act.eng.wait_ge(on("no_ps"), act.takes("no_ps"))
                        act_copy(nt_hi[:, bass.ds(NAT_TURN * i + j, 1), :],
                                 ps[7][:, 0:SEQ].unsqueeze(1)).then_inc(on("nt_hi"), act.gives("nt_hi"))
            for _ in range(5):
                split_hi(act)

        def dve_k(dve, j):
            dve.eng.wait_ge(on("nqk_ps"), dve.takes("nqk_ps"))
            V.tensor_copy(nk[:, j % 2, :], ps[1][:, :]).then_inc(on("n_k"), dve.gives("n_k"))

        def dve_nat(dve):
            dve.eng.wait_ge(on("zs_new"), dve.takes("zs_new", len(ALL)))
            dve.eng.sem_inc(on("nt"), 1)
            dve.made["nt"] = 1
            split_lo(dve)
            split_lo(dve)
            split_lo(dve)
            with dve.turns("nat", NF // NAT_TURN) as i:
                split_lo(dve)
                dve_k(dve, 0)
                for g in range(NAT_STEPS + 3):
                    if g < NAT_STEPS:
                        j, h, t, b = g // 8, g % 8 // 2, g % 2, g % 3
                        if g % 8 == 0:
                            dve.eng.wait_ge(on("n_bias"), dve.takes("n_bias"))
                        dve.eng.wait_ge(on("ns_ps"), dve.takes("ns_ps"))
                        s_, slots = heads(ps[S_BANK[b]][:, SEQ:2 * SEQ], 4), slice(2 - 2 * t, 6 - 2 * t)
                        V.tensor_tensor(s_, s_, nb[:, j % 2, h, slots, :], ALU.add).then_inc(
                            on("n_biased"), dve.gives("n_biased"))
                        dve.eng.wait_ge(on("n_biased"), dve.given("n_biased"))
                        V.tensor_reduce(nsm[:, b:b + 1], ps[S_BANK[b]][:, :], AX_X, ALU.max).then_inc(
                            on("v_step"), dve.gives("v_step"))
                        dve.eng.wait_ge(on("v_step"), dve.given("v_step"))
                        V.tensor_scalar(nsm[:, 3 + b:4 + b], nsm[:, b:b + 1], -1.0, None, ALU.mult).then_inc(
                            on("n_max"), dve.gives("n_max"))
                    if 1 <= g <= NAT_STEPS:
                        b = (g - 1) % 3
                        dve.eng.wait_ge(on("n_exp"), dve.takes("n_exp"))
                        V.reciprocal(nsm[:, 9 + b:10 + b], nsm[:, 6 + b:7 + b]).then_inc(
                            on("v_step"), dve.gives("v_step"))
                        dve.eng.wait_ge(on("v_step"), dve.given("v_step"))
                        V.tensor_scalar(nd[:, b, :], cst[:, C_REV:C_REV + P], nsm[:, 9 + b:10 + b], None,
                                        ALU.mult).then_inc(on("n_diag"), dve.gives("n_diag"))
                    if g % 8 == 4 and g // 8 + 1 < NAT_TURN:
                        dve_k(dve, g // 8 + 1)
                    if g % 8 == 7 and g // 8 + 1 < NAT_TURN:
                        split_lo(dve)
                    if g >= 10 and g % 8 == 2:
                        j = (g - 10) // 8
                        dve.eng.wait_ge(on("nt_hi"), dve.takes("nt_hi"))
                        V.tensor_tensor(nt_lo[:, bass.ds(NAT_TURN * i + j, 1), :], ps[7][:, 0:SEQ].unsqueeze(1),
                                        nt_hi[:, bass.ds(NAT_TURN * i + j, 1), :].bitcast(F32),
                                        ALU.subtract).then_inc(on("nt"), dve.gives("nt"))
            for _ in range(5):
                split_lo(dve)

        block = ctx.enter_context(nc.Block())

        @block.sync
        def _(eng):
            sp = Lane("sync", eng)
            eng.dma_start(xs[:, :, :], a["x"].rearrange("b (t p) d -> p (b t) d", p=P)).then_inc(
                on("x_in"), sp.gives("x_in", 16))
            for l in range(DEPTH):
                w = a["ada_w_2"][l]
                with sp.turns("ada", 6) as i:
                    for b in range(2):
                        for j in range(2):
                            fetch(sp, rows_unit(w, 4 * j, i * 1024 + 512 * b))
            for l in range(DEPTH):
                sp_layer(sp, l)
            sp_ret(sp)
            sp_mlp(sp, 0)
            sp_nat(sp)
            sp_mlp(sp, 1)
            sp.eng.wait_ge(on("zs_new"), sp.takes("zs_new", 4 * len(ALL) - 4))
            eng.dma_start(out.rearrange("b (t p) d -> p (b t) d", p=P), xs[:, :, :]).then_inc(
                on("stored"), sp.gives("stored", 16))
            sp.eng.wait_ge(on("stored"), sp.given("stored"))

        @block.gpsimd
        def _(eng):
            pool = Lane("gpsimd", eng)
            pool_start(pool)
            pool_params(pool, 0)
            for l in range(DEPTH):
                pool_mixer(pool, l)
                pool_gains(pool, l)
                if l + 1 < DEPTH:
                    pool_params(pool, l + 1)
                pool_norm(pool, lambda t: xn1[:, t, :], 0)
                pool.eng.wait_ge(on("y_ps"), pool.takes("y_ps"))
                if l + 1 == DEPTH:
                    eng.dma_start(xc[:, :, :], a["ctx_2"].rearrange("b (t p) d -> p (b t) d", p=P)).then_inc(
                        on("xc_in"), pool.gives("xc_in", 16))
                pool_norm(pool, lambda t: xn1[:, t, :], 1)
            pool.eng.wait_ge(on("xT"), pool.takes("xT", 3 * NT))
            pool.eng.wait_ge(on("xs_new"), pool.given("xs_new"))
            eng.dma_start(rope[:, :], a["table_2"]).then_inc(on("rdec_in"), pool.gives("rdec_in", 16))
            eng.dma_start(rsm[:, 72:80], a["ret_decay_2"].rearrange("a d h -> (a d h)").partition_broadcast(P)).then_inc(
                on("rdec_in"), pool.gives("rdec_in", 16))
            pool_ret(pool)
            pool_norm2(pool, 0, 0, ALL)
            pool_norm2(pool, 0, 1, ALL)
            pool_nat(pool)
            pool_norm2(pool, 1, 0, LAT)
            pool_norm2(pool, 1, 1, LAT)

        @block.scalar
        def _(eng):
            act = Lane("scalar", eng)
            act_start(act)
            for l in range(DEPTH):
                act_ada(act)
            for l in range(DEPTH):
                act_mixer(act, l)
                act_norm(act, par[:, 0, 88:96], par[:, 0, 96:104], xf1, xt_hi)
                act_ffn(act)
                if l + 1 < DEPTH:
                    act_norm(act, par[:, 0, 104:112], par[:, 0, 112:120], xf1, xt_hi)
            act.eng.wait_ge(on("coef"), act.takes("coef", 2))
            act_norm(act, coef[:, 1, 0, :], coef[:, 1, 1, :], xf1, zt_hi[:, :, SEQ:2 * SEQ])
            act.eng.wait_ge(on("xT"), act.takes("xT", 4 * DEPTH))
            for t in range(NT):
                act.eng.wait_ge(on("xnt_ps"), act.takes("xnt_ps"))
                for k in range(KT):
                    A.activation(xf1[:, t, k, :], ps[2 * t + k // 4][:, hs(k % 4)], ACT.Identity,
                                         scale=coef[:, 0, 0, k:k + 1], bias=coef[:, 0, 1, k:k + 1]).then_inc(
                                             on("a_step"), act.gives("a_step"))
                act.eng.wait_ge(on("a_step"), act.given("a_step"))
                act_copy(zt_hi[:, :, t * P:(t + 1) * P], xf1[:, t, :, :]).then_inc(on("x_hi"), act.gives("x_hi"))
            act_ret(act)
            act.turned = 0
            act_gates(act, ALL)
            act_norm2(act, ALL, (2, 3))
            act_mlp(act, ALL)
            act_norm2(act, ALL, (4, 5))
            act_nat(act)
            act_gates(act, LAT)
            act_norm2(act, LAT, (6,))
            act_mlp(act, LAT, final=True)

        @block.vector
        def _(eng):
            dve = Lane("vector", eng)
            dve_start(dve)
            for l in range(DEPTH):
                dve_ada(dve, l)
            dve_mods(dve)
            dve.eng.wait_ge(on("x_in"), dve.takes("x_in", 16))
            for l in range(DEPTH):
                if l:
                    dve.eng.wait_ge(on("xs_new"), dve.takes("xs_new", NT))
                dve_mixer(dve, l)
                dve_norm(dve, 2, xf1, xt_hi, xt_lo)
                dve_ffn(dve)
                dve.eng.wait_ge(on("xs_new"), dve.takes("xs_new", NT))
                if l + 1 < DEPTH:
                    dve_norm(dve, 1, xf1, xt_hi, xt_lo)
            dve_coef(dve, 1, par[:, 0, 104:112], par[:, 0, 112:120], 0, 0, 0, "coef")
            dve_norm(dve, 1, xf1, zt_hi[:, :, SEQ:2 * SEQ], zt_lo[:, :, SEQ:2 * SEQ])
            for t in range(NT):
                dve.eng.wait_ge(on("x_hi"), dve.takes("x_hi"))
                x = (slice(None), slice(None), slice(t * P, (t + 1) * P))
                V.tensor_tensor(zt_lo[x], xf1[:, t, :, :], zt_hi[x].bitcast(F32), ALU.subtract).then_inc(
                    on("xT"), dve.gives("xT"))
            dve.eng.sem_inc(on("y_add"), 4)
            dve.made["y_add"] = 4
            dve_ret(dve)
            dve_gates(dve, 0, 2, ALL)
            dve_norm2(dve, ALL, False)
            dve_gates(dve, 0, 5, ALL)
            dve_mlp(dve, ALL)
            dve_norm2(dve, ALL, False)
            dve_nat(dve)
            dve_gates(dve, 1, 2, LAT)
            for c in range(2):
                dve.eng.wait_ge(on("ny_ps"), dve.takes("ny_ps"))
            dve_norm2(dve, LAT, False, ps)
            dve_gates(dve, 1, 5, LAT)
            dve_mlp(dve, LAT, final=True)
            dve_norm2(dve, LAT, True)

        @block.tensor
        def _(eng):
            pe = Lane("tensor", eng)
            pe.used["w_split"] = RAW_SLOTS
            pe.released = True
            pe_start(pe)
            pe.eng.wait_ge(on("c_lo"), pe.takes("c_lo", 2))
            for l in range(DEPTH):
                pe_ada(pe, l)
            pe.released = False
            for l in range(DEPTH):
                pe_mixer(pe, l)
                pe_norm(pe, lambda t: xn1[:, t, :])
                pe_ffn(pe)
                pe_norm(pe, lambda t: xn1[:, t, :])
            pe.eng.wait_ge(on("xc_in"), pe.takes("xc_in", 16))
            for t in range(NT):
                pe_turned(pe, xc[:, t, :], 2 * t)
            pe.eng.wait_ge(on("xT"), pe.takes("xT", NT))
            pe_ret(pe)
            pe_gates(pe, ALL)
            pe_gates_end(pe, ALL)
            pe_norm2(pe, ALL)
            pe_mlp(pe, ALL)
            pe_norm2(pe, ALL)
            pe_nat(pe)
            pe_gates(pe, LAT)
            pe_gates_end(pe, LAT)
            pe_norm2(pe, LAT)
            pe_mlp(pe, LAT)


_INS = ["x", "w_in", "gdn_conv_w", "gdn_a_log", "gdn_dt_bias", "gdn_norm_g", "w_out", "ln1_g", "ln1_b", "w_up",
        "ffn_conv_w", "ffn_conv_b", "w_down", "ln2_g", "ln2_b", "c_2", "ctx_2", "c_ctx_2", "ada_w_2", "ada_b_2",
        "ret_w_in_2", "ret_w_o_2", "ret_decay_2", "nat_w_in_2", "nat_w_o_2", "nat_rpb_2", "mlp_w1_2", "mlp_w2_2",
        "ln_g_2", "ln_b_2"]


def make(arrays, bacc):
    nc = bacc.Bacc("TRN2", target_bir_lowering=False, num_devices=1)
    aps = {n: nc.dram_tensor(f"in_{n}", v.shape, mybir.dt.from_np(v.dtype), kind="ExternalInput").ap()
           for n, v in arrays.items()}
    out = nc.dram_tensor("out", (1, SEQ, D), F32, kind="ExternalOutput").ap()
    build(nc, aps, out)
    return nc


def kernel(**inputs):
    import numpy as np
    import concourse.bacc as bacc
    from concourse.bass_utils import run_bass_kernel_spmd

    arrays = {n: np.ascontiguousarray(inputs[n]) for n in _INS}
    arrays["table_1"], arrays["table_2"] = constants()
    nc = make(arrays, bacc)
    r = run_bass_kernel_spmd(nc, [{f"in_{n}": v for n, v in arrays.items()}], core_ids=[0])
    return r.results[0]["out"]
```
